# Optimizing a Trainium2 kernel written in Bass

```python
import jax, jax.numpy as jnp
from jax import lax
import numpy as np
import math

D_MODEL = 1024
BATCH = 1
SEQ = 512
DEPTH = 2

GRID_W = 64
CTX_LEN = 256
CHUNK = 128
A_HEADS = 4
A_HEAD_DIM = 128
A_W = A_HEADS * A_HEAD_DIM
B_GROUPS = 4
B_GROUP_DIM = 128
B_W = B_GROUPS * B_GROUP_DIM
AB_IN = 3 * A_W + 2 * B_W
AB_OUT = A_W + B_W
C_HEADS = 16
C_KV_HEADS = 4
C_GROUP = C_HEADS // C_KV_HEADS
C_HEAD_DIM = 64
C_Q_W = C_HEADS * C_HEAD_DIM
C_KV_W = C_KV_HEADS * C_HEAD_DIM
C_IN = 2 * C_Q_W + 2 * C_KV_W
WINDOW = 128
Q_BLOCK = 128
ROPE_BASE = 10000.0
NORM_EPS = 1e-6
NEG_INF = -1e30
N_EVEN = (DEPTH + 1) // 2
N_ODD = DEPTH // 2


def rms_norm(x, g):
    xf = x.astype(jnp.float32)
    y = xf * lax.rsqrt(jnp.mean(xf * xf, axis=-1, keepdims=True) + NORM_EPS)
    return (y * g.astype(jnp.float32)).astype(x.dtype)

def layer_norm(x, g):
    xf = x.astype(jnp.float32)
    mu = jnp.mean(xf, axis=-1, keepdims=True)
    xc = xf - mu
    y = xc * lax.rsqrt(jnp.mean(xc * xc, axis=-1, keepdims=True) + NORM_EPS)
    return (y * g.astype(jnp.float32)).astype(x.dtype)

def adaln(cond, w, b):
    m = jax.nn.silu(cond) @ w + b
    return jnp.split(m, 3, axis=-1)

def rope_1d(x, pos):
    nf = x.shape[-1] // 2
    inv = ROPE_BASE ** (-jnp.arange(nf, dtype=jnp.float32) / nf)
    ang = pos.astype(jnp.float32)[:, None] * inv[None, :]
    cos = jnp.cos(ang)[None, :, None, :].astype(x.dtype)
    sin = jnp.sin(ang)[None, :, None, :].astype(x.dtype)
    x1, x2 = x[..., :nf], x[..., nf:]
    return jnp.concatenate([x1 * cos - x2 * sin, x2 * cos + x1 * sin], axis=-1)

def rope_2d(x, row, col):
    half = x.shape[-1] // 2
    return jnp.concatenate([rope_1d(x[..., :half], row), rope_1d(x[..., half:], col)], axis=-1)

def sink_softmax(scores, sink):
    s = jnp.broadcast_to(sink, scores.shape[:-1] + (1,))
    p = jax.nn.softmax(jnp.concatenate([s, scores], axis=-1), axis=-1)
    return p[..., 1:]

def mixer_ab(h, w_in, v_g, s_w, s_b, w_out):
    bsz, L, _ = h.shape
    z = h @ w_in
    u, v, g_a, x_b, g_b = jnp.split(z, [A_W, 2 * A_W, 3 * A_W, 3 * A_W + B_W], axis=-1)
    v = layer_norm(v, v_g).reshape(bsz, L // CHUNK, CHUNK, A_HEADS, A_HEAD_DIM)
    sv = jnp.einsum('bnphc,hqp->bnqhc', v, s_w) + s_b.T[:, :, None]
    y_a = u * sv.reshape(bsz, L, A_W) * jax.nn.silu(g_a)
    xb = x_b.reshape(bsz, L, B_GROUPS, B_GROUP_DIM).astype(jnp.float32)
    f = jnp.real(jnp.fft.fft2(xb, axes=(1, 3), norm='ortho')).astype(h.dtype).reshape(bsz, L, B_W)
    y_b = f * jax.nn.silu(g_b)
    return jnp.concatenate([y_a, y_b], axis=-1) @ w_out

def split_c(z):
    return jnp.split(z, [C_Q_W, C_Q_W + C_KV_W, C_Q_W + 2 * C_KV_W], axis=-1)

def window_attention(q, k, v, k_ctx, v_ctx, sink):
    bsz, S, _, hd = q.shape
    qg = q.reshape(bsz, S, C_KV_HEADS, C_GROUP, hd)
    pad = ((0, 0), (WINDOW, WINDOW), (0, 0), (0, 0))
    kp, vp = jnp.pad(k, pad), jnp.pad(v, pad)
    kb_len = Q_BLOCK + 2 * WINDOW
    scale = hd ** -0.5
    sink_b = sink.reshape(C_KV_HEADS, C_GROUP).astype(jnp.float32)[None, :, :, None, None]

    def one_block(n):
        start = n * Q_BLOCK
        qb = lax.dynamic_slice_in_dim(qg, start, Q_BLOCK, axis=1)
        kb = lax.dynamic_slice_in_dim(kp, start, kb_len, axis=1)
        vb = lax.dynamic_slice_in_dim(vp, start, kb_len, axis=1)
        qpos = start + jnp.arange(Q_BLOCK)
        kpos = start - WINDOW + jnp.arange(kb_len)
        valid = (jnp.abs(qpos[:, None] - kpos[None, :]) <= WINDOW) & (kpos[None, :] >= 0) & (kpos[None, :] < S)
        s_win = jnp.einsum('bqkgd,bjkd->bkgqj', qb, kb).astype(jnp.float32) * scale
        s_win = jnp.where(valid, s_win, NEG_INF)
        s_ctx = jnp.einsum('bqkgd,bjkd->bkgqj', qb, k_ctx).astype(jnp.float32) * scale
        p = sink_softmax(jnp.concatenate([s_ctx, s_win], axis=-1), sink_b)
        vals = jnp.concatenate([v_ctx, vb], axis=1)
        return jnp.einsum('bkgqj,bjkd->bqkgd', p.astype(v.dtype), vals)

    out = lax.map(one_block, jnp.arange(S // Q_BLOCK))
    return jnp.moveaxis(out, 0, 1).reshape(bsz, S, C_Q_W)

def context_attention(q, k, v, sink):
    bsz, L, _, hd = q.shape
    qg = q.reshape(bsz, L, C_KV_HEADS, C_GROUP, hd)
    s = jnp.einsum('bqkgd,bjkd->bkgqj', qg, k).astype(jnp.float32) * hd ** -0.5
    sink_b = sink.reshape(C_KV_HEADS, C_GROUP).astype(jnp.float32)[None, :, :, None, None]
    p = sink_softmax(s, sink_b)
    o = jnp.einsum('bkgqj,bjkd->bqkgd', p.astype(v.dtype), v)
    return o.reshape(bsz, L, C_Q_W)

def first_inputs(seed: int = 0) -> dict:
    key = jax.random.key(seed)
    ks = jax.random.split(key, 16)

    def nrm(k, shape, s):
        return jax.random.normal(k, shape, jnp.float32) * s

    return {
        'x': nrm(ks[0], (BATCH, SEQ, D_MODEL), 1.0),
        'c': nrm(ks[1], (BATCH, D_MODEL), 1.0),
        'ctx': nrm(ks[2], (BATCH, CTX_LEN, D_MODEL), 1.0),
        'c_ctx': nrm(ks[3], (D_MODEL,), 1.0),
        'norm_g': 1.0 + nrm(ks[4], (DEPTH, D_MODEL), 0.02),
        'ada_w': nrm(ks[5], (DEPTH, D_MODEL, 3 * D_MODEL), 0.5 * D_MODEL ** -0.5),
        'ada_b': nrm(ks[6], (DEPTH, 3 * D_MODEL), 0.02),
        'w_in_ab': nrm(ks[7], (N_EVEN, D_MODEL, AB_IN), D_MODEL ** -0.5),
        'v_norm_g': 1.0 + nrm(ks[8], (N_EVEN, A_W), 0.02),
        'spatial_w': nrm(ks[9], (N_EVEN, A_HEADS, CHUNK, CHUNK), CHUNK ** -0.5),
        'spatial_b': 1.0 + nrm(ks[10], (N_EVEN, A_HEADS, CHUNK), 0.02),
        'w_out_ab': nrm(ks[11], (N_EVEN, AB_OUT, D_MODEL), AB_OUT ** -0.5),
        'w_in_c': nrm(ks[12], (N_ODD, D_MODEL, C_IN), D_MODEL ** -0.5),
        'sink_logit': nrm(ks[13], (N_ODD, C_HEADS), 0.5),
        'w_out_c': nrm(ks[14], (N_ODD, C_Q_W, D_MODEL), C_Q_W ** -0.5),
        'final_g': 1.0 + nrm(ks[15], (D_MODEL,), 0.02),
    }

def first_block(x, c, ctx, c_ctx, norm_g, ada_w, ada_b, w_in_ab, v_norm_g, spatial_w, spatial_b,
              w_out_ab, w_in_c, sink_logit, w_out_c, final_g):
    bsz, S, _ = x.shape
    rows = S // GRID_W
    row = jnp.repeat(jnp.arange(rows), GRID_W)
    col = jnp.tile(jnp.arange(GRID_W), rows)

    for layer in range(DEPTH):
        need_ctx_out = layer < DEPTH - 1
        shift, scale, gate = adaln(c[:, None, :], ada_w[layer], ada_b[layer])
        shift_c, scale_c, gate_c = adaln(c_ctx, ada_w[layer], ada_b[layer])
        h = rms_norm(x, norm_g[layer]) * (1.0 + scale) + shift
        if layer % 2 == 0:
            i = layer // 2
            y = mixer_ab(h, w_in_ab[i], v_norm_g[i], spatial_w[i], spatial_b[i], w_out_ab[i])
            if need_ctx_out:
                hc = rms_norm(ctx, norm_g[layer]) * (1.0 + scale_c) + shift_c
                yc = mixer_ab(hc, w_in_ab[i], v_norm_g[i], spatial_w[i], spatial_b[i], w_out_ab[i])
                ctx = ctx + gate_c * yc
            x = x + gate * y
        else:
            i = layer // 2
            w_in = w_in_c[i]
            hc = rms_norm(ctx, norm_g[layer]) * (1.0 + scale_c) + shift_c
            q, k, v, g = split_c(h @ w_in)
            q = rope_2d(q.reshape(bsz, S, C_HEADS, C_HEAD_DIM), row, col)
            k = rope_2d(k.reshape(bsz, S, C_KV_HEADS, C_HEAD_DIM), row, col)
            v = v.reshape(bsz, S, C_KV_HEADS, C_HEAD_DIM)
            Lc = ctx.shape[1]
            if need_ctx_out:
                q_c, k_c, v_c, g_c = split_c(hc @ w_in)
            else:
                k_c, v_c = jnp.split(hc @ w_in[:, C_Q_W:C_Q_W + 2 * C_KV_W], 2, axis=-1)
            k_c = k_c.reshape(bsz, Lc, C_KV_HEADS, C_HEAD_DIM)
            v_c = v_c.reshape(bsz, Lc, C_KV_HEADS, C_HEAD_DIM)
            o = window_attention(q, k, v, k_c, v_c, sink_logit[i])
            y = (o * jax.nn.silu(g)) @ w_out_c[i]
            if need_ctx_out:
                o_c = context_attention(q_c.reshape(bsz, Lc, C_HEADS, C_HEAD_DIM), k_c, v_c, sink_logit[i])
                ctx = ctx + gate_c * ((o_c * jax.nn.silu(g_c)) @ w_out_c[i])
            x = x + gate * y

    return rms_norm(x, final_g)


DEPTH_2 = 1

N_META = 16
SSD_HEAD_DIM = 64
SSD_INNER = D_MODEL
SSD_HEADS = SSD_INNER // SSD_HEAD_DIM
SSD_GROUPS = 2
SSD_STATE = 128
SSD_CONV = 4
SB_HEAD_DIM = 64
SB_WIDTH = D_MODEL
SB_HEADS = SB_WIDTH // SB_HEAD_DIM
MIX_WIDTH = SSD_INNER + SB_WIDTH
D_FF = 256 * ((8 * D_MODEL // 3 + 255) // 256)
FFN_CONV = 3
EPS = 1e-6

XBC_WIDTH = SSD_INNER + 2 * SSD_GROUPS * SSD_STATE
OFF_Z = 0
OFF_XBC = OFF_Z + SSD_INNER
OFF_DT = OFF_XBC + XBC_WIDTH
OFF_Q = OFF_DT + SSD_HEADS
OFF_K = OFF_Q + SB_WIDTH
OFF_V = OFF_K + SB_WIDTH
IN_COLS = OFF_V + SB_WIDTH


def rms_norm_2(x, g):
    x32 = x.astype(jnp.float32)
    y = x32 * lax.rsqrt(jnp.mean(x32 * x32, axis=-1, keepdims=True) + EPS)
    return (y * g.astype(jnp.float32)).astype(x.dtype)

def causal_dwconv(x, w, b):
    K = w.shape[0]
    L = x.shape[1]
    xp = jnp.pad(x, ((0, 0), (K - 1, 0), (0, 0)))
    y = b
    for k in range(K):
        y = y + xp[:, k:k + L] * w[k]
    return y

def ssd_mixer(z, xbc, dt_raw, conv_w, conv_b, dt_bias, a_log, d_skip, norm_g):
    out_dtype = z.dtype
    Bsz, L, _ = xbc.shape
    H, P, G, N = SSD_HEADS, SSD_HEAD_DIM, SSD_GROUPS, SSD_STATE
    J = H // G
    f32 = jnp.float32
    xbc = jax.nn.silu(causal_dwconv(xbc, conv_w, conv_b)).astype(f32)
    xs = xbc[..., :SSD_INNER].reshape(Bsz, L, H, P)
    Bm = xbc[..., SSD_INNER:SSD_INNER + G * N].reshape(Bsz, L, G, N)
    Cm = xbc[..., SSD_INNER + G * N:].reshape(Bsz, L, G, N)
    dt = jax.nn.softplus(dt_raw.astype(f32) + dt_bias.astype(f32))
    A = -jnp.exp(a_log.astype(f32))

    pad = CHUNK - N_META
    Lp = L + pad
    nc = Lp // CHUNK

    def front_pad(t):
        return jnp.pad(t, ((0, 0), (pad, 0)) + ((0, 0),) * (t.ndim - 2))

    Xdt = front_pad(xs * dt[..., None]).reshape(Bsz, nc, CHUNK, G, J, P)
    Adt = front_pad(dt * A).reshape(Bsz, nc, CHUNK, G, J).transpose(0, 3, 4, 1, 2)
    Bc = front_pad(Bm).reshape(Bsz, nc, CHUNK, G, N)
    Cc = front_pad(Cm).reshape(Bsz, nc, CHUNK, G, N)

    Acs = jnp.cumsum(Adt, axis=-1)
    causal = jnp.tril(jnp.ones((CHUNK, CHUNK), dtype=bool))
    seg = Acs[..., :, None] - Acs[..., None, :]
    Ldec = jnp.where(causal, jnp.exp(jnp.where(causal, seg, 0.0)), 0.0)

    CB = jnp.einsum('bclgn,bcsgn->bgcls', Cc, Bc)
    y_diag = jnp.einsum('bgcls,bgjcls,bcsgjp->bclgjp', CB, Ldec, Xdt)

    decay_states = jnp.exp(Acs[..., -1:] - Acs)
    states = jnp.einsum('bclgn,bgjcl,bclgjp->bcgjpn', Bc, decay_states, Xdt)
    chunk_decay = jnp.exp(Acs[..., -1])

    def step(carry, inp):
        st, dec = inp
        return carry * dec[..., None, None] + st, carry

    init = jnp.zeros((Bsz, G, J, P, N), f32)
    _, prev = lax.scan(step, init, (states.transpose(1, 0, 2, 3, 4, 5),
                                    chunk_decay.transpose(3, 0, 1, 2)))
    prev = prev.transpose(1, 0, 2, 3, 4, 5)

    y_off = jnp.einsum('bclgn,bcgjpn,bgjcl->bclgjp', Cc, prev, jnp.exp(Acs))

    y = (y_diag + y_off).reshape(Bsz, Lp, H, P)[:, pad:]
    y = y + xs * d_skip.astype(f32)[:, None]
    y = y.reshape(Bsz, L, SSD_INNER) * jax.nn.silu(z.astype(f32))
    return rms_norm_2(y, norm_g).astype(out_dtype)

def stick_breaking_attention(q, k, v):
    out_dtype = q.dtype
    Bsz, L, H, D = q.shape
    f32 = jnp.float32
    scale = 1.0 / math.sqrt(D)
    pad = Q_BLOCK - N_META
    Lp = L + pad
    nb = Lp // Q_BLOCK
    padw = ((0, 0), (pad, 0), (0, 0), (0, 0))
    qp = jnp.pad(q.astype(f32), padw)
    kp = jnp.pad(k.astype(f32), padw)
    vp = jnp.pad(v.astype(f32), padw)
    qb = qp.reshape(Bsz, nb, Q_BLOCK, H, D).transpose(1, 0, 2, 3, 4)
    key_pos = jnp.arange(Lp)

    def block(args):
        i, qi = args
        q_pos = i * Q_BLOCK + jnp.arange(Q_BLOCK)
        valid = (key_pos[None, :] < q_pos[:, None]) & (key_pos[None, :] >= pad)
        zlog = jnp.einsum('bqhd,bkhd->bhqk', qi, kp) * scale
        log_beta = jax.nn.log_sigmoid(zlog)
        log_keep = jnp.where(valid, log_beta - zlog, 0.0)
        after = lax.cumsum(log_keep, axis=3, reverse=True) - log_keep
        w = jnp.where(valid, jnp.exp(log_beta + after), 0.0)
        return jnp.einsum('bhqk,bkhd->bqhd', w, vp)

    o = lax.map(block, (jnp.arange(nb), qb))
    o = o.transpose(1, 0, 2, 3, 4).reshape(Bsz, Lp, H, D)[:, pad:]
    return o.astype(out_dtype)

def second_inputs(seed: int = 0) -> dict:
    key = jax.random.key(seed)
    ks = jax.random.split(key, 20)
    f32 = jnp.float32

    def gain(k, n):
        return 1.0 + 0.05 * jax.random.normal(k, (DEPTH_2, n), f32)

    dt0 = jnp.exp(jax.random.uniform(ks[5], (DEPTH_2, SSD_HEADS), f32,
                                     math.log(1e-3), math.log(1e-1)))
    dt_bias = dt0 + jnp.log(-jnp.expm1(-dt0))
    return {
        "x": jax.random.normal(ks[0], (BATCH, SEQ, D_MODEL), f32),
        "meta_tokens": jax.random.normal(ks[1], (N_META, D_MODEL), f32),
        "mix_pre_g": gain(ks[2], D_MODEL),
        "w_in": jax.random.normal(ks[3], (DEPTH_2, D_MODEL, IN_COLS), f32) * D_MODEL ** -0.5,
        "ssd_conv_w": jax.random.normal(ks[4], (DEPTH_2, SSD_CONV, XBC_WIDTH), f32) * SSD_CONV ** -0.5,
        "ssd_conv_b": 0.01 * jax.random.normal(ks[6], (DEPTH_2, XBC_WIDTH), f32),
        "ssd_dt_bias": dt_bias,
        "ssd_a_log": jnp.log(jax.random.uniform(ks[7], (DEPTH_2, SSD_HEADS), f32, 1.0, 16.0)),
        "ssd_d": 1.0 + 0.1 * jax.random.normal(ks[8], (DEPTH_2, SSD_HEADS), f32),
        "ssd_norm_g": gain(ks[9], SSD_INNER),
        "sb_norm_g": gain(ks[10], SB_WIDTH),
        "w_out": jax.random.normal(ks[11], (DEPTH_2, MIX_WIDTH, D_MODEL), f32) * MIX_WIDTH ** -0.5,
        "mix_post_g": gain(ks[12], D_MODEL),
        "ffn_pre_g": gain(ks[13], D_MODEL),
        "w_up": jax.random.normal(ks[14], (DEPTH_2, D_MODEL, 2 * D_FF), f32) * D_MODEL ** -0.5,
        "ffn_conv_w": jax.random.normal(ks[15], (DEPTH_2, FFN_CONV, D_FF), f32) * FFN_CONV ** -0.5,
        "ffn_conv_b": 0.01 * jax.random.normal(ks[16], (DEPTH_2, D_FF), f32),
        "w_down": jax.random.normal(ks[17], (DEPTH_2, D_FF, D_MODEL), f32) * D_FF ** -0.5,
        "ffn_post_g": gain(ks[18], D_MODEL),
    }

def second_block(x, meta_tokens, mix_pre_g, w_in, ssd_conv_w, ssd_conv_b, ssd_dt_bias,
              ssd_a_log, ssd_d, ssd_norm_g, sb_norm_g, w_out, mix_post_g, ffn_pre_g,
              w_up, ffn_conv_w, ffn_conv_b, w_down, ffn_post_g):
    Bsz = x.shape[0]
    meta = jnp.broadcast_to(meta_tokens.astype(x.dtype)[None], (Bsz, N_META, x.shape[-1]))
    h = jnp.concatenate([meta, x], axis=1)
    L = h.shape[1]
    for l in range(DEPTH_2):
        xn = rms_norm_2(h, mix_pre_g[l])
        proj = xn @ w_in[l]
        z = proj[..., OFF_Z:OFF_XBC]
        xbc = proj[..., OFF_XBC:OFF_DT]
        dt_raw = proj[..., OFF_DT:OFF_Q]
        q = proj[..., OFF_Q:OFF_K].reshape(Bsz, L, SB_HEADS, SB_HEAD_DIM)
        k = proj[..., OFF_K:OFF_V].reshape(Bsz, L, SB_HEADS, SB_HEAD_DIM)
        v = proj[..., OFF_V:IN_COLS].reshape(Bsz, L, SB_HEADS, SB_HEAD_DIM)
        y_ssd = ssd_mixer(z, xbc, dt_raw, ssd_conv_w[l], ssd_conv_b[l], ssd_dt_bias[l],
                          ssd_a_log[l], ssd_d[l], ssd_norm_g[l])
        y_sb = rms_norm_2(stick_breaking_attention(q, k, v).reshape(Bsz, L, SB_WIDTH), sb_norm_g[l])
        mix = jnp.concatenate([y_ssd, y_sb], axis=-1) @ w_out[l]
        h = h + rms_norm_2(mix, mix_post_g[l])
        xn = rms_norm_2(h, ffn_pre_g[l])
        gu = xn @ w_up[l]
        g = causal_dwconv(gu[..., :D_FF], ffn_conv_w[l], ffn_conv_b[l])
        f = (jax.nn.gelu(g, approximate=True) * gu[..., D_FF:]) @ w_down[l]
        h = h + rms_norm_2(f, ffn_post_g[l])
    return h[:, N_META:]


def setup_inputs(seed=0):
    out = dict(first_inputs(seed))
    for name, value in second_inputs(seed + 1).items():
        if name != "x":
            out[name + "_2"] = value
    return out


def reference(
    x, c, ctx, c_ctx, norm_g, ada_w, ada_b, w_in_ab, v_norm_g, spatial_w, spatial_b, w_out_ab,
    w_in_c, sink_logit, w_out_c, final_g, meta_tokens_2, mix_pre_g_2, w_in_2, ssd_conv_w_2,
    ssd_conv_b_2, ssd_dt_bias_2, ssd_a_log_2, ssd_d_2, ssd_norm_g_2, sb_norm_g_2, w_out_2,
    mix_post_g_2, ffn_pre_g_2, w_up_2, ffn_conv_w_2, ffn_conv_b_2, w_down_2, ffn_post_g_2,
):
    x = first_block(
        x, c, ctx, c_ctx, norm_g, ada_w, ada_b, w_in_ab, v_norm_g, spatial_w, spatial_b,
        w_out_ab, w_in_c, sink_logit, w_out_c, final_g,
    )
    return second_block(
        x, meta_tokens_2, mix_pre_g_2, w_in_2, ssd_conv_w_2, ssd_conv_b_2, ssd_dt_bias_2,
        ssd_a_log_2, ssd_d_2, ssd_norm_g_2, sb_norm_g_2, w_out_2, mix_post_g_2, ffn_pre_g_2,
        w_up_2, ffn_conv_w_2, ffn_conv_b_2, w_down_2, ffn_post_g_2,
    )


_drawn_inputs = setup_inputs


def setup_inputs(seed=0):
    import zlib

    import numpy as np

    out = dict(_drawn_inputs(seed))
    spreads = {}
    factors = {'ctx': 2.9,
     'norm_g': 5.743,
     'v_norm_g': 8.0,
     'spatial_b': 8.0,
     'sink_logit': 8.0,
     'ssd_conv_b_2': 6.845,
     'ffn_conv_b_2': 8.0}
    for name, (base, spread) in spreads.items():
        noise = np.random.default_rng([zlib.crc32(name.encode()), seed]).standard_normal(out[name].shape)
        drawn = base * np.exp(spread * noise) if base else spread * noise
        out[name] = __import__('jax').numpy.asarray(drawn.astype(out[name].dtype))
    for name, factor in factors.items():
        out[name] = (out[name] * factor).astype(out[name].dtype)
    return out
```

```python
from contextlib import ExitStack

import numpy as np

import concourse.bass as bass
from concourse import mybir

ALU = mybir.AluOpType
ACT = mybir.ActivationFunctionType
AX = mybir.AxisListType
F32 = mybir.dt.float32
F32R = mybir.dt.float32r

P = 128
D = 1024
KC = D // P
S = 512
CTX = 256
META = 16
SX = S + CTX
T2 = META + S
PAD = P - META
TP = PAD + T2
NT = TP // P
HALF = T2 // 2
GRID_W = 64
EPS = 1e-6
NEG = -1e30
FF = 2816
FC = FF // P
AB_IN = 2560
HEAD = 64
ATT_SCALE = HEAD ** -0.5
ROPE_BASE = 10000.0
XBC = 1536
XC = XBC // P
OFF_XBC, OFF_DT = 1024, 2560
OFF_Q, OFF_K, OFF_V = 2576, 3600, 4624
DK = 11

STREAM = [("uv", 8, 1), ("ga", 4, 1), ("xb", 4, 1), ("gb", 4, 1), ("wo_ab", 8, 1),
          ("q", 8, 1), ("kv", 4, 1), ("gc", 8, 1), ("wo_c", 8, 1),
          ("z", 8, 1), ("xbc", 12, 1), ("dt", 1, 1), ("sb", 24, 1),
          ("wo_2", 16, 2), ("up", 44, 1), ("down", 16, 2)]
SLAB0, BLOCK0, SLABS, PER = {}, {}, {}, {}
_g = _b = 0
for _name, _n, _per in STREAM:
    SLAB0[_name], BLOCK0[_name], SLABS[_name], PER[_name] = _g, _b, _n, _per
    _g += _n
    _b += _n // _per

VEC_A = {"norm_g": 0, "ada_b": 16, "c": 64, "c_ctx": 72, "final_g": 80, "mix_pre": 88,
         "ssd_norm": 96, "sb_norm": 104, "mix_post": 112}
VEC_B = {"conv_w": 0, "conv_b": 48, "ffn_b": 60, "ffn_pre": 82, "ffn_post": 90, "v_norm": 98}
COL = {**VEC_A, **{k: 128 + v for k, v in VEC_B.items()}, "ffn_w": 256}
VEC_ROWS = (120, 102, 66)

OP_DONE = {"l0": 8, "y0": 16, "l1": 24, "y1": 32, "pre": 40, "ssd": 48, "sbn": 56, "ffn": 64}


class Steps:

    def __init__(self, eng, sem):
        self.eng, self.sem, self.n, self.i, self.per = eng, sem, 0, None, 0

    def __call__(self, ins):
        self.n += 1
        ins.then_inc(self.sem, 1)

    def wait(self):
        self.eng.wait_ge(self.sem, self.n if self.i is None else self.n + self.i * self.per)

    def begin(self, i, per):
        self.i, self.per, self.at = i, per, self.n

    def end(self, count):
        assert self.n - self.at == self.per, (self.n - self.at, self.per)
        self.n = self.at + count * self.per
        self.i = None


def shape_constants():
    r = np.arange(P)
    ident = np.eye(P)
    tri = (r[:, None] <= r[None, :]) * 1.0
    at_or_after = np.where(r[None, :] >= r[:, None], 0.0, NEG)
    at_or_before = np.where(r[None, :] <= r[:, None], 0.0, NEG)
    before = np.where(r[None, :] < r[:, None], 0.0, NEG)
    t = np.arange(S)
    d = r % HEAD
    nf = HEAD // 4
    inv = np.float32(ROPE_BASE) ** (-np.arange(nf, dtype=np.float32) / np.float32(nf))
    place = np.where((d // 32)[:, None] == 0, (t // GRID_W)[None, :], (t % GRID_W)[None, :]).astype(np.float32)
    ang = (place * inv[d % nf][:, None].astype(np.float32)).astype(np.float64)
    sign = np.where(d % 32 < nf, -1.0, 1.0)[:, None]
    a = 2 * np.pi * np.outer(r, r) / P
    b = 2 * np.pi * (np.outer(t, t) % S) / S
    seq = np.stack([np.cos(b), -np.sin(b)], 1) / np.sqrt(S)
    seq = seq.reshape(S // P, P, 2, S).transpose(1, 0, 2, 3).reshape(P, -1)
    parts = {"ident": ident, "tri": tri, "at_or_after": at_or_after, "at_or_before": at_or_before,
             "before": before, "cos": np.cos(ang), "sin": np.sin(ang) * sign,
             "dft_ch": np.concatenate([np.cos(a), np.sin(a)], 1) / np.sqrt(P), "dft_seq": seq}
    first, n = {}, 0
    for name, v in parts.items():
        first[name] = n
        n += v.shape[1]
    return np.ascontiguousarray(np.concatenate(list(parts.values()), 1).astype(np.float32)), first


CONST_FIRST = shape_constants()[1]


def two_blocks(nc, x, c, ctx, c_ctx, norm_g, ada_w, ada_b, w_in_ab, v_norm_g, spatial_w, spatial_b,
               w_out_ab, w_in_c, sink_logit, w_out_c, final_g, meta_tokens_2, mix_pre_g_2, w_in_2,
               ssd_conv_w_2, ssd_conv_b_2, ssd_dt_bias_2, ssd_a_log_2, ssd_d_2, ssd_norm_g_2, sb_norm_g_2,
               w_out_2, mix_post_g_2, ffn_pre_g_2, w_up_2, ffn_conv_w_2, ffn_conv_b_2, w_down_2,
               ffn_post_g_2, consts, out):
    stack = ExitStack()
    with stack:
        cursor = [(nc.sbuf_base + 63) // 64 * 64]

        def at(name, shape, offset, dt=F32):
            return nc.alloc_sbuf_tensor_at(name, shape, dt, offset=offset)

        def size(shape):
            return (int(np.prod(shape[1:])) * 4 + 31) // 32 * 32

        def sb(name, shape, dt=F32):
            t = at(name, shape, cursor[0], dt)
            cursor[0] += size(shape)
            return t

        raw = sb("raw", [P, 2, KC, P])
        w_hi = sb("w_hi", [P, 2, KC, P], F32R)
        w_lo = sb("w_lo", [P, 2, KC, P], F32R)
        xT = sb("xT", [P, KC, T2])
        cols = sb("cols", [P, 3, P])
        mod = sb("mod", [P, 48, 2])
        modg = sb("modg", [P, 2, 2, KC])
        ident = sb("ident", [P, P])
        tri = sb("tri", [P, P])
        at_or_after = sb("at_or_after", [P, P])
        at_or_before = sb("at_or_before", [P, P])
        before = sb("before", [P, P])
        ones = sb("ones", [P, P])
        zeros = sb("zeros", [P, P])
        eps = sb("eps", [P, 8])
        stat = sb("stat", [P, 8])
        rstd = sb("rstd", [P, 8])
        cond = sb("cond", [P, KC, 2])
        bn = sb("bn", [P, 8])
        mv = sb("mv", [P, 8])
        sink = sb("sink", [P, 16])
        neg_sink = sb("neg_sink", [P, 16])
        neg_a = sb("neg_a", [P, 16])
        a_log = sb("a_log", [P, 16])
        skip = sb("skip", [P, KC])
        dt_bias = sb("dt_bias", [P, 8])
        sm = sb("sm", [P, 2, 8])
        stage0 = cursor[0]

        def plan(*items, start=None):
            at_ = stage0 if start is None else start
            made = []
            for name, shape, *dt in items:
                made.append(at(name, shape, at_, *dt))
                at_ += size(shape)
            assert at_ <= nc.sbuf_usable_end, (items[-1][0], at_, nc.sbuf_usable_end)
            return made

        ctxT, op_hi, op_lo = plan(("ctxT", [P, KC, CTX]), ("op_hi", [P, KC, SX], F32R),
                                  ("op_lo", [P, KC, SX], F32R))
        layer0 = stage0 + size([P, KC, CTX]) + 2 * size([P, KC, SX])
        ada_ring, = plan(("ada_ring", [P, 8, KC, P]), start=stage0 + size([P, KC, CTX]))
        zT, dft_ch, dft_seq, sw, swT, s_bias, vt, pq = plan(
            ("zT", [P, 20, SX]), ("dft_ch", [P, 2 * P]), ("dft_seq", [P, S // P, 2, S]),
            ("sw", [P, 4, P]), ("swT", [P, 4, P]), ("s_bias", [P, 4, P]),
            ("vt", [P, SX // P, S]), ("pq", [P, SX // P, 2 * P]), start=layer0)
        x_in, ctx_in, meta_in, vec_in = plan(
            ("x_in", [P, S // P, D]), ("ctx_in", [P, CTX // P, D]), ("meta_in", [META, D]),
            ("vec_in", [P, 3, P]), start=layer0)
        tail0 = layer0 + sum(size(s) for s in ([P, 20, SX], [P, 2 * P], [P, S // P, 2, S], [P, 4, P],
                                               [P, 4, P], [P, 4, P]))
        sq0, hp0 = plan(("sq0", [P, 2, SX]), ("hp0", [P, 3, SX]), start=tail0)
        gmlp, = plan(("gmlp", [P, SX]), start=tail0 + size([P, SX // P, S]))
        q_t, kv_t, g_t, k_dup, v_tok, cos, sin, q_st, rot, k_st, v_st, p_sb, pT = plan(
            ("q_t", [P, KC, S]), ("kv_t", [P, 4, SX]), ("g_t", [P, KC, S]), ("k_dup", [P, 4, SX]),
            ("v_tok", [P, SX // P, CTX]), ("cos", [P, S]), ("sin", [P, S]), ("q_st", [P, 2, S]),
            ("rot", [P, 2, S]), ("k_st", [P, SX]), ("v_st", [P, SX // P, HEAD]),
            ("p_sb", [P, 2, 640]), ("pT", [P, 2, 640]), start=layer0)
        sq1, hp1 = plan(("sq1", [P, 2, SX]), ("hp1", [P, 3, SX]),
                        start=layer0 + 2 * size([P, KC, S]) + size([P, 4, SX]))
        xn_hi, xn_lo, zs, xbc = plan(("xn_hi", [P, KC, T2], F32R), ("xn_lo", [P, KC, T2], F32R),
                                     ("zs", [P, KC, TP]), ("xbc", [P, XC + 1, TP]))
        mixer = stage0 + 2 * size([P, KC, T2]) + size([P, KC, TP]) + size([P, XC + 1, TP])
        y_hi, y_lo = plan(("y_hi", [P, 2 * KC, T2], F32R), ("y_lo", [P, 2 * KC, T2], F32R))
        (xst, b_tok, xdt, xdd, seg, cexp, prev, conv, dt_t, dt_k, adt, acs, dec, dtm, ysb) = plan(
            ("xst", [P, XC, P]), ("b_tok", [P, 2 * P]), ("xdt", [P, D]), ("xdd", [P, D]),
            ("seg", [P, 16, P]), ("cexp", [P, 16, P]), ("prev", [P, D]), ("conv", [P, 2, T2]),
            ("dt_t", [P, P]), ("dt_k", [P, 16]), ("adt", [P, 16]), ("acs", [P, 32]), ("dec", [P, 32]),
            ("dtm", [P, 3, T2]), ("ysb", [P, KC, T2]), start=mixer)
        qs, ks, vs, v_sb, sb_abs, sb_relu, sb_exp, sb_sum, sb_w, sb_wT = plan(
            ("qs", [P, 2, T2]), ("ks", [P, 2, T2]), ("vs", [P, 2, T2]), ("v_sb", [P, 2, NT, P]),
            ("sb_abs", [P, T2]), ("sb_relu", [P, T2]), ("sb_exp", [P, T2]), ("sb_sum", [P, T2]),
            ("sb_w", [P, T2]), ("sb_wT", [P, NT, P]), start=mixer)
        mixT, sq2, hp2 = plan(("mixT", [P, KC, T2]), ("sq2", [P, 2, T2]), ("hp2", [P, 3, T2]), start=mixer)
        f_hi, f_lo, u_hi, u_lo, gp, gacc, fgl, fT = plan(
            ("f_hi", [P, FC, T2], F32R), ("f_lo", [P, FC, T2], F32R), ("u_hi", [P, KC, T2], F32R),
            ("u_lo", [P, KC, T2], F32R), ("gp", [P, T2 + 8]), ("gacc", [P, T2]), ("fgl", [P, T2]),
            ("fT", [P, KC, T2]))
        down0 = stage0 + 2 * size([P, FC, T2])
        raw_d, wd_hi, wd_lo = plan(("raw_d", [P, 2, DK, P]), ("wd_hi", [P, 2, DK, P], F32R),
                                   ("wd_lo", [P, 2, DK, P], F32R), start=down0)
        ffn_tail = down0 + 2 * size([P, KC, T2])
        sq3, hp3 = plan(("sq3", [P, 2, T2]), ("hp3", [P, 3, T2]), start=ffn_tail)
        sq4, hp4 = plan(("sq4", [P, 2, T2]), ("hp4", [P, 3, T2]), start=down0 + 6 * DK * P * 4)
        y_out, = plan(("y_out", [P, S // P, D]), start=stage0)

        ps = stack.enter_context(nc.psum_tensor("ps", [P, 8 * 512], F32))

        def bank(b, n=1):
            return ps[:, 512 * b:512 * (b + n)]

        gemm_ps = [bank(0, 2), bank(2, 2)]
        pair_ps = [bank(4, 2), bank(6, 2)]

        def sem(name):
            return stack.enter_context(nc.semaphore(name))

        names = """vec_in x_in consts_in small_in vec_turned cols_ready cond_ready x_turned x_ready
            ada_used mod_ready fill_ready raw0 raw1 rawd0 rawd1 split slab_done evac0 evac1 slab_taken
            sq sq_used ssq std rstd rstd_rows hp op_hi op_ready norm_done
            v_turned v_stat v_std v_ready sw_turned sw_ready spatial ya_ready ch_dft pq_ready seq_dft yb_ready
            rope_ready vtok_turned vtok_ready att_in scores nmax exps probs p_turned p_copied att_out att_o
            conv_in conv_done dt_e dt_l dt_ready chunk_in chunk_turned chunk_scaled chunk_b chunk_acs dec_in dec_ready
            chunk_e seg_ready seg_e ssd_operands ssd_y ssd_state ssd_used
            qkv_in sb_vt sb_v sb_scores sb_in sb_l sb_d sb_wr sb_wt sb_wc sb_o sb_y
            gate_conv gelu ffn_f ffn_hi ffn_used out_turned out_ready stored
            pe_gate act_steps dve_steps pool_steps""".split()
        s = {n: sem("s_" + n) for n in names}
        s_ada_in = [sem(f"s_ada_in{j}") for j in range(8)]
        s_raw = [s["raw0"], s["raw1"]]
        s_rawd = [s["rawd0"], s["rawd1"]]
        s_evac = [s["evac0"], s["evac1"]]

        SMALL = 16 * 7

        def col(name, k, n=1):
            i = COL[name] + k
            return cols[:, i // P, i % P:i % P + n]

        def block_done(name, n):
            return SLAB0[name] + n * PER[name]

        def all_evacuated(eng, name):
            last = BLOCK0[name] + SLABS[name] // PER[name]
            eng.wait_ge(s_evac[0], 1 + (last + 1) // 2)
            eng.wait_ge(s_evac[1], 1 + last // 2)

        def seg2(ap):
            return ap.rearrange("p (h n) -> p h n", h=2)[:, :, 0:HALF]

        def two(ap):
            return ap.rearrange("p (h n) -> p h n", h=2)

        SEG_X = [(0, S)]
        SEG_XC = [(0, S), (S, CTX)]
        SEG_2 = [(0, HALF), (HALF, HALF)]
        TILES_XC = [(t * P, P) for t in range(SX // P)]
        TILES_X = TILES_XC[:S // P]
        TILES_2 = [(0, META)] + [(META + t * P, P) for t in range(S // P)]

        def lat(k):
            return xT[:, k, META:T2]

        NORMS = {
            "l0": (0, TILES_XC, 0, sq0, hp0), "l1": (1, TILES_XC, 0, sq1, hp1),
            "final": (2, TILES_X, 0, sq1, hp1), "pre": (3, TILES_2, PAD, sq2, hp2),
            "ssd": (4, TILES_2, PAD, sq2, hp2), "sbn": (5, TILES_2, PAD, sq2, hp2),
            "post": (6, TILES_2, PAD, sq2, hp2), "ffn": (7, TILES_2, PAD, sq3, hp3),
            "fin": (8, TILES_2, PAD, sq4, hp4)}
        HP0 = {"l0": 0, "l1": 8, "pre": 16, "ssd": 24, "sbn": 32, "ffn": 40}

        def norm_sources(name, k):
            if name in ("l0", "l1"):
                layer = int(name[1])
                return [(lat(k), 0, S, modg[:, layer, 0, k:k + 1], mod[:, 24 * layer + k, 0:1]),
                        (ctxT[:, k, :], S, CTX, modg[:, layer, 1, k:k + 1], mod[:, 24 * layer + k, 1:2])]
            if name == "final":
                return [(lat(k), 0, S, col("final_g", k), None)]
            src, gain = {"pre": (xT[:, k, :], "mix_pre"), "ssd": (zs[:, k, PAD:TP], "ssd_norm"),
                         "sbn": (ysb[:, k, :], "sb_norm"), "post": (mixT[:, k, :], "mix_post"),
                         "ffn": (xT[:, k, :], "ffn_pre"), "fin": (fT[:, k, :], "ffn_post")}[name]
            return [(src, 0, T2, col(gain, k), None)]

        OPERAND = {"l0": (op_hi, op_lo, 0), "l1": (op_hi, op_lo, 0), "pre": (xn_hi, xn_lo, 0),
                   "ssd": (y_hi, y_lo, 0), "sbn": (y_hi, y_lo, KC), "ffn": (u_hi, u_lo, 0)}

        def rstd_rows(name, c0, n):
            base = NORMS[name][2]
            return pair_ps[0][:, base + c0:base + c0 + n]

        def y0_chunk(k):
            return zT[:, k if k < 4 else 8 + k, :]

        def att_lat(n):
            lo, hi = max(n - 1, 0), min(n + 1, S // P - 1)
            return lo, hi - lo + 1

        UNITS = [(c2, n, par) for c2 in range(2) for n in range(S // P) for par in range(2)]
        SBU = [(par, blk) for par in range(2) for blk in range(NT)]

        def sb_shape(blk):
            return (META, 0, META) if blk == 0 else (P, META + (blk - 1) * P, META + blk * P)

        block = stack.enter_context(nc.Block())

        @block.sync
        def _(sp):
            for tile, rows in ((0, [(norm_g, "norm_g"), (ada_b, "ada_b"), (c, "c"), (c_ctx, "c_ctx"),
                                    (final_g, "final_g"), (mix_pre_g_2, "mix_pre"), (ssd_norm_g_2, "ssd_norm"),
                                    (sb_norm_g_2, "sb_norm"), (mix_post_g_2, "mix_post")]),
                               (1, [(ssd_conv_w_2, "conv_w"), (ssd_conv_b_2, "conv_b"), (ffn_conv_b_2, "ffn_b"),
                                    (ffn_pre_g_2, "ffn_pre"), (ffn_post_g_2, "ffn_post"), (v_norm_g, "v_norm")]),
                               (2, [(ffn_conv_w_2, "ffn_w")])):
                for src, name in rows:
                    n = src.shape[0] // P
                    r = COL[name] - P * tile
                    flat = src.rearrange("(k p) -> k p", p=P)
                    sp.dma_start(vec_in[r:r + n, tile, :], flat).then_inc(s["vec_in"], 16)
            for name, dst in (("ident", ident), ("tri", tri), ("at_or_after", at_or_after),
                              ("at_or_before", at_or_before), ("before", before)):
                f = CONST_FIRST[name]
                sp.dma_start(dst[:, :], consts[:, f:f + P]).then_inc(s["consts_in"], 16)
            sp.dma_start(x_in[:, :, :], x.rearrange("(t p) d -> p t d", p=P)).then_inc(s["x_in"], 16)
            sp.dma_start(ctx_in[:, :, :], ctx.rearrange("(t p) d -> p t d", p=P)).then_inc(s["x_in"], 16)
            sp.dma_start(meta_in[:, :], meta_tokens_2).then_inc(s["x_in"], 16)
            ada = [ada_w[layer].rearrange("(k p) n -> p k n", p=P) for layer in range(2)]
            for layer in range(2):
                with sp.Fori(0, 3) as i:
                    for j in range(8):
                        sp.wait_ge(s["ada_used"], 24 * layer + 8 * i + j + 1)
                        sp.dma_start(ada_ring[:, j, :, :], ada[layer][:, :, bass.ds(i * 1024 + j * P, P)])\
                          .then_inc(s_ada_in[j], 16)
            f = CONST_FIRST["dft_ch"]
            sp.dma_start(dft_ch[:, :], consts[:, f:f + 2 * P]).then_inc(s["small_in"], 16)
            f = CONST_FIRST["dft_seq"]
            sp.dma_start(dft_seq[:, :, :, :].rearrange("p a b n -> p (a b n)"),
                         consts[:, f:f + 2 * S * S // P]).then_inc(s["small_in"], 16)
            sp.dma_start(sw[:, :, :], spatial_w.rearrange("h q p -> q h p")).then_inc(s["small_in"], 16)
            sp.dma_start(s_bias[:, :, :], spatial_b.partition_broadcast(P)).then_inc(s["small_in"], 16)
            sp.dma_start(sink[:, :], sink_logit.partition_broadcast(P)).then_inc(s["small_in"], 16)
            sp.dma_start(a_log[:, :], ssd_a_log_2.partition_broadcast(P)).then_inc(s["small_in"], 16)
            sp.dma_start(dt_bias[0:16, 0:1], ssd_dt_bias_2.rearrange("(h o) -> h o", o=1),
                         allow_slow_non_contiguous=True).then_inc(s["small_in"], 16)
            d_by_half = ssd_d_2.rearrange("(k h) -> h k", h=2)
            for h in range(2):
                sp.dma_start(skip[HEAD * h:HEAD * h + HEAD, :], d_by_half[h].partition_broadcast(HEAD),
                             allow_slow_non_contiguous=True).then_inc(s["consts_in"], 16)

            def cols_of(w):
                return w.rearrange("(k p) n -> p k n", p=P)

            def stream(name, src):
                u = 2 if SLABS[name] % 2 == 0 else 1
                g0 = SLAB0[name]

                def load(i, j):
                    if not (isinstance(i, int) and g0 + j + u * i < 2):
                        sp.wait_ge(s["split"], g0 + j - 1 + u * i)
                    sp.dma_start(raw[:, (g0 + j) % 2, :, :], src(i, j)).then_inc(s_raw[(g0 + j) % 2], 16)

                first = 0
                if g0 == 0:
                    load(0, 0)
                    load(0, 1)
                    first = 1
                if SLABS[name] // u - first == 1:
                    for j in range(u):
                        load(first, j)
                    return
                with sp.Fori(first, SLABS[name] // u) as i:
                    for j in range(u):
                        load(i, j)

            def plain(w, c0):
                return lambda i, j: cols_of(w)[:, :, bass.ds(i * 2 * P + (j * P + c0), P)]

            stream("uv", plain(w_in_ab, 0))
            stream("ga", plain(w_in_ab, 1024))
            stream("xb", plain(w_in_ab, 1536))
            stream("gb", plain(w_in_ab, 2048))
            stream("wo_ab", plain(w_out_ab, 0))
            sp.wait_ge(s["op_ready"], OP_DONE["l1"])
            for name, dst in (("cos", cos), ("sin", sin)):
                f = CONST_FIRST[name]
                sp.dma_start(dst[:, :], consts[:, f:f + S]).then_inc(s["consts_in"], 16)
            stream("q", plain(w_in_c, 0))
            stream("kv", plain(w_in_c, 1024))
            stream("gc", plain(w_in_c, 1536))
            stream("wo_c", plain(w_out_c, 0))
            stream("z", plain(w_in_2, 0))
            stream("xbc", plain(w_in_2, OFF_XBC))
            stream("dt", lambda i, j: cols_of(w_in_2)[:, :, OFF_DT:OFF_DT + P])
            g0 = SLAB0["sb"]
            with sp.Fori(0, 4) as i:
                for j in range(6):
                    sp.wait_ge(s["split"], g0 + j - 1 + 6 * i)
                    c0 = (OFF_Q, OFF_K, OFF_V)[j % 3] + (j // 3) * P
                    sp.dma_start(raw[:, (g0 + j) % 2, :, :], cols_of(w_in_2)[:, :, bass.ds(i * 2 * P + c0, P)])\
                      .then_inc(s_raw[(g0 + j) % 2], 16)
            wo2 = w_out_2.rearrange("(h k p) n -> p h k n", h=2, p=P)
            g0 = SLAB0["wo_2"]
            with sp.Fori(0, KC) as i:
                for h in range(2):
                    sp.wait_ge(s["split"], g0 + h - 1 + 2 * i)
                    sp.dma_start(raw[:, (g0 + h) % 2, :, :], wo2[:, h, :, bass.ds(i * P, P)])\
                      .then_inc(s_raw[(g0 + h) % 2], 16)
            g0 = SLAB0["up"]
            with sp.Fori(0, FC) as i:
                for h in range(2):
                    sp.wait_ge(s["split"], g0 + h - 1 + 2 * i)
                    sp.dma_start(raw[:, (g0 + h) % 2, :, :], cols_of(w_up_2)[:, :, bass.ds(i * P + h * FF, P)])\
                      .then_inc(s_raw[(g0 + h) % 2], 16)
            wd = w_down_2.rearrange("(h k p) n -> p h k n", h=2, p=P)
            g0 = SLAB0["down"]
            sp.wait_ge(s["slab_done"], g0)
            for h in range(2):
                sp.dma_start(raw_d[:, h, :, :], wd[:, h, :, 0:P]).then_inc(s_rawd[h], 16)
            with sp.Fori(1, KC) as i:
                for h in range(2):
                    sp.wait_ge(s["split"], g0 + h - 1 + 2 * i)
                    sp.dma_start(raw_d[:, h, :, :], wd[:, h, :, bass.ds(i * P, P)]).then_inc(s_rawd[h], 16)
            for t in range(S // P):
                sp.wait_ge(s["out_ready"], t + 1)
                sp.dma_start(out[t * P:(t + 1) * P, :], y_out[:, t, :]).then_inc(s["stored"], 16)
            sp.wait_ge(s["stored"], 16 * (S // P))

        @block.gpsimd
        def _(pool):
            steps = Steps(pool, s["pool_steps"])
            nc.gpsimd.memset(ones[:, :], 1.0).then_inc(s["fill_ready"], 1)
            nc.gpsimd.memset(zeros[:, :], 0.0).then_inc(s["fill_ready"], 1)
            nc.gpsimd.memset(eps[:, :], EPS).then_inc(s["fill_ready"], 1)

            def split(r, hi, lo):
                pool.sem_inc(s["slab_taken"], 1)
                steps(nc.gpsimd.tensor_scalar(hi, r, 1.0, 0.0, ALU.mult, ALU.add))
                steps.wait()
                nc.gpsimd.tensor_tensor(lo, r, hi.bitcast(F32), ALU.subtract).then_inc(s["split"], 1)

            def slab(i, j, before_it):
                pool.wait_ge(s_raw[j], 16 * i + 16)
                if before_it:
                    pool.wait_ge(s["slab_done"], 2 * i + j - 1)
                split(raw[:, j, :, :], w_hi[:, j, :, :], w_lo[:, j, :, :])

            for j in range(2):
                slab(0, j, False)
            last = SLAB0["down"]
            n = last // 2
            with pool.Fori(1, n) as i:
                steps.begin(i - 1, 2)
                for j in range(2):
                    slab(i, j, True)
                steps.end(n - 1)
            if last % 2:
                slab(n, 0, True)
            g0 = SLAB0["down"]
            pool.wait_ge(s["slab_done"], g0)
            for j in range(2):
                pool.wait_ge(s_rawd[j], 16)
                split(raw_d[:, j, :, :], wd_hi[:, j, :, :], wd_lo[:, j, :, :])
            with pool.Fori(1, KC) as i:
                steps.begin(i - 1, 2)
                for j in range(2):
                    pool.wait_ge(s_rawd[j], 16 * i + 16)
                    pool.wait_ge(s["slab_done"], g0 + 2 * i + j - 1)
                    split(raw_d[:, j, :, :], wd_hi[:, j, :, :], wd_lo[:, j, :, :])
                steps.end(KC - 1)

        @block.scalar
        def _(act):
            steps = Steps(act, s["act_steps"])

            def norm_squares(name):
                k0, tiles, base, sq, hp = NORMS[name]
                for k in range(KC):
                    if 8 * k0 + k - 1 > 0:
                        act.wait_ge(s["sq_used"], 8 * k0 + k - 1)
                    parts = norm_sources(name, k)
                    for src, c0, n, _, _ in parts:
                        ins = nc.scalar.activation(sq[:, k % 2, c0:c0 + n], src, ACT.Square)
                    ins.then_inc(s["sq"], 1)
                act.wait_ge(s["ssq"], k0 + 1)
                nc.scalar.activation(stat[:, 0:len(tiles)], pair_ps[1][:, 0:len(tiles)], ACT.Sqrt,
                                     bias=eps[:, 0:1], scale=1.0 / D).then_inc(s["std"], 1)

            def norm_hi(name):
                _, _, _, _, hp = NORMS[name]
                hi, _, c = OPERAND[name]
                for k in range(KC):
                    act.wait_ge(s["hp"], HP0[name] + k + 1)
                    for _, c0, n, _, shift in norm_sources(name, k):
                        if shift is None:
                            ins = nc.scalar.copy(hi[:, c + k, c0:c0 + n], hp[:, k % 3, c0:c0 + n])
                        else:
                            ins = nc.scalar.activation(hi[:, c + k, c0:c0 + n], hp[:, k % 3, c0:c0 + n],
                                                       ACT.Identity, bias=shift)
                    ins.then_inc(s["op_hi"], 1)

            def evacuate(name, dst, src, func, scale=1.0):
                n, b0 = SLABS[name] // PER[name], BLOCK0[name]
                u = 2 if n % 2 == 0 else 1
                if n == 1:
                    act.wait_ge(s["slab_done"], block_done(name, 1))
                    nc.scalar.activation(dst(0), src(gemm_ps[b0 % 2]), func).then_inc(s_evac[b0 % 2], 1)
                    return
                with act.Fori(0, n // u) as i:
                    for j in range(u):
                        act.wait_ge(s["slab_done"], block_done(name, j + 1) + u * PER[name] * i)
                        nc.scalar.activation(dst(i * u + j), src(gemm_ps[(b0 + j) % 2]), func)\
                          .then_inc(s_evac[(b0 + j) % 2], 1)

            act.sem_inc(s_evac[0], 1)
            act.sem_inc(s_evac[1], 1)
            act.sem_inc(s["ada_used"], 8)
            act.sem_inc(s["conv_done"], 2)
            act.sem_inc(s["sb_y"], 1)
            act.wait_ge(s["cols_ready"], 3)
            for k, name in enumerate(("c", "c_ctx")):
                nc.scalar.activation(cond[:, :, k], col(name, 0, KC), ACT.Silu).then_inc(s["cond_ready"], 1)
            act.wait_ge(s["x_ready"], 13)
            act.wait_ge(s["fill_ready"], 3)
            norm_squares("l0")
            act.wait_ge(s["mod_ready"], 1)
            norm_hi("l0")

            def wide(ps_):
                return ps_[:, 0:SX].unsqueeze(1)

            def zdst(b0):
                return lambda b: zT[:, bass.ds(b + b0, 1), :]

            evacuate("uv", zdst(0), wide, ACT.Copy)
            evacuate("ga", zdst(8), wide, ACT.Silu)
            evacuate("xb", zdst(12), wide, ACT.Copy)
            evacuate("gb", zdst(16), wide, ACT.Silu)
            for t in range(SX // P):
                act.wait_ge(s["v_stat"], t + 1)
                nc.scalar.activation(mv[:, 2:3], mv[:, 1:2], ACT.Sqrt, bias=eps[:, 0:1]).then_inc(s["v_std"], 1)
            for g in range(4):
                act.wait_ge(s["ch_dft"], g + 1)
                if g:
                    act.wait_ge(s["seq_dft"], g)
                nc.scalar.copy(pq[:, :, :], ps[:, 4 * 512:7 * 512].rearrange("p (t n) -> p t n", t=SX // P))\
                  .then_inc(s["pq_ready"], 1)
            for k in range(KC):
                if k == 0:
                    act.wait_ge(s["ya_ready"], 4)
                    act.wait_ge(s["slab_done"], SLAB0["wo_ab"])
                if k >= 4:
                    act.wait_ge(s["yb_ready"], k - 3)
                nc.scalar.copy(op_hi[:, k, :], y0_chunk(k)).then_inc(s["op_hi"], 1)
            all_evacuated(act, "wo_ab")
            norm_squares("l1")
            norm_hi("l1")

            def narrow(ps_):
                return ps_[:, 0:S].unsqueeze(1)

            evacuate("q", lambda b: q_t[:, bass.ds(b, 1), :], narrow, ACT.Copy)
            evacuate("kv", lambda b: kv_t[:, bass.ds(b, 1), :], wide, ACT.Copy)
            evacuate("gc", lambda b: g_t[:, bass.ds(b, 1), :], narrow, ACT.Silu)
            nu = len(UNITS)
            with act.Fori(0, 4) as i:
                steps.begin(i, 0)
                for u in range(nu + 1):
                    if u < nu:
                        c2, n, par = UNITS[u]
                        w = att_lat(n)[1] * P
                        act.wait_ge(s["nmax"], nu * i + u + 1)
                        head = 2 * c2 + par
                        if u >= 2:
                            act.wait_ge(s["p_turned"], nu * i + u - 1)
                        nc.scalar.activation(p_sb[:, u % 2, 0:CTX + w], pair_ps[u % 2][:, CTX:S + w], ACT.Exp,
                                             bias=sm[:, u % 2, 1:2], scale=ATT_SCALE,
                                             accum_out=sm[:, u % 2, 3:4]).then_inc(s["exps"], 1)
                        nc.scalar.activation(sm[:, u % 2, 2:3], neg_sink[:, bass.ds(4 * i + head, 1)], ACT.Exp,
                                             bias=sm[:, u % 2, 1:2], scale=-1.0).then_inc(s["exps"], 1)
                    if u >= 1:
                        n = UNITS[u - 1][1]
                        w = att_lat(n)[1] * P
                        act.wait_ge(s["p_turned"], nu * i + u)
                        nc.scalar.copy(pT[:, (u - 1) % 2, 0:CTX + w], bank(0, 2)[:, 0:CTX + w])\
                          .then_inc(s["p_copied"], 1)
                steps.end(4)
            for k in range(KC):
                if k == 0:
                    act.wait_ge(s["att_o"], 8)
                nc.scalar.copy(op_hi[:, k, 0:S], g_t[:, k, :]).then_inc(s["op_hi"], 1)
            all_evacuated(act, "wo_c")
            norm_squares("final")
            act.wait_ge(s["norm_done"], 8)
            norm_squares("pre")
            norm_hi("pre")

            def halves(ps_):
                return seg2(ps_)

            evacuate("z", lambda b: two(zs[:, bass.ds(b, 1), PAD:TP].rearrange("p a n -> p (a n)")), halves,
                     ACT.Silu)
            evacuate("xbc", lambda b: two(xbc[:, bass.ds(b, 1), PAD:TP].rearrange("p a n -> p (a n)")), halves,
                     ACT.Copy)
            evacuate("dt", lambda b: two(xbc[:, XC, PAD:TP]), halves, ACT.Copy)
            with act.Fori(0, XC // 2) as i:
                for j in range(2):
                    act.wait_ge(s["conv_in"], 2 * i + j + 1)
                    nc.scalar.activation(xbc[:, bass.ds(2 * i + j, 1), PAD:TP], conv[:, j:j + 1, :], ACT.Silu)\
                      .then_inc(s["conv_done"], 1)
            nc.scalar.preload_act_table_set("natural_log_exp_and_others")
            act.wait_ge(s["small_in"], SMALL)
            steps(nc.scalar.activation(neg_a[:, :], a_log[:, :], ACT.Exp))
            act.wait_ge(s["dt_e"], 1)
            steps(nc.scalar.activation(dtm[0:16, 2, :], dtm[0:16, 1, :], ACT.Exp))
            steps.wait()
            nc.scalar.activation(dtm[0:16, 1, :], dtm[0:16, 2, :], ACT.Ln, bias=1.0).then_inc(s["dt_l"], 1)
            with act.Fori(0, NT) as t:
                act.wait_ge(s["dt_ready"], 1)
                act.wait_ge(s["ssd_used"], t + 1)
                nc.scalar.copy(xst[:, :, :], xbc[:, 0:XC, bass.ds(t * P, P)]).then_inc(s["chunk_in"], 1)
                nc.scalar.copy(dt_t[0:16, :], xbc[0:16, XC, bass.ds(t * P, P)]).then_inc(s["chunk_in"], 1)
                act.wait_ge(s["chunk_acs"], t + 1)
                nc.scalar.activation(cexp[:, :, :].rearrange("p h l -> p (h l)"), bank(0, 4), ACT.Exp)\
                  .then_inc(s["chunk_e"], 1)
                act.wait_ge(s["dec_in"], t + 1)
                nc.scalar.activation(dec[:, :], acs[:, :], ACT.Exp).then_inc(s["dec_ready"], 1)
                act.wait_ge(s["seg_ready"], t + 1)
                nc.scalar.activation(seg[:, :, :], seg[:, :, :], ACT.Exp).then_inc(s["seg_e"], 1)
            g0, b0 = SLAB0["sb"], BLOCK0["sb"]
            nu = len(SBU)
            act.wait_ge(s["ssd_used"], NT + 1)
            with act.Fori(0, 4) as i:
                for m in range(2):
                    for j, (dst, scale) in enumerate(((qs, ATT_SCALE), (ks, 1.0), (vs, 1.0))):
                        b = b0 + 3 * m + j
                        act.wait_ge(s["slab_done"], g0 + 3 * m + j + 1 + 6 * i)
                        nc.scalar.activation(two(dst[:, m, :]), seg2(gemm_ps[b % 2]), ACT.Copy, scale=scale)\
                          .then_inc(s_evac[b % 2], 1)
                    for u, (par, blk) in enumerate(SBU):
                        nq, q0, nk = sb_shape(blk)
                        done = 2 * nu * i + nu * m + u + 1
                        act.wait_ge(s["sb_in"], done)
                        nc.scalar.activation(sb_exp[0:nq, 0:nk], sb_abs[0:nq, 0:nk], ACT.Exp)\
                          .then_inc(s["sb_l"], 1)
                        act.wait_ge(s["sb_l"], 2 * done - 1)
                        nc.scalar.activation(sb_abs[0:nq, 0:nk], sb_exp[0:nq, 0:nk], ACT.Ln, bias=1.0)\
                          .then_inc(s["sb_l"], 1)
                        act.wait_ge(s["sb_d"], done)
                        nc.scalar.activation(sb_w[0:nq, 0:nk], sb_sum[0:nq, 0:nk], ACT.Exp).then_inc(s["sb_wr"], 1)
                        act.wait_ge(s["sb_wt"], done)
                        if blk:
                            nc.scalar.copy(sb_wT[0:META, 0, 0:nq], bank(0, 2)[0:META, 0:nq])
                            nc.scalar.copy(sb_wT[:, 1:1 + blk, :].rearrange("p a n -> p (a n)"),
                                           bank(0, 2)[:, P:P + blk * P]).then_inc(s["sb_wc"], 1)
                        else:
                            nc.scalar.copy(sb_wT[0:META, 0, 0:nq], bank(0, 2)[0:META, 0:nq])\
                              .then_inc(s["sb_wc"], 1)
            act.wait_ge(s["sb_y"], KC + 1)
            norm_squares("ssd")
            norm_hi("ssd")
            norm_squares("sbn")
            norm_hi("sbn")
            evacuate("wo_2", lambda b: two(mixT[:, bass.ds(b, 1), :].rearrange("p a n -> p (a n)")), halves,
                     ACT.Copy)
            all_evacuated(act, "wo_2")
            norm_squares("post")
            act.wait_ge(s["norm_done"], 16)
            norm_squares("ffn")
            norm_hi("ffn")
            g0, b0 = SLAB0["up"], BLOCK0["up"]
            with act.Fori(0, FC) as i:
                act.wait_ge(s["slab_done"], g0 + 1 + 2 * i)
                act.wait_ge(s["ffn_used"], i + 1)
                nc.scalar.copy(two(gp[:, 2:2 + T2]), seg2(gemm_ps[b0 % 2])).then_inc(s_evac[b0 % 2], 1)
                act.wait_ge(s["gate_conv"], i + 1)
                nc.scalar.activation(gacc[:, :], gacc[:, :], ACT.Gelu_apprx_tanh).then_inc(s["gelu"], 1)
                act.wait_ge(s["ffn_f"], i + 1)
                nc.scalar.copy(f_hi[:, bass.ds(i, 1), :], fgl[:, :].unsqueeze(1)).then_inc(s["ffn_hi"], 1)
            evacuate("down", lambda b: two(fT[:, bass.ds(b, 1), :].rearrange("p a n -> p (a n)")), halves,
                     ACT.Copy)
            all_evacuated(act, "down")
            norm_squares("fin")

        @block.vector
        def _(dve):
            steps = Steps(dve, s["dve_steps"])

            def norm_rstd(name):
                k0, tiles, _, _, _ = NORMS[name]
                dve.wait_ge(s["std"], k0 + 1)
                nc.vector.reciprocal(rstd[:, 0:len(tiles)], stat[:, 0:len(tiles)]).then_inc(s["rstd"], 1)
                dve.wait_ge(s["rstd_rows"], k0 + 1)

            def norm_operand(name):
                _, _, _, _, hp = NORMS[name]
                hi, lo, c = OPERAND[name]
                hi0 = OP_DONE[name] - KC
                for k in range(KC + 1):
                    if k < KC:
                        if k >= 3:
                            dve.wait_ge(s["op_ready"], hi0 + k - 2)
                        for src, c0, n, gain, _ in norm_sources(name, k):
                            ins = nc.vector.scalar_tensor_tensor(hp[:, k % 3, c0:c0 + n], src, gain,
                                                                 rstd_rows(name, c0, n), ALU.mult, ALU.mult)
                        ins.then_inc(s["hp"], 1)
                    if k >= 1:
                        dve.wait_ge(s["op_hi"], hi0 + k)
                        for _, c0, n, _, shift in norm_sources(name, k - 1):
                            o, h = lo[:, c + k - 1, c0:c0 + n], hi[:, c + k - 1, c0:c0 + n].bitcast(F32)
                            a = hp[:, (k - 1) % 3, c0:c0 + n]
                            if shift is None:
                                ins = nc.vector.tensor_tensor(o, a, h, ALU.subtract)
                            else:
                                ins = nc.vector.scalar_tensor_tensor(o, a, shift, h, ALU.add, ALU.subtract)
                        ins.then_inc(s["op_ready"], 1)

            for v in range(3):
                dve.wait_ge(s["vec_turned"], v + 1)
                r = VEC_ROWS[v]
                nc.vector.tensor_copy(cols[:, v, 0:r], bank(4 + v)[:, 0:r]).then_inc(s["cols_ready"], 1)
            for k in range(KC):
                dve.wait_ge(s["x_turned"], k + 1)
                nc.vector.tensor_copy(lat(k), bank(k % 4)[:, :]).then_inc(s["x_ready"], 1)
            for k in range(0, KC, 2):
                dve.wait_ge(s["x_turned"], KC + k // 2 + 1)
                nc.vector.tensor_copy(ctxT[:, k:k + 2, :].rearrange("p k n -> p (k n)"),
                                      bank(k // 2 % 4)[:, :]).then_inc(s["x_ready"], 1)
            dve.wait_ge(s["x_turned"], 13)
            nc.vector.tensor_copy(xT[:, :, 0:META], bank(0)[:, 0:KC * META].rearrange("p (k n) -> p k n", k=KC))\
              .then_inc(s["x_ready"], 1)
            dve.wait_ge(s["ada_used"], 8 + 48)
            steps(nc.vector.tensor_tensor(mod[:, :, :], bank(7)[:, 0:96].rearrange("p (n c) -> p n c", c=2),
                                          col("ada_b", 0, 48).unsqueeze(2).to_broadcast([P, 48, 2]), ALU.add))
            steps.wait()
            for layer in range(2):
                for k in range(2):
                    ins = nc.vector.scalar_tensor_tensor(
                        modg[:, layer, k, :], mod[:, 24 * layer + KC:24 * layer + 2 * KC, k], 1.0,
                        col("norm_g", KC * layer, KC), ALU.add, ALU.mult)
                    steps(ins)
            steps.wait()
            dve.sem_inc(s["mod_ready"], 1)
            norm_rstd("l0")
            norm_operand("l0")
            dve.wait_ge(s["sw_turned"], 1)
            nc.vector.tensor_copy(swT[:, :, :].rearrange("p h q -> p (h q)"), bank(7)[:, :]).then_inc(s["sw_ready"], 1)
            for t in range(SX // P):
                dve.wait_ge(s["v_turned"], t + 1)
                v_ps = bank(4 + t % 2)[:, :]
                if t:
                    dve.wait_ge(s["v_ready"], t)
                steps(nc.vector.bn_stats(bn[:, 0:6], v_ps))
                steps.wait()
                nc.vector.bn_aggr(mv[:, 0:2], bn[:, 0:6]).then_inc(s["v_stat"], 1)
                dve.wait_ge(s["v_std"], t + 1)
                steps(nc.vector.reciprocal(mv[:, 3:4], mv[:, 2:3]))
                steps.wait()
                nc.vector.tensor_scalar(vt[:, t, :], v_ps, mv[:, 0:1], mv[:, 3:4], ALU.subtract, ALU.mult)\
                  .then_inc(s["v_ready"], 1)
            dve.wait_ge(s["small_in"], SMALL)
            for h in range(4):
                dve.wait_ge(s["spatial"], h + 1)
                nt = SX // P
                steps(nc.vector.scalar_tensor_tensor(
                    gmlp[:, :].rearrange("p (t q) -> p t q", t=nt),
                    pair_ps[h % 2][:, 0:SX].rearrange("p (t q) -> p t q", t=nt), col("v_norm", h),
                    s_bias[:, h:h + 1, :].to_broadcast([P, nt, P]), ALU.mult, ALU.add))
                steps.wait()
                steps(nc.vector.tensor_tensor(zT[:, h, :], zT[:, h, :], gmlp[:, :], ALU.mult))
                steps.wait()
                nc.vector.tensor_tensor(zT[:, h, :], zT[:, h, :], zT[:, 8 + h, :], ALU.mult).then_inc(s["ya_ready"], 1)
            for g in range(4):
                dve.wait_ge(s["seq_dft"], g + 1)
                f_ps = gemm_ps[g % 2]
                nc.vector.tensor_tensor(zT[:, 12 + g, 0:S], f_ps[:, 0:S], zT[:, 16 + g, 0:S], ALU.mult)
                nc.vector.scalar_tensor_tensor(zT[:, 12 + g, S:SX], f_ps[:, S:SX], float(np.sqrt(S / CTX)),
                                               zT[:, 16 + g, S:SX], ALU.mult, ALU.mult).then_inc(s["yb_ready"], 1)
            for k in range(KC):
                dve.wait_ge(s["op_hi"], OP_DONE["l0"] + k + 1)
                if k == 0:
                    dve.wait_ge(s["ya_ready"], 4)
                    dve.wait_ge(s["yb_ready"], 4)
                nc.vector.tensor_tensor(op_lo[:, k, :], y0_chunk(k), op_hi[:, k, :].bitcast(F32), ALU.subtract)\
                  .then_inc(s["op_ready"], 1)

            def add_gated(name, layer, with_ctx):
                b0 = BLOCK0[name]
                with dve.Fori(0, KC // 2) as i:
                    for j in range(2):
                        dve.wait_ge(s["slab_done"], block_done(name, j + 1) + 2 * i)
                        o = gemm_ps[(b0 + j) % 2]
                        gate = mod[:, bass.ds(2 * i + (24 * layer + 2 * KC + j), 1), :]
                        x_k = xT[:, bass.ds(2 * i + j, 1), META:T2]
                        ins = nc.vector.scalar_tensor_tensor(x_k, o[:, 0:S].unsqueeze(1), gate[:, 0, 0:1], x_k,
                                                             ALU.mult, ALU.add)
                        if with_ctx:
                            c_k = ctxT[:, bass.ds(2 * i + j, 1), :]
                            ins = nc.vector.scalar_tensor_tensor(c_k, o[:, S:SX].unsqueeze(1), gate[:, 0, 1:2], c_k,
                                                                 ALU.mult, ALU.add)
                        ins.then_inc(s_evac[(b0 + j) % 2], 1)

            add_gated("wo_ab", 0, True)
            all_evacuated(dve, "wo_ab")
            norm_rstd("l1")
            norm_operand("l1")
            steps(nc.vector.tensor_scalar(neg_sink[:, :], sink[:, :], -1.0, None, ALU.mult))
            HALF_SWAP = [p ^ 16 for p in range(32)]
            dve.wait_ge(s["consts_in"], 16 * 9)
            all_evacuated(dve, "kv")
            for k in range(2):
                steps(nc.vector.stream_shuffle(rot[:, 0, :], kv_t[:, k, 0:S], HALF_SWAP))
                steps.wait()
                steps(nc.vector.tensor_tensor(rot[:, 0, :], rot[:, 0, :], sin[:, :], ALU.mult))
                steps(nc.vector.tensor_tensor(rot[:, 1, :], kv_t[:, k, 0:S], cos[:, :], ALU.mult))
                steps.wait()
                steps(nc.vector.tensor_tensor(kv_t[:, k, 0:S], rot[:, 0, :], rot[:, 1, :], ALU.add))
                steps.wait()
            for h in range(4):
                for half in range(2):
                    a = HEAD * (h % 2)
                    steps(nc.vector.tensor_copy(k_dup[HEAD * half:HEAD * half + HEAD, h, :],
                                                kv_t[a:a + HEAD, h // 2, :]))
            dve.wait_ge(s["vtok_turned"], 1)
            steps(nc.vector.tensor_copy(v_tok[:, :, :],
                                        bank(4, 3).rearrange("p (t n) -> p t n", t=SX // P)))
            steps.wait()
            dve.sem_inc(s["vtok_ready"], 1)
            all_evacuated(dve, "gc")
            nu = len(UNITS)
            per = 10 + 2 + sum(1 + (n > 0) + (n < 3) for _, n, _ in UNITS) + 2 * nu
            with dve.Fori(0, 4) as i:
                steps.begin(i, per)
                dve.wait_ge(s["att_out"], nu * i + nu)
                for c2 in range(2):
                    q_k = q_t[:, bass.ds(2 * i + c2, 1), :]
                    steps.wait()
                    steps(nc.vector.tensor_copy(rot[:, 1:2, :], q_k))
                    steps.wait()
                    steps(nc.vector.tensor_tensor(q_st[:, c2, :], rot[:, 1, :], cos[:, :], ALU.mult))
                    steps(nc.vector.stream_shuffle(rot[:, 0, :], rot[:, 1, :], HALF_SWAP))
                    steps.wait()
                    steps(nc.vector.tensor_tensor(rot[:, 0, :], rot[:, 0, :], sin[:, :], ALU.mult))
                    steps.wait()
                    steps(nc.vector.tensor_tensor(q_st[:, c2, :], q_st[:, c2, :], rot[:, 0, :], ALU.add))
                steps(nc.vector.tensor_copy(k_st[:, :].unsqueeze(1), k_dup[:, bass.ds(i, 1), :]))
                steps(nc.vector.tensor_copy(v_st[:, :, :], v_tok[:, :, bass.ds(HEAD * i, HEAD)]))
                steps.wait()
                dve.sem_inc(s["att_in"], 1)
                for u in range(nu + 1):
                    if u < nu:
                        c2, n, par = UNITS[u]
                        w = att_lat(n)[1] * P
                        sc = pair_ps[u % 2]
                        dve.wait_ge(s["scores"], nu * i + u + 1)
                        if n > 0:
                            steps(nc.vector.tensor_tensor(sc[:, S:S + P], sc[:, S:S + P], at_or_after[:, :], ALU.add))
                        if n < 3:
                            steps(nc.vector.tensor_tensor(sc[:, S + w - P:S + w], sc[:, S + w - P:S + w],
                                                          at_or_before[:, :], ALU.add))
                        steps.wait()
                        steps(nc.vector.tensor_reduce(sm[:, u % 2, 0:1], sc[:, CTX:S + w], AX.X, ALU.max))
                        steps.wait()
                        head = 2 * c2 + par
                        nc.vector.tensor_scalar(sm[:, u % 2, 1:2], sm[:, u % 2, 0:1], -ATT_SCALE,
                                                neg_sink[:, bass.ds(4 * i + head, 1)], ALU.mult, ALU.min)\
                          .then_inc(s["nmax"], 1)
                    if u >= 1:
                        v = (u - 1) % 2
                        w = att_lat(UNITS[u - 1][1])[1] * P
                        dve.wait_ge(s["exps"], 2 * nu * i + 2 * u)
                        steps(nc.vector.tensor_tensor(sm[:, v, 4:5], sm[:, v, 2:3], sm[:, v, 3:4], ALU.add))
                        steps.wait()
                        steps(nc.vector.reciprocal(sm[:, v, 5:6], sm[:, v, 4:5]))
                        steps.wait()
                        nc.vector.tensor_scalar(p_sb[:, v, 0:CTX + w], p_sb[:, v, 0:CTX + w], sm[:, v, 5:6], None,
                                                ALU.mult).then_inc(s["probs"], 1)
                for c2 in range(2):
                    dve.wait_ge(s["att_out"], nu * i + nu + 8 * (c2 + 1))
                    g_k = g_t[:, bass.ds(2 * i + c2, 1), :]
                    nc.vector.tensor_tensor(g_k, bank(2 + c2)[:, :].unsqueeze(1), g_k, ALU.mult)\
                      .then_inc(s["att_o"], 1)
                steps.end(4)
            for k in range(KC):
                dve.wait_ge(s["op_hi"], OP_DONE["l1"] + k + 1)
                if k == 0:
                    dve.wait_ge(s["att_o"], 8)
                nc.vector.tensor_tensor(op_lo[:, k, 0:S], g_t[:, k, :], op_hi[:, k, 0:S].bitcast(F32), ALU.subtract)\
                  .then_inc(s["op_ready"], 1)
            add_gated("wo_c", 1, False)
            all_evacuated(dve, "wo_c")
            norm_rstd("final")
            for k in range(KC):
                src, c0, n, gain, _ = norm_sources("final", k)[0]
                nc.vector.scalar_tensor_tensor(src, src, gain, rstd_rows("final", c0, n), ALU.mult, ALU.mult)\
                  .then_inc(s["norm_done"], 1)
            dve.wait_ge(s["norm_done"], 8)
            norm_rstd("pre")
            norm_operand("pre")
            nc.vector.memset(zs[:, :, 0:PAD], 0.0)
            steps(nc.vector.memset(xbc[:, :, 0:PAD], 0.0))
            steps(nc.vector.memset(prev[:, :], 0.0))
            all_evacuated(dve, "dt")
            taps = 4
            with dve.Fori(0, XC // 2) as i:
                steps.begin(i, 2 * (taps - 1))
                for j in range(2):
                    xk = xbc[:, bass.ds(2 * i + j, 1), :]

                    def w_col(k):
                        return cols[:, 1, bass.ds(2 * i + (j + XC * k), 1)]

                    dve.wait_ge(s["conv_done"], 2 * i + j + 1)
                    steps(nc.vector.tensor_scalar(conv[:, j:j + 1, :], xk[:, :, PAD:TP], w_col(taps - 1),
                                                  cols[:, 1, bass.ds(2 * i + (j + VEC_B["conv_b"]), 1)],
                                                  ALU.mult, ALU.add))
                    for k in range(1, taps):
                        steps.wait()
                        o = conv[:, j:j + 1, k:T2]
                        ins = nc.vector.scalar_tensor_tensor(o, xk[:, :, PAD:TP - k], w_col(taps - 1 - k), o,
                                                             ALU.mult, ALU.add)
                        if k < taps - 1:
                            steps(ins)
                        else:
                            ins.then_inc(s["conv_in"], 1)
                steps.end(XC // 2)
            dtr = xbc[0:16, XC, PAD:TP]
            dve.wait_ge(s["small_in"], SMALL)
            steps(nc.vector.tensor_scalar(dtm[0:16, 0, :], dtr, dt_bias[0:16, 0:1], None, ALU.add))
            steps.wait()
            steps(nc.vector.tensor_scalar(dtm[0:16, 2, :], dtm[0:16, 0, :], 0.0, -2.0, ALU.max, ALU.mult))
            steps.wait()
            nc.vector.tensor_tensor(dtm[0:16, 1, :], dtm[0:16, 0, :], dtm[0:16, 2, :], ALU.add)\
              .then_inc(s["dt_e"], 1)
            dve.wait_ge(s["dt_l"], 1)
            steps(nc.vector.scalar_tensor_tensor(dtr, dtm[0:16, 0, :], 0.0, dtm[0:16, 1, :], ALU.max, ALU.add))
            steps(nc.vector.tensor_scalar(neg_a[:, :], neg_a[:, :], -1.0, None, ALU.mult))
            steps.wait()
            dve.wait_ge(s["conv_done"], XC + 2)
            dve.sem_inc(s["dt_ready"], 1)
            dve.sem_inc(s["ssd_used"], 1)
            H = 16
            with dve.Fori(0, NT) as t:
                steps.begin(t, 15)
                steps.wait()

                def by_head(ap, n):
                    return ap.unsqueeze(2).to_broadcast([P, H, n])

                dve.wait_ge(s["chunk_turned"], t + 1)
                steps(nc.vector.tensor_copy(dt_k[:, :], pair_ps[1][:, 2 * P:2 * P + H]))
                nc.vector.tensor_copy(b_tok[:, :], pair_ps[1][:, 0:2 * P]).then_inc(s["chunk_b"], 1)
                steps.wait()
                steps(nc.vector.tensor_tensor(adt[:, :], dt_k[:, :], neg_a[:, :], ALU.mult))
                steps(nc.vector.tensor_tensor(xdt[:, :].rearrange("p (h d) -> p h d", h=H),
                                              pair_ps[0][:, :].rearrange("p (h d) -> p h d", h=H),
                                              by_head(dt_k[:, :], HEAD), ALU.mult))
                steps.wait()
                dve.sem_inc(s["chunk_scaled"], 1)
                dve.wait_ge(s["chunk_acs"], t + 1)
                a_ps = pair_ps[1][:, S:S + 2 * H]
                steps(nc.vector.tensor_copy(acs[:, :], a_ps))
                steps.wait()
                dve.wait_ge(s["chunk_e"], t + 1)
                steps(nc.vector.tensor_tensor(seg[:, :, :], bank(0, 4).rearrange("p (h l) -> p h l", h=H),
                                              by_head(acs[:, 0:H], P), ALU.subtract))
                steps.wait()
                nc.vector.tensor_tensor(seg[:, :, :], seg[:, :, :],
                                        at_or_after[:, :].unsqueeze(1).to_broadcast([P, H, P]), ALU.add)\
                  .then_inc(s["seg_ready"], 1)
                steps(nc.vector.tensor_tensor(acs[:, 0:H], acs[:, H:2 * H], acs[:, 0:H], ALU.subtract))
                steps.wait()
                dve.sem_inc(s["dec_in"], 1)
                dve.wait_ge(s["chunk_e"], t + 1)
                for g in range(2):
                    c_g = cexp[:, 8 * g:8 * g + 8, :]
                    steps(nc.vector.tensor_tensor(c_g, c_g, xst[:, 10 + g:11 + g, :].to_broadcast([P, 8, P]),
                                                  ALU.mult))
                dve.wait_ge(s["dec_ready"], t + 1)
                steps(nc.vector.tensor_tensor(xdd[:, :].rearrange("p (h d) -> p h d", h=H),
                                              xdt[:, :].rearrange("p (h d) -> p h d", h=H),
                                              by_head(dec[:, 0:H], HEAD), ALU.mult))
                dve.wait_ge(s["seg_e"], t + 1)
                for g in range(2):
                    l_g = seg[:, 8 * g:8 * g + 8, :]
                    cb = pair_ps[1][:, S + P + g * P:S + 2 * P + g * P].unsqueeze(1).to_broadcast([P, 8, P])
                    steps(nc.vector.tensor_tensor(l_g, l_g, cb, ALU.mult))
                steps.wait()
                dve.sem_inc(s["ssd_operands"], 1)
                steps(nc.vector.tensor_tensor(xst[:, 0:KC, :], xst[:, 0:KC, :],
                                              skip[:, :].unsqueeze(2).to_broadcast([P, KC, P]), ALU.mult))
                steps.wait()
                dve.wait_ge(s["ssd_y"], t + 1)
                steps(nc.vector.tensor_tensor(xst[:, 0:KC, :], xst[:, 0:KC, :],
                                              pair_ps[0][:, :].rearrange("p (k l) -> p k l", k=KC), ALU.add))
                steps.wait()
                z_t = zs[:, :, bass.ds(t * P, P)]
                steps(nc.vector.tensor_tensor(z_t, z_t, xst[:, 0:KC, :], ALU.mult))
                pv = prev[:, :].rearrange("p (h d) -> p h d", h=H)
                steps(nc.vector.tensor_tensor(pv, pv, by_head(dec[:, H:2 * H], HEAD), ALU.mult))
                steps.wait()
                dve.wait_ge(s["ssd_state"], t + 1)
                nc.vector.tensor_tensor(prev[:, :], prev[:, :], pair_ps[1][:, :], ALU.add).then_inc(s["ssd_used"], 1)
                steps.end(NT)
            g0 = SLAB0["sb"]
            nu = len(SBU)
            dve.wait_ge(s["ssd_used"], NT + 1)
            with dve.Fori(0, 4) as i:
                steps.begin(i, 2 * (2 + 3 * nu))
                for m in range(2):
                    dve.wait_ge(s["sb_vt"], 2 * i + m + 1)
                    steps(nc.vector.tensor_copy(v_sb[0:META, m, 0, :], pair_ps[0][0:META, 0:P]))
                    steps(nc.vector.tensor_copy(v_sb[:, m, 1:NT, :].rearrange("p t n -> p (t n)"),
                                                pair_ps[0][:, P:NT * P]))
                    steps.wait()
                    dve.sem_inc(s["sb_v"], 1)
                    for u, (par, blk) in enumerate(SBU):
                        nq, q0, nk = sb_shape(blk)
                        done = 2 * nu * i + nu * m + u + 1
                        z_ps = pair_ps[1][0:nq, S - META:S - META + nk]
                        dve.wait_ge(s["sb_scores"], done)
                        own = z_ps[:, nk - nq:nk]
                        steps(nc.vector.tensor_tensor(own, own, before[0:nq, 0:nq], ALU.add))
                        steps.wait()
                        steps(nc.vector.tensor_scalar(sb_relu[0:nq, 0:nk], z_ps, 0.0, None, ALU.max))
                        steps.wait()
                        nc.vector.scalar_tensor_tensor(sb_abs[0:nq, 0:nk], sb_relu[0:nq, 0:nk], -2.0, z_ps,
                                                       ALU.mult, ALU.add).then_inc(s["sb_in"], 1)
                        dve.wait_ge(s["sb_l"], 2 * done)
                        steps(nc.vector.tensor_tensor_scan(sb_sum[0:nq, nk - 1::-1], sb_relu[0:nq, nk - 1::-1],
                                                           sb_abs[0:nq, nk - 1::-1], 0.0, ALU.add, ALU.add))
                        steps.wait()
                        nc.vector.tensor_tensor(sb_sum[0:nq, 0:nk], z_ps, sb_sum[0:nq, 0:nk], ALU.subtract)\
                          .then_inc(s["sb_d"], 1)
                    dve.wait_ge(s["sb_o"], 2 * nu * i + nu * (m + 1))
                    nc.vector.tensor_copy(ysb[:, bass.ds(2 * i + m, 1), :], bank(2, 2)[:, PAD:TP].unsqueeze(1))\
                      .then_inc(s["sb_y"], 1)
                steps.end(4)
            dve.wait_ge(s["sb_y"], KC + 1)
            for name in ("ssd", "sbn"):
                norm_rstd(name)
                dve.wait_ge(s["slab_done"], SLAB0["wo_2"])
                norm_operand(name)

            def add_normed(name, done):
                _, _, _, _, hp = NORMS[name]
                norm_rstd(name)
                for k in range(KC):
                    src, c0, n, gain, _ = norm_sources(name, k)[0]
                    steps(nc.vector.scalar_tensor_tensor(hp[:, k % 3, 0:n], src, gain, rstd_rows(name, c0, n),
                                                         ALU.mult, ALU.mult))
                    steps.wait()
                    nc.vector.tensor_tensor(xT[:, k, :], xT[:, k, :], hp[:, k % 3, 0:n], ALU.add)\
                      .then_inc(s["norm_done"], 1)

            all_evacuated(dve, "wo_2")
            add_normed("post", 16)
            dve.wait_ge(s["norm_done"], 16)
            norm_rstd("ffn")
            norm_operand("ffn")
            steps(nc.vector.memset(gp[:, 0:2], 0.0))
            steps.wait()
            dve.sem_inc(s["ffn_used"], 1)
            g0, b0 = SLAB0["up"], BLOCK0["up"]
            with dve.Fori(0, FC) as i:
                steps.begin(i, 2)

                def w_col(k):
                    return cols[:, 2, bass.ds(i + FC * k, 1)]

                dve.wait_ge(s_evac[b0 % 2], 2 + b0 // 2 + i)
                steps(nc.vector.tensor_scalar(gacc[:, :], gp[:, 2:2 + T2], w_col(2),
                                              cols[:, 1, bass.ds(i + VEC_B["ffn_b"], 1)], ALU.mult, ALU.add))
                steps.wait()
                steps(nc.vector.scalar_tensor_tensor(gacc[:, :], gp[:, 1:1 + T2], w_col(1), gacc[:, :],
                                                     ALU.mult, ALU.add))
                steps.wait()
                nc.vector.scalar_tensor_tensor(gacc[:, :], gp[:, 0:T2], w_col(0), gacc[:, :], ALU.mult, ALU.add)\
                  .then_inc(s["gate_conv"], 1)
                dve.wait_ge(s["gate_conv"], i + 1)
                dve.sem_inc(s["ffn_used"], 1)
                dve.wait_ge(s["gelu"], i + 1)
                dve.wait_ge(s["slab_done"], g0 + 2 + 2 * i)
                nc.vector.tensor_tensor(two(fgl[:, :]), seg2(gemm_ps[(b0 + 1) % 2]), two(gacc[:, :]), ALU.mult)\
                  .then_inc(s["ffn_f"], 1)
                dve.wait_ge(s["ffn_f"], i + 1)
                dve.sem_inc(s_evac[(b0 + 1) % 2], 1)
                dve.wait_ge(s["ffn_hi"], i + 1)
                nc.vector.tensor_tensor(f_lo[:, bass.ds(i, 1), :], fgl[:, :].unsqueeze(1),
                                        f_hi[:, bass.ds(i, 1), :].bitcast(F32), ALU.subtract)\
                  .then_inc(s["op_ready"], 1)
                steps.end(FC)
            all_evacuated(dve, "down")
            add_normed("fin", 24)
            for t in range(S // P):
                dve.wait_ge(s["out_turned"], t + 1)
                nc.vector.tensor_copy(y_out[:, t, :], gemm_ps[t % 2][:, :]).then_inc(s["out_ready"], 1)

        @block.tensor
        def _(pe):
            mm = nc.tensor.matmul

            def norm_sums(name):
                k0, tiles, base, sq, _ = NORMS[name]
                o = pair_ps[1]
                mm(o[:, 0:len(tiles)], zeros[:, :], zeros[:, 0:len(tiles)], start=True, stop=True)
                for k in range(KC):
                    pe.wait_ge(s["sq"], 8 * k0 + k + 1)
                    for t, (c0, n) in enumerate(tiles):
                        ins = mm(o[0:n, t:t + 1], sq[:, k % 2, c0:c0 + n], ones[:, 0:1], start=False,
                                 stop=True, skip_group_check=True)
                    ins.then_inc(s["sq_used"], 1)
                pe.wait_ge(s["sq_used"], 8 * k0 + 8)
                pe.sem_inc(s["ssq"], 1)
                pe.wait_ge(s["rstd"], k0 + 1)
                for t, (c0, n) in enumerate(tiles):
                    ins = mm(rstd_rows(name, c0, n), rstd[0:n, t:t + 1].to_broadcast([n, P]), ident[0:n, 0:n],
                             start=True, stop=True)
                ins.then_inc(s["rstd_rows"], 1)

            def products(o, hi, lo, w_h, w_l, kn, k0, segs, first, last):
                for k in range(kn):
                    a, z = first and k == 0, last and k == kn - 1
                    for b, (c0, n) in enumerate(segs):
                        mm(o[:, 512 * b:512 * b + n], w_h[:, k, :], hi[:, k0 + k, c0:c0 + n], start=a, stop=False)
                        mm(o[:, 512 * b:512 * b + n], w_h[:, k, :], lo[:, k0 + k, c0:c0 + n], start=False, stop=False)
                    for b, (c0, n) in enumerate(segs):
                        ins = mm(o[:, 512 * b:512 * b + n], w_l[:, k, :], hi[:, k0 + k, c0:c0 + n], start=False,
                                 stop=z)
                ins.then_inc(s["slab_done"], 1)

            def gemm(name, hi, lo, segs, ring=(w_hi, w_lo), kn=KC):
                per, g0, b0 = PER[name], SLAB0[name], BLOCK0[name]
                n = SLABS[name] // per
                u = 2 if n % 2 == 0 else 1

                def body(i):
                    for jb in range(u):
                        b = b0 + jb
                        pe.wait_ge(s_evac[b % 2], 1 + b // 2 + (i if u == 2 else 0))
                        for h in range(per):
                            j = jb * per + h
                            slot = (g0 + j) % 2 if kn == KC else j % 2
                            pe.wait_ge(s["split"], g0 + j + 1 + u * per * i)
                            products(gemm_ps[b % 2], hi, lo, ring[0][:, slot, :, :], ring[1][:, slot, :, :], kn,
                                     h * kn, segs, h == 0, h == per - 1)

                if n == 1:
                    body(0)
                else:
                    with pe.Fori(0, n // u) as i:
                        body(i)

            pe.wait_ge(s["vec_in"], 16 * 16)
            pe.wait_ge(s["consts_in"], 16 * 5)
            for v, r in enumerate(VEC_ROWS):
                nc.tensor.transpose(bank(4 + v)[:, 0:r], vec_in[0:r, v, :], ident[0:r, 0:r]).then_inc(s["vec_turned"], 1)
            pe.wait_ge(s["x_in"], 16 * 3)
            for k in range(KC):
                if k >= 4:
                    pe.wait_ge(s["x_ready"], k - 3)
                for t in range(S // P):
                    ins = nc.tensor.transpose(bank(k % 4)[:, t * P:(t + 1) * P], x_in[:, t, k * P:(k + 1) * P],
                                              ident[:, :])
                ins.then_inc(s["x_turned"], 1)
            for k in range(0, KC, 2):
                pe.wait_ge(s["x_ready"], 5 + k // 2)
                for a in range(2):
                    for t in range(CTX // P):
                        ins = nc.tensor.transpose(bank(k // 2 % 4)[:, a * CTX + t * P:a * CTX + (t + 1) * P],
                                                  ctx_in[:, t, (k + a) * P:(k + a + 1) * P], ident[:, :])
                ins.then_inc(s["x_turned"], 1)
            pe.wait_ge(s["x_ready"], 9)
            for k in range(KC):
                ins = nc.tensor.transpose(bank(0)[:, k * META:(k + 1) * META], meta_in[:, k * P:(k + 1) * P],
                                          ident[0:META, 0:META])
            ins.then_inc(s["x_turned"], 1)
            pe.wait_ge(s["cond_ready"], 2)
            with pe.Fori(0, 6) as i:
                for j in range(8):
                    pe.wait_ge(s_ada_in[j], 16 * i + 16)
                    for k in range(KC):
                        ins = mm(bank(7)[:, bass.ds(16 * i + 2 * j, 2)], ada_ring[:, j, k, :], cond[:, k, :],
                                 start=(k == 0), stop=(k == KC - 1))
                    ins.then_inc(s["ada_used"], 1)
            pe.wait_ge(s["mod_ready"], 1)
            pe.wait_ge(s["fill_ready"], 3)
            norm_sums("l0")
            pe.wait_ge(s["op_ready"], OP_DONE["l0"])
            gemm("uv", op_hi, op_lo, SEG_XC)
            gemm("ga", op_hi, op_lo, SEG_XC)
            gemm("xb", op_hi, op_lo, SEG_XC)
            gemm("gb", op_hi, op_lo, SEG_XC)
            pe.wait_ge(s["small_in"], SMALL)
            for h in range(4):
                ins = nc.tensor.transpose(bank(7)[:, h * P:(h + 1) * P], sw[:, h, :], ident[:, :])
            ins.then_inc(s["sw_turned"], 1)
            all_evacuated(pe, "gb")
            for t in range(SX // P):
                if t >= 2:
                    pe.wait_ge(s["v_ready"], t - 1)
                for h in range(4):
                    ins = nc.tensor.transpose(bank(4 + t % 2)[:, h * P:(h + 1) * P],
                                              zT[:, 4 + h, t * P:(t + 1) * P], ident[:, :])
                ins.then_inc(s["v_turned"], 1)
            pe.wait_ge(s["v_ready"], SX // P)
            pe.wait_ge(s["sw_ready"], 1)
            for h in range(4):
                if h >= 2:
                    pe.wait_ge(s["ya_ready"], h - 1)
                for t in range(SX // P):
                    ins = mm(pair_ps[h % 2][:, t * P:(t + 1) * P], vt[:, t, h * P:(h + 1) * P], swT[:, h, :],
                             start=True, stop=True)
                ins.then_inc(s["spatial"], 1)
            pe.wait_ge(s["ya_ready"], 4)
            for g in range(4):
                if g:
                    pe.wait_ge(s["pq_ready"], g)
                for t in range(SX // P):
                    ins = mm(ps[:, 4 * 512 + t * 2 * P:4 * 512 + (t + 1) * 2 * P], zT[:, 12 + g, t * P:(t + 1) * P],
                             dft_ch[:, :], start=True, stop=True)
                ins.then_inc(s["ch_dft"], 1)
                pe.wait_ge(s["pq_ready"], g + 1)
                if g >= 2:
                    pe.wait_ge(s["yb_ready"], g - 1)
                o = gemm_ps[g % 2]
                nx = S // P
                for t in range(nx):
                    for r in range(2):
                        mm(o[:, 0:S], pq[:, t, r * P:(r + 1) * P], dft_seq[:, t, r, :], start=(t + r == 0),
                           stop=(t == nx - 1 and r == 1))
                for t in range(CTX // P):
                    for r in range(2):
                        ins = mm(o[:, S:SX], pq[:, nx + t, r * P:(r + 1) * P], dft_seq[:, t, r, 0:S:S // CTX],
                                 start=(t + r == 0), stop=(t == CTX // P - 1 and r == 1))
                ins.then_inc(s["seq_dft"], 1)
            pe.wait_ge(s["op_ready"], OP_DONE["y0"])
            gemm("wo_ab", op_hi, op_lo, SEG_XC)
            norm_sums("l1")
            pe.wait_ge(s["op_ready"], OP_DONE["l1"])
            gemm("q", op_hi, op_lo, SEG_X)
            gemm("kv", op_hi, op_lo, SEG_XC)
            gemm("gc", op_hi, op_lo, SEG_X)
            all_evacuated(pe, "kv")
            for t in range(SX // P):
                for k in range(2):
                    a = 4 * 512 + t * CTX + k * P
                    ins = nc.tensor.transpose(ps[:, a:a + P], kv_t[:, 2 + k, t * P:(t + 1) * P], ident[:, :])
            ins.then_inc(s["vtok_turned"], 1)
            pe.wait_ge(s["vtok_ready"], 1)
            all_evacuated(pe, "gc")
            nu = len(UNITS)
            pe.sem_inc(s["att_out"], nu)
            with pe.Fori(0, 4) as i:
                pe.wait_ge(s["att_in"], i + 1)
                for u in range(nu + 2):
                    if u < nu:
                        c2, n, par = UNITS[u]
                        lo, nb = att_lat(n)
                        h = slice(HEAD * par, HEAD * par + HEAD)
                        sc = pair_ps[u % 2]
                        if u >= 2:
                            pe.wait_ge(s["exps"], 2 * nu * i + 2 * (u - 1))
                        q_u = q_st[h, c2, n * P:(n + 1) * P]
                        mm(sc[:, CTX:S], q_u, k_st[h, S:SX], start=True, stop=True)
                        mm(sc[:, S:S + nb * P], q_u, k_st[h, lo * P:(lo + nb) * P], start=True, stop=True)\
                            .then_inc(s["scores"], 1)
                    if 1 <= u <= nu:
                        nb = att_lat(UNITS[u - 1][1])[1] + CTX // P
                        pe.wait_ge(s["probs"], nu * i + u)
                        if u >= 2:
                            pe.wait_ge(s["p_copied"], nu * i + u - 1)
                        for b in range(nb):
                            ins = nc.tensor.transpose(bank(0, 2)[:, b * P:(b + 1) * P],
                                                      p_sb[:, (u - 1) % 2, b * P:(b + 1) * P], ident[:, :])
                        ins.then_inc(s["p_turned"], 1)
                    if u >= 2:
                        c2, n, par = UNITS[u - 2]
                        lo, nb = att_lat(n)
                        pe.wait_ge(s["p_copied"], nu * i + u - 1)
                        o = bank(2 + c2)[HEAD * par:HEAD * par + HEAD, n * P:(n + 1) * P]
                        tiles = [S // P, S // P + 1] + list(range(lo, lo + nb))
                        for b, t in enumerate(tiles):
                            ins = mm(o, v_st[:, t, :], pT[:, u % 2, b * P:(b + 1) * P], start=(b == 0),
                                     stop=(b == len(tiles) - 1))
                        ins.then_inc(s["att_out"], 1)
            pe.wait_ge(s["op_ready"], OP_DONE["y1"])
            gemm("wo_c", op_hi, op_lo, SEG_X)
            norm_sums("final")
            norm_sums("pre")
            pe.wait_ge(s["op_ready"], OP_DONE["pre"])
            gemm("z", xn_hi, xn_lo, SEG_2)
            gemm("xbc", xn_hi, xn_lo, SEG_2)
            gemm("dt", xn_hi, xn_lo, SEG_2)
            all_evacuated(pe, "dt")
            H = 16
            with pe.Fori(0, NT) as t:
                pe.wait_ge(s["chunk_in"], 2 * t + 2)
                for k in range(KC):
                    nc.tensor.transpose(pair_ps[0][:, k * P:(k + 1) * P], xst[:, k, :], ident[:, :])
                for g in range(2):
                    nc.tensor.transpose(pair_ps[1][:, g * P:(g + 1) * P], xst[:, KC + g, :], ident[:, :])
                for g in range(2):
                    mm(pair_ps[1][:, S + P + g * P:S + 2 * P + g * P], xst[:, KC + g, :], xst[:, KC + 2 + g, :],
                       start=True, stop=True)
                nc.tensor.transpose(pair_ps[1][:, 2 * P:2 * P + H], dt_t[0:H, :], ident[0:H, 0:H])\
                    .then_inc(s["chunk_turned"], 1)
                pe.wait_ge(s["chunk_scaled"], t + 1)
                mm(pair_ps[1][:, S:S + H], tri[:, :], adt[:, :], start=True, stop=True)
                mm(pair_ps[1][:, S + H:S + 2 * H], ones[:, :], adt[:, :], start=True, stop=True)
                for h in range(H):
                    ins = mm(bank(0, 4)[:, h * P:(h + 1) * P], adt[:, h:h + 1].to_broadcast([P, P]), tri[:, :],
                             start=True, stop=True)
                ins.then_inc(s["chunk_acs"], 1)
                pe.wait_ge(s["ssd_operands"], t + 1)
                pe.wait_ge(s["chunk_b"], t + 1)
                for h in range(H):
                    o = pair_ps[0][HEAD * (h % 2):HEAD * (h % 2) + HEAD, (h // 2) * P:(h // 2 + 1) * P]
                    mm(o, xdt[:, h * HEAD:(h + 1) * HEAD], seg[:, h, :], start=True, stop=False)
                    ins = mm(o, prev[:, h * HEAD:(h + 1) * HEAD], cexp[:, h, :], start=False, stop=True)
                ins.then_inc(s["ssd_y"], 1)
                for g in range(2):
                    ins = mm(pair_ps[1][:, g * S:(g + 1) * S], b_tok[:, g * P:(g + 1) * P],
                             xdd[:, g * S:(g + 1) * S], start=True, stop=True)
                ins.then_inc(s["ssd_state"], 1)
            g0, b0 = SLAB0["sb"], BLOCK0["sb"]
            nu = len(SBU)
            pe.wait_ge(s["ssd_used"], NT + 1)
            with pe.Fori(0, 4) as i:
                for m in range(2):
                    for j in range(3):
                        b, g = b0 + 3 * m + j, g0 + 3 * m + j
                        pe.wait_ge(s_evac[b % 2], 1 + b // 2 + 3 * i)
                        pe.wait_ge(s["split"], g + 1 + 6 * i)
                        if j < 2:
                            pe.wait_ge(s["sb_y"], 2 * i + m + 1)
                        products(gemm_ps[b % 2], xn_hi, xn_lo, w_hi[:, g % 2, :, :], w_lo[:, g % 2, :, :], KC, 0,
                                 SEG_2, True, True)
                    for j in range(3):
                        b = b0 + 3 * m + j
                        pe.wait_ge(s_evac[b % 2], 2 + b // 2 + 3 * i)
                    for t in range(NT):
                        n, c0 = (META, 0) if t == 0 else (P, META + (t - 1) * P)
                        ins = nc.tensor.transpose(pair_ps[0][0:n, t * P:(t + 1) * P], vs[:, m, c0:c0 + n],
                                                  ident[:, :])
                    ins.then_inc(s["sb_vt"], 1)
                    pe.wait_ge(s["sb_v"], 2 * i + m + 1)
                    pe.sem_inc(s["pe_gate"], 1)
                    for u, (par, blk) in enumerate(SBU):
                        nq, q0, nk = sb_shape(blk)
                        done = 2 * nu * i + nu * m + u + 1
                        h = slice(HEAD * par, HEAD * par + HEAD)
                        q_u = qs[h, m, q0:q0 + nq]
                        z_ps = pair_ps[1]
                        ins = mm(z_ps[0:nq, S - META:S], q_u, ks[h, m, 0:META], start=True, stop=True)
                        if blk:
                            ins = mm(z_ps[:, S:S + blk * P], q_u, ks[h, m, META:nk], start=True, stop=True)
                        ins.then_inc(s["sb_scores"], 1)
                        pe.wait_ge(s["sb_wr"], done)
                        if blk == 0:
                            pe.sem_inc(s["pe_gate"], 1)
                        for t in range(blk + 1):
                            n, c0 = (META, 0) if t == 0 else (P, META + (t - 1) * P)
                            ins = nc.tensor.transpose(bank(0, 2)[0:n, t * P:t * P + nq], sb_w[0:nq, c0:c0 + n],
                                                      ident[0:nq, 0:nq])
                        ins.then_inc(s["sb_wt"], 1)
                        pe.wait_ge(s["sb_wc"], done)
                        o = bank(2, 2)[HEAD * par:HEAD * par + HEAD, PAD + q0:PAD + q0 + nq]
                        for t in range(blk + 1):
                            n = META if t == 0 else P
                            ins = mm(o, v_sb[0:n, m, t, h], sb_wT[0:n, t, 0:nq], start=(t == 0), stop=(t == blk))
                        ins.then_inc(s["sb_o"], 1)
            norm_sums("ssd")
            pe.wait_ge(s["op_ready"], OP_DONE["ssd"])
            norm_sums("sbn")
            pe.wait_ge(s["op_ready"], OP_DONE["sbn"])
            gemm("wo_2", y_hi, y_lo, SEG_2)
            norm_sums("post")
            pe.wait_ge(s["norm_done"], 16)
            norm_sums("ffn")
            pe.wait_ge(s["op_ready"], OP_DONE["ffn"])
            gemm("up", u_hi, u_lo, SEG_2)
            pe.wait_ge(s["op_ready"], OP_DONE["ffn"] + FC)
            gemm("down", f_hi, f_lo, SEG_2, (wd_hi, wd_lo), DK)
            norm_sums("fin")
            pe.wait_ge(s["norm_done"], 24)
            for t in range(S // P):
                if t >= 2:
                    pe.wait_ge(s["out_ready"], t - 1)
                for k in range(KC):
                    ins = nc.tensor.transpose(gemm_ps[t % 2][:, k * P:(k + 1) * P],
                                              xT[:, k, META + t * P:META + (t + 1) * P], ident[:, :])
                ins.then_inc(s["out_turned"], 1)


INPUTS = ["x", "c", "ctx", "c_ctx", "norm_g", "ada_w", "ada_b", "w_in_ab", "v_norm_g", "spatial_w", "spatial_b",
          "w_out_ab", "w_in_c", "sink_logit", "w_out_c", "final_g", "meta_tokens_2", "mix_pre_g_2", "w_in_2",
          "ssd_conv_w_2", "ssd_conv_b_2", "ssd_dt_bias_2", "ssd_a_log_2", "ssd_d_2", "ssd_norm_g_2",
          "sb_norm_g_2", "w_out_2", "mix_post_g_2", "ffn_pre_g_2", "w_up_2", "ffn_conv_w_2", "ffn_conv_b_2",
          "w_down_2", "ffn_post_g_2"]
FLAT = {"c", "c_ctx", "norm_g", "ada_b", "v_norm_g", "spatial_b", "sink_logit", "final_g", "mix_pre_g_2",
        "ssd_conv_w_2", "ssd_conv_b_2", "ssd_dt_bias_2", "ssd_a_log_2", "ssd_d_2", "ssd_norm_g_2", "sb_norm_g_2",
        "mix_post_g_2", "ffn_pre_g_2", "ffn_conv_w_2", "ffn_conv_b_2", "ffn_post_g_2"}


def kernel(**inputs):
    import concourse.bacc as bacc
    from concourse.bass_utils import run_bass_kernel_spmd

    nc = bacc.Bacc("TRN2", target_bir_lowering=False, num_devices=1)
    nc, arrays = build(nc, inputs)
    r = run_bass_kernel_spmd(nc, [arrays], core_ids=[0])
    return r.results[0]["out_dram"].reshape(1, S, D)


def build(nc, inputs):
    arrays, args = {}, []
    for name in INPUTS:
        a = np.ascontiguousarray(inputs[name])
        if name in FLAT:
            a = a.reshape(-1)
        elif name not in ("ada_w", "meta_tokens_2"):
            a = a.reshape(a.shape[1:])
        arrays[f"in_{name}"] = a
        args.append(nc.dram_tensor(f"in_{name}", a.shape, F32, kind="ExternalInput").ap())
    arrays["consts"] = shape_constants()[0]
    args.append(nc.dram_tensor("consts", arrays["consts"].shape, F32, kind="ExternalInput").ap())
    args.append(nc.dram_tensor("out_dram", (S, D), F32, kind="ExternalOutput").ap())
    two_blocks(nc, *args)
    return nc, arrays
```

```python
from contextlib import ExitStack

import numpy as np

import concourse.bass as bass
from concourse import mybir

ALU = mybir.AluOpType
ACT = mybir.ActivationFunctionType
AX = mybir.AxisListType
F32 = mybir.dt.float32
F32R = mybir.dt.float32r

P = 128
D = 1024
KC = D // P
S = 512
CTX = 256
META = 16
SX = S + CTX
T2 = META + S
PAD = P - META
TP = PAD + T2
NT = TP // P
HALF = T2 // 2
GRID_W = 64
EPS = 1e-6
NEG = -1e30
FF = 2816
FC = FF // P
AB_IN = 2560
HEAD = 64
ATT_SCALE = HEAD ** -0.5
ROPE_BASE = 10000.0
XBC = 1536
XC = XBC // P
OFF_XBC, OFF_DT = 1024, 2560
OFF_Q, OFF_K, OFF_V = 2576, 3600, 4624
ADA_FIRST = 4
ADA_RING = 4
ADA_L0, ADA_L1 = 28, 4
ATT_BUFS = 4
SB_BUFS = 3
DOWN = [(0, 8), (8, 8), (16, 6)]

STREAM = [("uv", 8, 1), ("ga", 4, 1), ("xb", 4, 1), ("gb", 4, 1), ("wo_ab", 8, 1),
          ("q", 8, 1), ("kv", 4, 1), ("gc", 8, 1), ("wo_c", 8, 1),
          ("xbc", 12, 1), ("dt", 1, 1), ("z", 8, 1), ("sb", 24, 1),
          ("wo_2", 16, 2), ("up", 44, 1), ("down", 24, 3)]
SLAB0, BLOCK0, SLABS, PER = {}, {}, {}, {}
_g = _b = 0
for _name, _n, _per in STREAM:
    SLAB0[_name], BLOCK0[_name], SLABS[_name], PER[_name] = _g, _b, _n, _per
    _g += _n
    _b += 0 if _name in ("z", "sb") else _n // _per

VEC_A = {"norm_g": 0, "ada_b": 16, "c": 64, "c_ctx": 72, "final_g": 80, "mix_pre": 88,
         "ssd_norm": 96, "sb_norm": 104, "mix_post": 112}
VEC_B = {"conv_w": 0, "conv_b": 48, "ffn_b": 60, "ffn_pre": 82, "ffn_post": 90, "v_norm": 98}
COL = {**VEC_A, **{k: 128 + v for k, v in VEC_B.items()}, "ffn_w": 256}
VEC_ROWS = (120, 102, 66)

OP_DONE = {"l0": 8, "y0": 16, "l1": 24, "y1": 32, "pre": 40, "ssd": 48, "sbn": 56, "ffn": 64}


class Steps:

    def __init__(self, eng, sem):
        self.eng, self.sem, self.n, self.i, self.per = eng, sem, 0, None, 0

    def __call__(self, ins):
        self.n += 1
        ins.then_inc(self.sem, 1)

    def wait(self, but=0):
        n = self.n - but
        self.eng.wait_ge(self.sem, n if self.i is None else n + self.i * self.per)

    def begin(self, i, per):
        self.i, self.per, self.at = i, per, self.n

    def end(self, count):
        assert self.n - self.at == self.per, (self.n - self.at, self.per)
        self.n = self.at + count * self.per
        self.i = None


def shape_constants():
    r = np.arange(P)
    ident = np.eye(P)
    tri = (r[:, None] <= r[None, :]) * 1.0
    at_or_after = np.where(r[None, :] >= r[:, None], 0.0, NEG)
    at_or_before = np.where(r[None, :] <= r[:, None], 0.0, NEG)
    before = np.where(r[None, :] < r[:, None], 0.0, NEG)
    before_meta = np.where(r[None, :META] < r[:, None] % 32, 0.0, NEG)
    t = np.arange(S)
    d = r % HEAD
    nf = HEAD // 4
    inv = np.float32(ROPE_BASE) ** (-np.arange(nf, dtype=np.float32) / np.float32(nf))
    place = np.where((d // 32)[:, None] == 0, (t // GRID_W)[None, :], (t % GRID_W)[None, :]).astype(np.float32)
    ang = (place * inv[d % nf][:, None].astype(np.float32)).astype(np.float64)
    sign = np.where(d % 32 < nf, -1.0, 1.0)[:, None]
    a = 2 * np.pi * np.outer(r, r) / P
    b = 2 * np.pi * (np.outer(t, t) % S) / S
    seq = np.stack([np.cos(b), -np.sin(b)], 1) / np.sqrt(S)
    seq = seq.reshape(S // P, P, 2, S).transpose(1, 0, 2, 3).reshape(P, -1)
    parts = {"ident": ident, "tri": tri, "at_or_after": at_or_after, "at_or_before": at_or_before,
             "before": before, "before_meta": before_meta, "cos": np.cos(ang), "sin": np.sin(ang) * sign,
             "dft_ch": np.concatenate([np.cos(a), np.sin(a)], 1) / np.sqrt(P), "dft_seq": seq}
    first, n = {}, 0
    for name, v in parts.items():
        first[name] = n
        n += v.shape[1]
    return np.ascontiguousarray(np.concatenate(list(parts.values()), 1).astype(np.float32)), first


CONST_FIRST = shape_constants()[1]


def two_blocks(nc, x, c, ctx, c_ctx, norm_g, ada_w, ada_b, w_in_ab, v_norm_g, spatial_w, spatial_b,
               w_out_ab, w_in_c, sink_logit, w_out_c, final_g, meta_tokens_2, mix_pre_g_2, w_in_2,
               ssd_conv_w_2, ssd_conv_b_2, ssd_dt_bias_2, ssd_a_log_2, ssd_d_2, ssd_norm_g_2, sb_norm_g_2,
               w_out_2, mix_post_g_2, ffn_pre_g_2, w_up_2, ffn_conv_w_2, ffn_conv_b_2, w_down_2,
               ffn_post_g_2, consts, out):
    stack = ExitStack()
    with stack:
        cursor = [(nc.sbuf_base + 63) // 64 * 64]

        def at(name, shape, offset, dt=F32):
            return nc.alloc_sbuf_tensor_at(name, shape, dt, offset=offset)

        def size(shape):
            return (int(np.prod(shape[1:])) * 4 + 31) // 32 * 32

        def sb(name, shape, dt=F32):
            t = at(name, shape, cursor[0], dt)
            cursor[0] += size(shape)
            return t

        raw = sb("raw", [P, 2, KC, P])
        w_hi = sb("w_hi", [P, 2, KC, P], F32R)
        w_lo = sb("w_lo", [P, 2, KC, P], F32R)
        xT = sb("xT", [P, KC, T2])
        cols = sb("cols", [P, 3, P])
        mod = sb("mod", [P, 48, 2])
        modg = sb("modg", [P, 2, 2, KC])
        ident = sb("ident", [P, P])
        tri = sb("tri", [P, P])
        at_or_after = sb("at_or_after", [P, P])
        at_or_before = sb("at_or_before", [P, P])
        before = sb("before", [P, P])
        before_meta = sb("before_meta", [P, META])
        ones = sb("ones", [P, P])
        zeros = sb("zeros", [P, P])
        eps = sb("eps", [P, 8])
        stat = sb("stat", [P, 8])
        rstd = sb("rstd", [P, 8])
        cond = sb("cond", [P, KC, 2])
        bn = sb("bn", [P, 8])
        mv = sb("mv", [P, 8])
        sink = sb("sink", [P, 16])
        neg_sink = sb("neg_sink", [P, 16])
        neg_a = sb("neg_a", [P, 16])
        a_log = sb("a_log", [P, 16])
        skip = sb("skip", [P, KC])
        dt_bias = sb("dt_bias", [P, 8])
        sm = sb("sm", [P, ATT_BUFS, 8])
        stage0 = cursor[0]

        def plan(*items, start=None):
            at_ = stage0 if start is None else start
            made = []
            for name, shape, *dt in items:
                made.append(at(name, shape, at_, *dt))
                at_ += size(shape)
            assert at_ <= nc.sbuf_usable_end, (items[-1][0], at_, nc.sbuf_usable_end)
            return made

        ctxT, op_hi, op_lo = plan(("ctxT", [P, KC, CTX]), ("op_hi", [P, KC, SX], F32R),
                                  ("op_lo", [P, KC, SX], F32R))
        layer0 = stage0 + size([P, KC, CTX]) + 2 * size([P, KC, SX])
        zT, dft_ch, dft_seq, sw, swT, s_bias, vt, pq = plan(
            ("zT", [P, 20, SX]), ("dft_ch", [P, 2 * P]), ("dft_seq", [P, S // P, 2, S]),
            ("sw", [P, 4, P]), ("swT", [P, 4, P]), ("s_bias", [P, 4, P]),
            ("vt", [P, SX // P, S]), ("pq", [P, SX // P, 2 * P]), start=layer0)
        x_in, ctx_in, meta_in, vec_in = plan(
            ("x_in", [P, S // P, D]), ("ctx_in", [P, CTX // P, D]), ("meta_in", [META, D]),
            ("vec_in", [P, 3, P]), start=layer0)
        ada_first, m_rows, sq0, hp0 = plan(
            ("ada_first", [P, ADA_FIRST - 1, KC, 4 * P]), ("m_rows", [2, ADA_FIRST * 4 * P]), ("sq0", [P, 3, SX]),
            ("hp0", [P, 3, SX]),
            start=layer0 + sum(size(s) for s in ([P, S // P, D], [P, CTX // P, D], [META, D], [P, 3, P])))
        ada_ring, = plan(("ada_ring", [P, ADA_RING, KC, P]), start=layer0 + size([P, 20, SX]))
        ada_acc, = plan(("ada_acc", [P, ADA_L0, 2, P]), start=(nc.sbuf_usable_end - size([P, ADA_L0, 2, P])) // 32 * 32)
        tail0 = layer0 + sum(size(s) for s in ([P, 20, SX], [P, 2 * P], [P, S // P, 2, S], [P, 4, P],
                                               [P, 4, P], [P, 4, P]))
        gmlp, = plan(("gmlp", [P, SX]), start=tail0 + size([P, SX // P, S]) + size([P, SX // P, 2 * P]))
        q_t, kv_t, g_t, k_dup, v_tok, cos, sin, q_st, rot, k_st, v_st, p_sb, pT = plan(
            ("q_t", [P, KC, S]), ("kv_t", [P, 4, SX]), ("g_t", [P, KC, S]), ("k_dup", [P, 4, SX]),
            ("v_tok", [P, SX // P, CTX]), ("cos", [P, S]), ("sin", [P, S]), ("q_st", [P, 2, S]),
            ("rot", [P, 2, S]), ("k_st", [P, SX]), ("v_st", [P, SX // P, HEAD]),
            ("p_sb", [P, ATT_BUFS, 640]), ("pT", [P, 2, 640]), start=layer0)
        ada_ring1, ada_acc1 = plan(
            ("ada_ring1", [P, ADA_RING, KC, P]), ("ada_acc1", [P, ADA_L1, 2, P]),
            start=layer0 + sum(size(s) for s in (
                [P, KC, S], [P, 4, SX], [P, KC, S], [P, 4, SX], [P, SX // P, CTX], [P, S], [P, S], [P, 2, S],
                [P, 2, S], [P, SX], [P, SX // P, HEAD])))
        sq1, hp1 = plan(("sq1", [P, 3, SX]), ("hp1", [P, 3, SX]),
                        start=layer0 + 2 * size([P, KC, S]) + size([P, 4, SX]))
        xn_hi, xn_lo, zs, xbc = plan(("xn_hi", [P, KC, T2], F32R), ("xn_lo", [P, KC, T2], F32R),
                                     ("zs", [P, KC, TP]), ("xbc", [P, XC + 1, TP]))
        ys_hi, ys_lo = plan(("ys_hi", [P, KC, T2], F32R), ("ys_lo", [P, KC, T2], F32R),
                            start=stage0 + 2 * size([P, KC, T2]) + size([P, KC, TP]))
        mixer = stage0 + 4 * size([P, KC, T2]) + size([P, KC, TP])
        assert size([P, XC + 1, TP]) <= 2 * size([P, KC, T2])
        (xst, b_tok, xdt, xdd, seg, cexp, prev, conv, dt_t, dt_k, adt, acs, dec, cb, dtm, ysb, hp_ssd, rstd_ssd) = plan(
            ("xst", [P, XC, P]), ("b_tok", [P, 2 * P]), ("xdt", [P, D]), ("xdd", [P, D]),
            ("seg", [P, 16, P]), ("cexp", [P, 16, P]), ("prev", [P, D]), ("conv", [P, 2, T2]),
            ("dt_t", [P, P]), ("dt_k", [P, 16]), ("adt", [P, 16]), ("acs", [P, 32]), ("dec", [P, 32]), ("cb", [P, 2, P]),
            ("dtm", [P, 3, T2]), ("ysb", [P, KC, T2]), ("hp_ssd", [P, 2, T2]),
            ("rstd_ssd", [P, T2]), start=mixer)
        qs, ks, vs, v_sb, sb_relu, sb_neg, sb_sum, sb_wT = plan(
            ("qs", [P, 2, T2]), ("ks", [P, 2, T2]), ("vs", [P, 2, T2]), ("v_sb", [P, 2, NT, P]),
            ("sb_relu", [P, SB_BUFS, T2]), ("sb_neg", [P, SB_BUFS, T2]), ("sb_sum", [P, SB_BUFS, T2]),
            ("sb_wT", [P, SB_BUFS, NT, P]), start=mixer)
        mixT, sq2, hp2 = plan(("mixT", [P, KC, T2]), ("sq2", [P, 3, T2]), ("hp2", [P, 3, T2]), start=mixer)
        u_hi, u_lo, f_hi, f_lo, gp, gacc, fgl, fT = plan(
            ("u_hi", [P, KC, T2], F32R), ("u_lo", [P, KC, T2], F32R), ("f_hi", [P, FC, T2], F32R),
            ("f_lo", [P, FC, T2], F32R), ("gp", [P, T2 + 8]), ("gacc", [P, T2]), ("fgl", [P, T2]),
            ("fT", [P, KC, T2]))
        ffn_tail = stage0 + 2 * size([P, FC, T2]) + 2 * size([P, KC, T2]) + size([P, T2 + 8]) + 2 * size([P, T2])
        sq3, hp3 = plan(("sq3", [P, 3, T2]), ("hp3", [P, 3, T2]), start=ffn_tail)
        rstd_ffn, = plan(("rstd_ffn", [P, T2]), start=ffn_tail + size([P, KC, T2]))
        sq4, hp4 = plan(("sq4", [P, 3, T2]), ("hp4", [P, 3, T2]), start=stage0 + size([P, S // P, D]))
        y_out, = plan(("y_out", [P, S // P, D]), start=stage0)

        ps = stack.enter_context(nc.psum_tensor("ps", [P, 8 * 512], F32))

        def bank(b, n=1):
            return ps[:, 512 * b:512 * (b + n)]

        gemm_ps = [bank(0, 2), bank(2, 2)]
        pair_ps = [bank(4, 2), bank(6, 2)]

        def sem(name):
            return stack.enter_context(nc.semaphore(name))

        names = """vec_in x_in consts_in small_in dft_in vec_turned cols_ready cond_ready x_turned x_ready
            vec2_in ada_rows rows_taken rows_turned ada1_in ada_acc ada_sums mod_ready mod1_ready gate1_ready fill_ready raw0 raw1 split slab_done evac0 evac1 slab_taken
            sq sq_used ssq std rstd rstd_rows hp op_hi op_ready norm_done
            v_turned v_stat v_std v_ready sw_turned sw_ready spatial ya_ready ch_dft pq_ready seq_dft yb_ready
            rope_ready vtok_turned vtok_ready att_in scores nmax exps probs p_turned p_copied att_out att_o
            conv_in conv_done dt_e dt_l dt_ready chunk_in chunk_turned chunk_scaled chunk_b chunk_acs dec_in dec_ready
            chunk_e seg_ready seg_e ssd_operands ssd_y ssd_state ssd_used
            z_evac seg_sub z_silu gated rows_kept sb_evac sb_vt sb_v sb_scores sb_in sb_l sb_d sb_wr sb_wt sb_wc sb_o sb_y
            normed gate_conv gelu ffn_f ffn_hi out_turned out_ready stored
            pe_gate act_gate act_steps dve_steps pool_steps""".split()
        s = {n: sem("s_" + n) for n in names}
        s_ada_first = [sem(f"s_ada_first{j}") for j in range(ADA_FIRST)]
        s_ada_in = [sem(f"s_ada_in{j}") for j in range(ADA_RING)]
        s_raw = [s["raw0"], s["raw1"]]
        s_evac = [s["evac0"], s["evac1"]]

        SMALL = 16 * 5

        def col(name, k, n=1):
            i = COL[name] + k
            return cols[:, i // P, i % P:i % P + n]

        def ada_rows_at(j):
            return bank(7 if j % 2 == 0 else 3)[0:2, :]

        def block_done(name, n):
            return SLAB0[name] + n * PER[name]

        def all_evacuated(eng, name):
            last = BLOCK0[name] + SLABS[name] // PER[name]
            eng.wait_ge(s_evac[0], 1 + (last + 1) // 2)
            eng.wait_ge(s_evac[1], 1 + last // 2)

        def seg2(ap):
            return ap.rearrange("p (h n) -> p h n", h=2)[:, :, 0:HALF]

        def two(ap):
            return ap.rearrange("p (h n) -> p h n", h=2)

        SEG_X = [(0, S)]
        SEG_XC = [(0, S), (S, CTX)]
        SEG_2 = [(0, HALF), (HALF, HALF)]
        TILES_XC = [(t * P, P) for t in range(SX // P)]
        TILES_X = TILES_XC[:S // P]
        TILES_2 = [(0, META)] + [(META + t * P, P) for t in range(S // P)]

        def lat(k):
            return xT[:, k, META:T2]

        NORMS = {
            "l0": (0, TILES_XC, 0, sq0, hp0), "l1": (1, TILES_XC, 0, sq1, hp1),
            "final": (2, TILES_X, 0, sq1, hp1), "pre": (3, TILES_2, PAD, sq2, hp2),
            "ssd": (4, TILES_2, PAD, sq2, hp2), "sbn": (5, TILES_2, PAD, sq2, hp2),
            "post": (6, TILES_2, PAD, sq2, hp2), "ffn": (7, TILES_2, PAD, sq3, hp3),
            "fin": (8, TILES_2, PAD, sq4, hp4)}
        HP0 = {"l0": 0, "l1": 8, "pre": 16, "ssd": 24, "sbn": 32, "ffn": 40}

        def norm_sources(name, k):
            if name in ("l0", "l1"):
                layer = int(name[1])
                return [(lat(k), 0, S, modg[:, layer, 0, k:k + 1], mod[:, 24 * layer + k, 0:1]),
                        (ctxT[:, k, :], S, CTX, modg[:, layer, 1, k:k + 1], mod[:, 24 * layer + k, 1:2])]
            if name == "final":
                return [(lat(k), 0, S, col("final_g", k), None)]
            src, gain = {"pre": (xT[:, k, :], "mix_pre"), "ssd": (zs[:, k, PAD:TP], "ssd_norm"),
                         "sbn": (ysb[:, k, :], "sb_norm"), "post": (mixT[:, k, :], "mix_post"),
                         "ffn": (xT[:, k, :], "ffn_pre"), "fin": (fT[:, k, :], "ffn_post")}[name]
            return [(src, 0, T2, col(gain, k), None)]

        OPERAND = {"l0": (op_hi, op_lo, 0), "l1": (op_hi, op_lo, 0), "pre": (xn_hi, xn_lo, 0),
                   "ssd": (ys_hi, ys_lo, 0), "sbn": (xn_hi, xn_lo, 0), "ffn": (u_hi, u_lo, 0)}

        def rstd_rows(name, c0, n):
            base = NORMS[name][2]
            return pair_ps[0][:, base + c0:base + c0 + n]

        def y0_chunk(k):
            return zT[:, k if k < 4 else 8 + k, :]

        def att_lat(n):
            lo, hi = max(n - 1, 0), min(n + 1, S // P - 1)
            return lo, hi - lo + 1

        UNITS = [(c2, n, par) for c2 in range(2) for n in range(S // P) for par in range(2)]
        SBU = [(0, 0)] + [(par, blk) for blk in range(1, NT) for par in range(2)]
        SBN = 2 * len(SBU)
        SB_PAIRS = 8
        SB_SKEW = 3

        def sb_unit(u):
            m, v = divmod(u, len(SBU))
            par, blk = SBU[v]
            if blk == 0:
                return m, par, blk, 2 * 32, 0, META, u % SB_BUFS
            return m, par, blk, P, META + (blk - 1) * P, META + blk * P, u % SB_BUFS

        def sb_out(u):
            m, v = divmod(u, len(SBU))
            return NT * m + (v + 1) // 2

        def sb_outputs(u):
            return u % len(SBU) % 2 == 0

        SB_CHUNKS = {1: 3, 2: 3, 3: 2, 4: 3, 5: 3, 6: 2, 7: 4, 8: 4,
                     10: 2, 11: 2, 12: 2, 13: 2, 14: 2, 15: 2, 16: 2, 17: 2, 18: 4, 19: 4}
        SB_TAKE = {0: (0, 2, -1), 4: (1, 0, 0), 7: (1, 1, 1), 9: (1, 2, 2), 14: (0, 0, 3), 18: (0, 1, 4)}

        SB_NORM = [6, 15]

        SB_BANKS, SB_HELD = [], []
        _turn, _holder = 0, {}
        for _u in range(SBN):
            _n = 1 if sb_unit(_u)[5] <= 512 else 2
            if _n == 2 and _turn % 6 == 5:
                _turn += 1
            SB_BANKS.append((2 + _turn % 6, _n))
            _held = [2 + (_turn + _j) % 6 for _j in range(_n)]
            SB_HELD.append(sorted({_holder[_j] for _j in _held if _j in _holder}))
            _holder.update({_j: _u for _j in _held})
            _turn += _n

        def sb_bank(u):
            return bank(*SB_BANKS[u])

        def sb_key0(u):
            return S - META if SB_BANKS[u][1] == 2 else 0

        def sb_tile(u, t):
            return t * P if t == 0 or SB_BANKS[u][1] == 1 else S + (t - 1) * P

        block = stack.enter_context(nc.Block())

        @block.sync
        def _(sp):
            for tile, rows in ((0, [(norm_g, "norm_g"), (ada_b, "ada_b"), (c, "c"), (c_ctx, "c_ctx"),
                                    (final_g, "final_g"), (mix_pre_g_2, "mix_pre"), (ssd_norm_g_2, "ssd_norm"),
                                    (sb_norm_g_2, "sb_norm"), (mix_post_g_2, "mix_post")]),
                               (1, [(ssd_conv_w_2, "conv_w"), (ssd_conv_b_2, "conv_b"), (ffn_conv_b_2, "ffn_b"),
                                    (ffn_pre_g_2, "ffn_pre"), (ffn_post_g_2, "ffn_post"), (v_norm_g, "v_norm")]),
                               (2, [(ffn_conv_w_2, "ffn_w")])):
                if tile == 1:
                    sp.dma_start(ident[:, :], consts[:, 0:P]).then_inc(s["consts_in"], 16)
                    ada0 = ada_w[0].rearrange("(k p) n -> p k n", p=P)

                    def ada_slab(j):
                        sp.dma_start(ada_first[:, j % 3, :, :], ada0[:, :, j * 4 * P:(j + 1) * 4 * P])\
                          .then_inc(s_ada_first[j], 16)

                    ada_slab(0)
                    sp.dma_start(x_in[:, :, :], x.rearrange("(t p) d -> p t d", p=P)).then_inc(s["x_in"], 16)
                    sp.dma_start(ctx_in[:, :, :], ctx.rearrange("(t p) d -> p t d", p=P)).then_inc(s["x_in"], 16)
                    sp.dma_start(meta_in[:, :], meta_tokens_2).then_inc(s["x_in"], 16)
                    ada_slab(1)
                    ada_slab(2)
                    sp.wait_ge(s["ada_rows"], 1)
                    ada_slab(3)
                for src, name in rows:
                    n = src.shape[0] // P
                    r = COL[name] - P * tile
                    flat = src.rearrange("(k p) -> k p", p=P)
                    sp.dma_start(vec_in[r:r + n, tile, :], flat).then_inc(s["vec2_in" if tile else "vec_in"], 16)
            for name, dst in (("tri", tri), ("at_or_after", at_or_after),
                              ("at_or_before", at_or_before), ("before", before), ("before_meta", before_meta)):
                f = CONST_FIRST[name]
                sp.dma_start(dst[:, :], consts[:, f:f + dst.shape[1]]).then_inc(s["consts_in"], 16)
            sp.dma_start(sink[:, :], sink_logit.partition_broadcast(P)).then_inc(s["small_in"], 16)
            sp.dma_start(a_log[:, :], ssd_a_log_2.partition_broadcast(P)).then_inc(s["small_in"], 16)
            sp.dma_start(dt_bias[0:16, 0:1], ssd_dt_bias_2.rearrange("(h o) -> h o", o=1),
                         allow_slow_non_contiguous=True).then_inc(s["small_in"], 16)
            d_by_half = ssd_d_2.rearrange("(k h) -> h k", h=2)
            for h in range(2):
                sp.dma_start(skip[HEAD * h:HEAD * h + HEAD, :], d_by_half[h].partition_broadcast(HEAD),
                             allow_slow_non_contiguous=True).then_inc(s["consts_in"], 16)

            def cols_of(w):
                return w.rearrange("(k p) n -> p k n", p=P)

            def stream(name, src, begin=0, end=None, beside=None):
                u = 2 if SLABS[name] % 2 == 0 else 1
                g0 = SLAB0[name]

                def load(i, j):
                    if not (isinstance(i, int) and g0 + j + u * i < 2):
                        sp.wait_ge(s["split"], g0 + j - 1 + u * i)
                    sp.dma_start(raw[:, (g0 + j) % 2, :, :], src(i, j)).then_inc(s_raw[(g0 + j) % 2], 16)

                def step(i):
                    for j in range(u):
                        load(i, j)
                    if beside:
                        beside(i)

                end = SLABS[name] // u if end is None else end
                if end - begin == 1:
                    step(begin)
                    return
                with sp.Fori(begin, end) as i:
                    step(i)

            def plain(w, c0):
                return lambda i, j: cols_of(w)[:, :, bass.ds(i * 2 * P + (j * P + c0), P)]

            def ada_beside(layer, c0, it0, ring, dma_sems):
                w = ada_w[layer].rearrange("(k p) n -> p k n", p=P)

                def load(i):
                    for j in range(ADA_RING):
                        sp.wait_ge(s["ada_acc"], ADA_RING * it0 + j + 1 + ADA_RING * i)
                        sp.dma_start(ring[:, j, :, :], w[:, :, bass.ds(i * ADA_RING * P + (c0 + j * P), P)])\
                          .then_inc(dma_sems[j], 16)

                return load

            stream("uv", plain(w_in_ab, 0), 0, 1)
            sp.wait_ge(s["mod_ready"], 1)
            stream("uv", plain(w_in_ab, 0), 1, 3, ada_beside(0, 2 * D - ADA_RING * P, -1, ada_ring, s_ada_in))
            stream("uv", plain(w_in_ab, 0), 3, 4, ada_beside(1, -3 * ADA_RING * P, -1, ada_ring, s_ada_in))
            stream("ga", plain(w_in_ab, 1024), beside=ada_beside(1, ADA_RING * P, 3, ada_ring, s_ada_in))
            stream("xb", plain(w_in_ab, 1536), beside=ada_beside(1, 3 * ADA_RING * P, 5, ada_ring, s_ada_in))
            stream("gb", plain(w_in_ab, 2048))
            sp.wait_ge(s["ada_acc"], ADA_RING + ADA_L0)
            f = CONST_FIRST["dft_ch"]
            sp.dma_start(dft_ch[:, :], consts[:, f:f + 2 * P]).then_inc(s["dft_in"], 16)
            f = CONST_FIRST["dft_seq"]
            sp.dma_start(dft_seq[:, :, :, :].rearrange("p a b n -> p (a b n)"),
                         consts[:, f:f + 2 * S * S // P]).then_inc(s["dft_in"], 16)
            sp.wait_ge(s["ada_sums"], 1)
            sp.dma_start(sw[:, :, :], spatial_w.rearrange("h q p -> q h p")).then_inc(s["small_in"], 16)
            sp.dma_start(s_bias[:, :, :], spatial_b.partition_broadcast(P)).then_inc(s["small_in"], 16)
            stream("wo_ab", plain(w_out_ab, 0))
            def second_layer(i):
                sp.wait_ge(s["op_ready"], OP_DONE["l1"])
                w = ada_w[1].rearrange("(k p) n -> p k n", p=P)
                sp.dma_start(ada_ring1[:, bass.ds(i, 1), :, :].rearrange("p a k n -> p (a k) n"),
                             w[:, :, bass.ds(i * P + (ADA_L0 - KC) * P, P)]).then_inc(s["ada1_in"], 16)

            stream("q", plain(w_in_c, 0), beside=second_layer)
            for name, dst in (("cos", cos), ("sin", sin)):
                f = CONST_FIRST[name]
                sp.dma_start(dst[:, :], consts[:, f:f + S]).then_inc(s["consts_in"], 16)
            stream("kv", plain(w_in_c, 1024))
            stream("gc", plain(w_in_c, 1536))
            stream("wo_c", plain(w_out_c, 0))
            stream("xbc", plain(w_in_2, OFF_XBC))
            stream("dt", lambda i, j: cols_of(w_in_2)[:, :, OFF_DT:OFF_DT + P])
            stream("z", plain(w_in_2, 0))
            g0 = SLAB0["sb"]
            with sp.Fori(0, 4) as i:
                for j in range(6):
                    sp.wait_ge(s["split"], g0 + j - 1 + 6 * i)
                    c0 = (OFF_Q, OFF_K, OFF_V)[j % 3] + (j // 3) * P
                    sp.dma_start(raw[:, (g0 + j) % 2, :, :], cols_of(w_in_2)[:, :, bass.ds(i * 2 * P + c0, P)])\
                      .then_inc(s_raw[(g0 + j) % 2], 16)
            wo2 = w_out_2.rearrange("(h k p) n -> p h k n", h=2, p=P)
            g0 = SLAB0["wo_2"]
            with sp.Fori(0, KC // 2) as i:
                for j in range(4):
                    sp.wait_ge(s["split"], g0 + j - 1 + 4 * i)
                    sp.dma_start(raw[:, (g0 + j) % 2, :, :], wo2[:, j // 2, :, bass.ds(i * 2 * P + j % 2 * P, P)])\
                      .then_inc(s_raw[(g0 + j) % 2], 16)
            g0 = SLAB0["up"]
            with sp.Fori(0, FC) as i:
                for h in range(2):
                    sp.wait_ge(s["split"], g0 + h - 1 + 2 * i)
                    sp.dma_start(raw[:, (g0 + h) % 2, :, :], cols_of(w_up_2)[:, :, bass.ds(i * P + h * FF, P)])\
                      .then_inc(s_raw[(g0 + h) % 2], 16)
            wd = w_down_2.rearrange("(k p) n -> p k n", p=P)
            g0 = SLAB0["down"]
            with sp.Fori(0, KC // 2) as i:
                for j in range(2 * len(DOWN)):
                    k0, n = DOWN[j % len(DOWN)]
                    sp.wait_ge(s["split"], g0 + j - 1 + 2 * len(DOWN) * i)
                    sp.dma_start(raw[:, (g0 + j) % 2, 0:n, :],
                                 wd[:, k0:k0 + n, bass.ds(i * 2 * P + j // len(DOWN) * P, P)])\
                      .then_inc(s_raw[(g0 + j) % 2], 16)
            for t in range(S // P):
                sp.wait_ge(s["out_ready"], t + 1)
                sp.dma_start(out[t * P:(t + 1) * P, :], y_out[:, t, :]).then_inc(s["stored"], 16)
            sp.wait_ge(s["stored"], 16 * (S // P))

        @block.gpsimd
        def _(pool):
            steps = Steps(pool, s["pool_steps"])
            nc.gpsimd.memset(ones[:, :], 1.0).then_inc(s["fill_ready"], 1)
            nc.gpsimd.memset(zeros[:, :], 0.0).then_inc(s["fill_ready"], 1)
            nc.gpsimd.memset(eps[:, :], EPS).then_inc(s["fill_ready"], 1)

            def split(r, hi, lo):
                pool.sem_inc(s["slab_taken"], 1)
                steps(nc.gpsimd.tensor_scalar(hi, r, 1.0, 0.0, ALU.mult, ALU.add))
                steps.wait()
                nc.gpsimd.tensor_tensor(lo, r, hi.bitcast(F32), ALU.subtract).then_inc(s["split"], 1)

            def slab(i, j, before_it):
                pool.wait_ge(s_raw[j], 16 * i + 16)
                if before_it:
                    pool.wait_ge(s["slab_done"], 2 * i + j - 1)
                split(raw[:, j, :, :], w_hi[:, j, :, :], w_lo[:, j, :, :])

            for j in range(2):
                slab(0, j, False)
            last = SLAB0["down"] + SLABS["down"]
            n = last // 2
            with pool.Fori(1, n) as i:
                steps.begin(i - 1, 2)
                for j in range(2):
                    slab(i, j, True)
                steps.end(n - 1)
            if last % 2:
                slab(n, 0, True)

        @block.scalar
        def _(act):
            steps = Steps(act, s["act_steps"])

            def norm_std(name):
                k0, tiles, _, _, _ = NORMS[name]
                act.wait_ge(s["ssq"], k0 + 1)
                nc.scalar.activation(stat[:, 0:len(tiles)], pair_ps[1][:, 0:len(tiles)], ACT.Sqrt,
                                     bias=eps[:, 0:1], scale=1.0 / D).then_inc(s["std"], 1)

            def norm_squares(name, chunk_ready=None):
                k0, tiles, base, sq, hp = NORMS[name]
                depth = 2
                for k in range(KC):
                    if chunk_ready:
                        act.wait_ge(chunk_ready, k + 1)
                    if k >= depth or k0:
                        act.wait_ge(s["sq_used"], 8 * k0 + max(k - depth + 1, 0))
                    for src, c0, n, _, _ in norm_sources(name, k):
                        ins = nc.scalar.activation(sq[:, k % depth, c0:c0 + n], src, ACT.Square)
                    ins.then_inc(s["sq"], 1)
                norm_std(name)

            def block_squares(name, i, parts, gemm_name=None):
                k0, _, _, sq, _ = NORMS[name]
                for j in range(2):
                    if gemm_name:
                        b = BLOCK0[gemm_name] + j
                        act.wait_ge(s_evac[b % 2], 2 + b // 2 + i)
                    act.wait_ge(s["sq_used"], 8 * k0 + j - 1 + 2 * i)
                    act.sem_inc(s["act_gate"], 1)
                    for src, c0, n in parts(bass.ds(2 * i + j, 1)):
                        ins = nc.scalar.activation(sq[:, j:j + 1, c0:c0 + n], src, ACT.Square)
                    ins.then_inc(s["sq"], 1)

            def stream_squares(name, gemm_name, parts):
                with act.Fori(0, KC // 2) as i:
                    block_squares(name, i, parts, gemm_name)
                norm_std(name)

            def norm_hi(name):
                _, _, _, _, hp = NORMS[name]
                hi, _, c = OPERAND[name]
                for k in range(KC):
                    act.wait_ge(s["hp"], HP0[name] + k + 1)
                    for _, c0, n, _, shift in norm_sources(name, k):
                        if shift is None:
                            ins = nc.scalar.copy(hi[:, c + k, c0:c0 + n], hp[:, k % 3, c0:c0 + n])
                        else:
                            ins = nc.scalar.activation(hi[:, c + k, c0:c0 + n], hp[:, k % 3, c0:c0 + n],
                                                       ACT.Identity, bias=shift)
                    ins.then_inc(s["op_hi"], 1)

            def evacuate(name, dst, src, func, squares=None, late=0):
                n, b0 = SLABS[name] // PER[name], BLOCK0[name]
                u = 2 if n % 2 == 0 else 1
                if n == 1:
                    act.wait_ge(s["slab_done"], block_done(name, 1))
                    nc.scalar.activation(dst(0), src(gemm_ps[b0 % 2]), func).then_inc(s_evac[b0 % 2], 1)
                    return
                with act.Fori(0, n // u) as i:
                    for j in range(u):
                        act.wait_ge(s["slab_done"], block_done(name, j + 1) + (late if j == 0 else 0) + u * PER[name] * i)
                        nc.scalar.activation(dst(i * u + j), src(gemm_ps[(b0 + j) % 2]), func)\
                          .then_inc(s_evac[(b0 + j) % 2], 1)
                    if squares:
                        norm, buf = squares
                        for j in range(2):
                            act.wait_ge(s_evac[(b0 + j) % 2], 2 + (b0 + j) // 2 + i)
                        block_squares(norm, i, lambda k: [(buf[:, k, :], 0, T2)])
                if squares:
                    norm_std(squares[0])

            act.sem_inc(s_evac[0], 1)
            act.sem_inc(s_evac[1], 1)
            act.sem_inc(s["ada_acc"], ADA_RING)
            act.sem_inc(s["conv_done"], 2)
            act.sem_inc(s["z_evac"], 1)
            act.sem_inc(s["sb_y"], 1)
            act.wait_ge(s["cols_ready"], 1)
            for k, name in enumerate(("c", "c_ctx")):
                nc.scalar.activation(cond[:, :, k], col(name, 0, KC), ACT.Silu).then_inc(s["cond_ready"], 1)
            def take_rows(j):
                act.wait_ge(s["ada_rows"], j + 1)
                nc.scalar.copy(m_rows[:, j * 4 * P:(j + 1) * 4 * P], ada_rows_at(j)).then_inc(s["rows_taken"], 1)

            take_rows(0)
            act.wait_ge(s["x_ready"], 13)
            act.wait_ge(s["fill_ready"], 3)
            norm_squares("l0")
            for j in range(1, ADA_FIRST):
                take_rows(j)
            act.wait_ge(s["mod_ready"], 1)
            norm_hi("l0")

            def wide(ps_):
                return ps_[:, 0:SX].unsqueeze(1)

            def zdst(b0):
                return lambda b: zT[:, bass.ds(b + b0, 1), :]

            evacuate("uv", zdst(0), wide, ACT.Copy)
            evacuate("ga", zdst(8), wide, ACT.Silu)
            evacuate("xb", zdst(12), wide, ACT.Copy)
            evacuate("gb", zdst(16), wide, ACT.Silu)
            def v_std(t):
                act.wait_ge(s["v_stat"], t + 1)
                nc.scalar.activation(mv[:, 2:3], mv[:, 1:2], ACT.Sqrt, bias=eps[:, 0:1]).then_inc(s["v_std"], 1)

            for g in range(4):
                act.wait_ge(s["ch_dft"], g + 1)
                if g:
                    act.wait_ge(s["seq_dft"], g)
                nc.scalar.copy(pq[:, :, :], ps[:, 4 * 512:7 * 512].rearrange("p (t n) -> p t n", t=SX // P))\
                  .then_inc(s["pq_ready"], 1)
                if g < 3:
                    v_std(2 * g)
                    v_std(2 * g + 1)
            for k in range(KC):
                if k == 0:
                    act.wait_ge(s["slab_done"], SLAB0["wo_ab"])
                if k < 4:
                    act.wait_ge(s["ya_ready"], k + 1)
                else:
                    act.wait_ge(s["yb_ready"], k - 3)
                nc.scalar.copy(op_hi[:, k, :], y0_chunk(k)).then_inc(s["op_hi"], 1)
            stream_squares("l1", "wo_ab", lambda k: [(xT[:, k, META:T2], 0, S), (ctxT[:, k, :], S, CTX)])
            norm_hi("l1")

            def narrow(ps_):
                return ps_[:, 0:S].unsqueeze(1)

            evacuate("q", lambda b: q_t[:, bass.ds(b, 1), :], narrow, ACT.Copy)
            evacuate("kv", lambda b: kv_t[:, bass.ds(b, 1), :], wide, ACT.Copy)
            evacuate("gc", lambda b: g_t[:, bass.ds(b, 1), :], narrow, ACT.Silu)
            nu = len(UNITS)
            with act.Fori(0, 4) as i:
                steps.begin(i, 0)
                for u in range(nu + 2):
                    if u < nu:
                        c2, n, par = UNITS[u]
                        v, w = u % ATT_BUFS, att_lat(n)[1] * P
                        act.wait_ge(s["nmax"], nu * i + u + 1)
                        head = 2 * c2 + par
                        if u >= ATT_BUFS:
                            act.wait_ge(s["p_turned"], nu * i + u - ATT_BUFS + 1)
                        nc.scalar.activation(p_sb[:, v, 0:CTX + w], pair_ps[u % 2][:, CTX:S + w], ACT.Exp,
                                             bias=sm[:, v, 1:2], scale=ATT_SCALE,
                                             accum_out=sm[:, v, 3:4]).then_inc(s["exps"], 1)
                        nc.scalar.activation(sm[:, v, 2:3], neg_sink[:, bass.ds(4 * i + head, 1)], ACT.Exp,
                                             bias=sm[:, v, 1:2], scale=-1.0).then_inc(s["exps"], 1)
                    if u >= 2:
                        n = UNITS[u - 2][1]
                        w = att_lat(n)[1] * P
                        if u >= 4:
                            act.wait_ge(s["att_out"], nu + nu * i + u - 3)
                        act.wait_ge(s["p_turned"], nu * i + u - 1)
                        nc.scalar.copy(pT[:, (u - 2) % 2, 0:CTX + w], bank(0, 2)[:, 0:CTX + w])\
                          .then_inc(s["p_copied"], 1)
                steps.end(4)
            for k in range(KC):
                if k == 0:
                    act.wait_ge(s["att_o"], 8)
                nc.scalar.copy(op_hi[:, k, 0:S], g_t[:, k, :]).then_inc(s["op_hi"], 1)
            stream_squares("final", "wo_c", lambda k: [(xT[:, k, META:T2], 0, S)])
            act.wait_ge(s["norm_done"], 8)
            norm_squares("pre")
            norm_hi("pre")

            def halves(ps_):
                return seg2(ps_)

            def conv_silu(b, j):
                act.wait_ge(s["conv_in"], b + 1)
                nc.scalar.activation(xbc[:, bass.ds(b, 1), PAD:TP], conv[:, j:j + 1, :], ACT.Silu)\
                  .then_inc(s["conv_done"], 1)

            g0, b0 = SLAB0["xbc"], BLOCK0["xbc"]

            def xbc_pair(i, silu):
                for j in range(2):
                    act.wait_ge(s["slab_done"], g0 + j + 1 + 2 * i)
                    nc.scalar.activation(two(xbc[:, bass.ds(2 * i + j, 1), PAD:TP].rearrange("p a n -> p (a n)")),
                                         halves(gemm_ps[(b0 + j) % 2]), ACT.Copy).then_inc(s_evac[(b0 + j) % 2], 1)
                for j in range(2):
                    if silu:
                        conv_silu(2 * i + j - 2, j)

            xbc_pair(0, False)
            with act.Fori(1, XC // 2) as i:
                xbc_pair(i, True)
            evacuate("dt", lambda b: two(xbc[:, XC, PAD:TP]), halves, ACT.Copy)
            for j in range(2):
                conv_silu(XC - 2 + j, j)
            nc.scalar.preload_act_table_set("natural_log_exp_and_others")
            act.wait_ge(s["small_in"], SMALL)
            steps(nc.scalar.activation(neg_a[:, :], a_log[:, :], ACT.Exp))
            act.wait_ge(s["dt_e"], 1)
            steps(nc.scalar.activation(dtm[0:16, 2, :], dtm[0:16, 1, :], ACT.Exp))
            steps.wait()
            nc.scalar.activation(dtm[0:16, 1, :], dtm[0:16, 2, :], ACT.Ln, bias=1.0).then_inc(s["dt_l"], 1)
            g0z = SLAB0["z"]

            def take_z(t, j):
                act.wait_ge(s["slab_done"], g0z + j + 1 + 2 * t)
                nc.scalar.copy(two(zs[:, bass.ds(2 * t + j, 1), PAD:TP].rearrange("p a n -> p (a n)")),
                               halves(gemm_ps[0])).then_inc(s["z_evac"], 1)

            def chunk(t, with_z):
                act.wait_ge(s["dt_ready"], 1)
                act.wait_ge(s["ssd_used"], t + 1)
                nc.scalar.copy(xst[:, :, :], xbc[:, 0:XC, bass.ds(t * P, P)]).then_inc(s["chunk_in"], 1)
                nc.scalar.copy(dt_t[0:16, :], xbc[0:16, XC, bass.ds(t * P, P)]).then_inc(s["chunk_in"], 1)
                for g in range(2):
                    act.wait_ge(s["chunk_acs"], 2 * t + g + 1)
                    nc.scalar.activation(cexp[:, 8 * g:8 * g + 8, :].rearrange("p h l -> p (h l)"), bank(2, 2),
                                         ACT.Exp).then_inc(s["chunk_e"], 1)
                    if g == 0 and with_z:
                        take_z(t, 0)
                act.wait_ge(s["dec_in"], t + 1)
                nc.scalar.activation(dec[:, :], acs[:, :], ACT.Exp).then_inc(s["dec_ready"], 1)
                for g in range(2):
                    act.wait_ge(s["seg_ready"], 2 * t + g + 1)
                    nc.scalar.activation(seg[:, 8 * g:8 * g + 8, :], seg[:, 8 * g:8 * g + 8, :], ACT.Exp)\
                      .then_inc(s["seg_e"], 1)
                if with_z:
                    take_z(t, 1)

            with act.Fori(0, NT - 1) as t:
                chunk(t, True)
            chunk(NT - 1, False)
            act.wait_ge(s["z_evac"], KC + 1)
            nc.scalar.activation(zs[:, :, PAD:TP], zs[:, :, PAD:TP], ACT.Silu).then_inc(s["z_silu"], 1)
            g0 = SLAB0["sb"]

            def take(m, kind, done):
                act.wait_ge(s["slab_done"], done)
                dst, scale = ((qs, ATT_SCALE), (ks, 1.0), (vs, 1.0))[kind]
                nc.scalar.activation(two(dst[:, m, :]), seg2(gemm_ps[0]), ACT.Copy, scale=scale)\
                  .then_inc(s["sb_evac"], 1)

            act.wait_ge(s["ssd_used"], NT + 1)
            take(0, 0, g0 + 1)
            take(0, 1, g0 + 2)
            norm_squares("ssd", s["gated"])
            nc.scalar.preload_act_table_set("natural_log_exp_and_others")

            def sb_iteration(i, last):
                act.wait_ge(s["sb_y"], 2 * NT * i + 1)
                for u in range(SBN + SB_SKEW - 1):
                    if u >= 2 and u - 2 < SBN:
                        m, par, blk, nq, q0, nk, buf = sb_unit(u - 2)
                        w_ps, a = sb_bank(u - 2), sb_tile(u - 2, 1)
                        if u - 2 >= SB_BUFS:
                            before_it = u - 2 - SB_BUFS
                            act.wait_ge(s["sb_o"], 2 * NT * i + sb_out(before_it) + 1)
                        act.wait_ge(s["sb_wt"], SBN * i + u - 1)
                        ins = nc.scalar.copy(sb_wT[0:META, buf, 0, 0:nq], w_ps[0:META, 0:nq])
                        if blk:
                            ins = nc.scalar.copy(sb_wT[:, buf, 1:1 + blk, :].rearrange("p a n -> p (a n)"),
                                                 w_ps[:, a:a + blk * P])
                        ins.then_inc(s["sb_wc"], 1)
                    if u in SB_NORM:
                        j = SB_NORM.index(u)
                        act.wait_ge(s["hp"], HP0["ssd"] + j + 1 + 2 * i)
                        act.sem_inc(s["act_gate"], 1)
                        nc.scalar.copy(ys_hi[:, bass.ds(2 * i + j, 1), :], hp_ssd[:, j:j + 1, :])\
                          .then_inc(s["op_hi"], 1)
                    if u in SB_TAKE and (u < 10 or not last):
                        m, kind, g = SB_TAKE[u]
                        take(m, kind, g0 + 3 + g + 1 + 6 * i)
                    if 1 <= u <= SBN:
                        m, par, blk, nq, q0, nk, buf = sb_unit(u - 1)
                        total = sb_sum[0:nq, buf, 0:nk]
                        act.wait_ge(s["sb_d"], SBN * i + u)
                        nc.scalar.activation(total, total, ACT.Exp).then_inc(s["sb_wr"], 1)
                    if u < SBN:
                        m, par, blk, nq, q0, nk, buf = sb_unit(u)
                        neg = sb_neg[0:nq, buf, 0:nk]
                        act.wait_ge(s["sb_in"], SBN * i + u + 1)
                        nc.scalar.activation(neg, neg, ACT.Exp).then_inc(s["sb_l"], 1)
                        act.wait_ge(s["sb_l"], 2 * SBN * i + 2 * u + 1)
                        nc.scalar.activation(neg, neg, ACT.Ln, bias=1.0).then_inc(s["sb_l"], 1)

            with act.Fori(0, SB_PAIRS // 2 - 1) as i:
                sb_iteration(i, False)
            sb_iteration(SB_PAIRS // 2 - 1, True)
            act.wait_ge(s["sb_y"], SB_PAIRS * NT + 1)
            norm_squares("sbn")
            norm_hi("sbn")
            evacuate("wo_2", lambda b: two(mixT[:, bass.ds(b, 1), :].rearrange("p a n -> p (a n)")), halves,
                     ACT.Copy, ("post", mixT), late=1)
            for k in range(KC):
                act.wait_ge(s["norm_done"], 8 + k + 1)
                nc.scalar.activation(u_hi[:, k, :], xT[:, k, :], ACT.Identity, scale=col("ffn_pre", k))\
                  .then_inc(s["op_hi"], 1)
            norm_squares("ffn")
            g0, b0 = SLAB0["up"], BLOCK0["up"]
            with act.Fori(0, FC) as i:
                act.wait_ge(s["gate_conv"], i + 1)
                nc.scalar.activation(gacc[:, :], gacc[:, :], ACT.Gelu_apprx_tanh).then_inc(s["gelu"], 1)
                act.wait_ge(s["ffn_f"], i + 1)
                nc.scalar.copy(f_hi[:, bass.ds(i, 1), :], fgl[:, :].unsqueeze(1)).then_inc(s["ffn_hi"], 1)
            evacuate("down", lambda b: two(fT[:, bass.ds(b, 1), :].rearrange("p a n -> p (a n)")), halves,
                     ACT.Copy, ("fin", fT))

        @block.vector
        def _(dve):
            steps = Steps(dve, s["dve_steps"])

            def clear_sum(name):
                steps(nc.vector.memset(NORMS[name][3][:, 2, :], 0.0))
                steps.wait()

            def add_squares(name, k, slot):
                k0, tiles, _, sq, _ = NORMS[name]
                dve.wait_ge(s["sq"], 8 * k0 + 1 + k)
                n = sum(n for _, n in tiles)
                if k0 or k:
                    dve.wait_ge(s["sq_used"], 8 * k0 + k)
                nc.vector.tensor_tensor(sq[:, 2, 0:n], sq[:, 2, 0:n], sq[:, slot, 0:n], ALU.add)\
                  .then_inc(s["sq_used"], 1)

            def norm_adds(name):
                clear_sum(name)
                for k in range(KC):
                    add_squares(name, k, k % 2)

            def stream_adds(name):
                clear_sum(name)
                with dve.Fori(0, KC // 2) as i:
                    for j in range(2):
                        add_squares(name, 2 * i + j, j)

            def norm_rstd(name):
                k0, tiles, _, _, _ = NORMS[name]
                dve.wait_ge(s["std"], k0 + 1)
                nc.vector.reciprocal(rstd[:, 0:len(tiles)], stat[:, 0:len(tiles)]).then_inc(s["rstd"], 1)
                dve.wait_ge(s["rstd_rows"], k0 + 1)

            def norm_operand(name):
                _, _, _, _, hp = NORMS[name]
                hi, lo, c = OPERAND[name]
                hi0 = OP_DONE[name] - KC
                for k in range(KC + 1):
                    if k < KC:
                        if k >= 3:
                            dve.wait_ge(s["op_ready"], hi0 + k - 2)
                        for src, c0, n, gain, _ in norm_sources(name, k):
                            ins = nc.vector.scalar_tensor_tensor(hp[:, k % 3, c0:c0 + n], src, gain,
                                                                 rstd_rows(name, c0, n), ALU.mult, ALU.mult)
                        ins.then_inc(s["hp"], 1)
                    if k >= 1:
                        dve.wait_ge(s["op_hi"], hi0 + k)
                        for _, c0, n, _, shift in norm_sources(name, k - 1):
                            o, h = lo[:, c + k - 1, c0:c0 + n], hi[:, c + k - 1, c0:c0 + n].bitcast(F32)
                            a = hp[:, (k - 1) % 3, c0:c0 + n]
                            if shift is None:
                                ins = nc.vector.tensor_tensor(o, a, h, ALU.subtract)
                            else:
                                ins = nc.vector.scalar_tensor_tensor(o, a, shift, h, ALU.add, ALU.subtract)
                        ins.then_inc(s["op_ready"], 1)

            def take_cols(v, src):
                dve.wait_ge(s["vec_turned"], 3 if v else 1)
                r = VEC_ROWS[v]
                nc.vector.tensor_copy(cols[:, v, 0:r], src[:, 0:r]).then_inc(s["cols_ready"], 1)

            take_cols(0, bank(0))
            for k in range(KC):
                dve.wait_ge(s["x_turned"], k + 1)
                nc.vector.tensor_copy(lat(k), bank(k % 4)[:, :]).then_inc(s["x_ready"], 1)
            for k in range(0, KC, 2):
                dve.wait_ge(s["x_turned"], KC + k // 2 + 1)
                nc.vector.tensor_copy(ctxT[:, k:k + 2, :].rearrange("p k n -> p (k n)"),
                                      bank(k // 2 % 4)[:, :]).then_inc(s["x_ready"], 1)
            dve.wait_ge(s["x_turned"], 13)
            nc.vector.tensor_copy(xT[:, :, 0:META], bank(0)[:, 0:KC * META].rearrange("p (k n) -> p k n", k=KC))\
              .then_inc(s["x_ready"], 1)
            norm_adds("l0")
            norm_rstd("l0")

            def modulation(n0, n, src):
                steps(nc.vector.tensor_tensor(mod[:, n0:n0 + n, :], src.rearrange("p (n c) -> p n c", c=2),
                                              col("ada_b", n0, n).unsqueeze(2).to_broadcast([P, n, 2]), ALU.add))
                steps.wait()

            def norm_gain(layer):
                for k in range(2):
                    steps(nc.vector.scalar_tensor_tensor(
                        modg[:, layer, k, :], mod[:, 24 * layer + KC:24 * layer + 2 * KC, k], 1.0,
                        col("norm_g", KC * layer, KC), ALU.add, ALU.mult))
                steps.wait()

            dve.wait_ge(s["rows_turned"], 1)
            modulation(0, 2 * KC, bank(2)[:, 0:4 * KC])
            norm_gain(0)
            dve.sem_inc(s["mod_ready"], 1)
            norm_operand("l0")
            for v in range(1, 3):
                take_cols(v, bank(7)[:, (v - 1) * P:v * P])

            def ada_products(w, acc):
                for k in range(KC):
                    for c_ in range(2):
                        if k:
                            steps.wait(but=1)
                            steps(nc.vector.scalar_tensor_tensor(acc(c_), w[:, k, :], cond[:, k, c_:c_ + 1], acc(c_),
                                                                 ALU.mult, ALU.add))
                        else:
                            steps(nc.vector.tensor_scalar(acc(c_), w[:, k, :], cond[:, k, c_:c_ + 1], None,
                                                          ALU.mult))
                steps.wait()
                dve.sem_inc(s["ada_acc"], 1)

            with dve.Fori(0, ADA_L0 // ADA_RING) as i:
                steps.begin(i, ADA_RING * 2 * KC)
                for j in range(ADA_RING):
                    dve.wait_ge(s_ada_in[j], 16 + 16 * i)
                    ada_products(ada_ring[:, j, :, :],
                                 lambda c_: ada_acc[:, bass.ds(ADA_RING * i + j, 1), c_, :])
                steps.end(ADA_L0 // ADA_RING)
            dve.wait_ge(s["ada_sums"], 1)
            modulation(2 * KC, ADA_L0, bank(2)[:, 0:2 * ADA_L0])
            norm_gain(1)
            dve.sem_inc(s["mod1_ready"], 1)

            def v_norm(t):
                dve.wait_ge(s["v_turned"], t + 1)
                v_ps = bank(7)[:, :]
                if t:
                    dve.wait_ge(s["v_ready"], t)
                steps(nc.vector.bn_stats(bn[:, 0:6], v_ps))
                steps.wait()
                nc.vector.bn_aggr(mv[:, 0:2], bn[:, 0:6]).then_inc(s["v_stat"], 1)
                dve.wait_ge(s["v_std"], t + 1)
                steps(nc.vector.reciprocal(mv[:, 3:4], mv[:, 2:3]))
                steps.wait()
                nc.vector.tensor_scalar(vt[:, t, :], v_ps, mv[:, 0:1], mv[:, 3:4], ALU.subtract, ALU.mult)\
                  .then_inc(s["v_ready"], 1)

            def fourier_gate(g):
                dve.wait_ge(s["seq_dft"], g + 1)
                f_ps = gemm_ps[g % 2]
                nc.vector.tensor_tensor(zT[:, 12 + g, 0:S], f_ps[:, 0:S], zT[:, 16 + g, 0:S], ALU.mult)
                nc.vector.scalar_tensor_tensor(zT[:, 12 + g, S:SX], f_ps[:, S:SX], float(np.sqrt(S / CTX)),
                                               zT[:, 16 + g, S:SX], ALU.mult, ALU.mult).then_inc(s["yb_ready"], 1)

            for g in range(3):
                v_norm(2 * g)
                v_norm(2 * g + 1)
                if g == 2:
                    dve.wait_ge(s["sw_turned"], 1)
                    nc.vector.tensor_copy(swT[:, :, :].rearrange("p h q -> p (h q)"), bank(7)[:, :])\
                      .then_inc(s["sw_ready"], 1)
                fourier_gate(g)
            dve.wait_ge(s["small_in"], SMALL)
            for h in range(4):
                dve.wait_ge(s["spatial"], h + 1)
                nt = SX // P
                steps(nc.vector.scalar_tensor_tensor(
                    gmlp[:, :].rearrange("p (t q) -> p t q", t=nt),
                    pair_ps[h % 2][:, 0:SX].rearrange("p (t q) -> p t q", t=nt), col("v_norm", h),
                    s_bias[:, h:h + 1, :].to_broadcast([P, nt, P]), ALU.mult, ALU.add))
                steps.wait()
                steps(nc.vector.tensor_tensor(zT[:, h, :], zT[:, h, :], gmlp[:, :], ALU.mult))
                steps.wait()
                nc.vector.tensor_tensor(zT[:, h, :], zT[:, h, :], zT[:, 8 + h, :], ALU.mult).then_inc(s["ya_ready"], 1)
            for k in range(KC):
                if k == 7:
                    fourier_gate(3)
                dve.wait_ge(s["op_hi"], OP_DONE["l0"] + k + 1)
                nc.vector.tensor_tensor(op_lo[:, k, :], y0_chunk(k), op_hi[:, k, :].bitcast(F32), ALU.subtract)\
                  .then_inc(s["op_ready"], 1)

            def add_gated(name, layer, with_ctx, norm):
                b0 = BLOCK0[name]
                clear_sum(norm)

                def blocks(i, adds):
                    for j in range(2):
                        dve.wait_ge(s["slab_done"], block_done(name, j + 1) + 2 * i)
                        o = gemm_ps[(b0 + j) % 2]
                        gate = mod[:, bass.ds(2 * i + (24 * layer + 2 * KC + j), 1), :]
                        x_k = xT[:, bass.ds(2 * i + j, 1), META:T2]
                        ins = nc.vector.scalar_tensor_tensor(x_k, o[:, 0:S].unsqueeze(1), gate[:, 0, 0:1], x_k,
                                                             ALU.mult, ALU.add)
                        if with_ctx:
                            c_k = ctxT[:, bass.ds(2 * i + j, 1), :]
                            ins = nc.vector.scalar_tensor_tensor(c_k, o[:, S:SX].unsqueeze(1), gate[:, 0, 1:2], c_k,
                                                                 ALU.mult, ALU.add)
                        ins.then_inc(s_evac[(b0 + j) % 2], 1)
                    for j in range(2):
                        if adds:
                            add_squares(norm, 2 * i + (j - 2), j)

                blocks(0, False)
                with dve.Fori(1, KC // 2) as i:
                    blocks(i, True)
                for j in range(2):
                    add_squares(norm, KC - 2 + j, j)

            add_gated("wo_ab", 0, True, "l1")
            all_evacuated(dve, "wo_ab")
            norm_rstd("l1")
            norm_operand("l1")
            for j in range(ADA_L1):
                dve.wait_ge(s["ada1_in"], 16 * ADA_L1)
                ada_products(ada_ring1[:, j, :, :], lambda c_: ada_acc1[:, j, c_, :])
            steps(nc.vector.tensor_scalar(neg_sink[:, :], sink[:, :], -1.0, None, ALU.mult))
            HALF_SWAP = [p ^ 16 for p in range(32)]
            dve.wait_ge(s["consts_in"], 16 * 10)
            all_evacuated(dve, "q")
            with dve.Fori(0, KC) as i:
                steps.begin(i, 5)
                q_k = q_t[:, bass.ds(i, 1), :]
                steps.wait()
                steps(nc.vector.tensor_copy(rot[:, 1:2, :], q_k))
                steps.wait()
                steps(nc.vector.tensor_tensor(q_k, rot[:, 1:2, :], cos[:, :].unsqueeze(1), ALU.mult))
                steps(nc.vector.stream_shuffle(rot[:, 0, :], rot[:, 1, :], HALF_SWAP))
                steps.wait()
                steps(nc.vector.tensor_tensor(rot[:, 0, :], rot[:, 0, :], sin[:, :], ALU.mult))
                steps.wait()
                steps(nc.vector.tensor_tensor(q_k, q_k, rot[:, 0:1, :], ALU.add))
                steps.end(KC)
            steps.wait()
            all_evacuated(dve, "kv")
            for k in range(2):
                steps(nc.vector.stream_shuffle(rot[:, 0, :], kv_t[:, k, 0:S], HALF_SWAP))
                steps.wait()
                steps(nc.vector.tensor_tensor(rot[:, 0, :], rot[:, 0, :], sin[:, :], ALU.mult))
                steps(nc.vector.tensor_tensor(rot[:, 1, :], kv_t[:, k, 0:S], cos[:, :], ALU.mult))
                steps.wait()
                steps(nc.vector.tensor_tensor(kv_t[:, k, 0:S], rot[:, 0, :], rot[:, 1, :], ALU.add))
                steps.wait()
            for h in range(4):
                for half in range(2):
                    a = HEAD * (h % 2)
                    steps(nc.vector.tensor_copy(k_dup[HEAD * half:HEAD * half + HEAD, h, :],
                                                kv_t[a:a + HEAD, h // 2, :]))
            dve.wait_ge(s["vtok_turned"], 1)
            steps(nc.vector.tensor_copy(v_tok[:, :, :],
                                        bank(4, 3).rearrange("p (t n) -> p t n", t=SX // P)))
            steps.wait()
            dve.sem_inc(s["vtok_ready"], 1)
            dve.wait_ge(s["ada_sums"], 2)
            modulation(2 * KC + ADA_L0, ADA_L1, bank(7)[:, 0:2 * ADA_L1])
            dve.sem_inc(s["gate1_ready"], 1)
            all_evacuated(dve, "gc")
            nu = len(UNITS)
            per = 3 + sum(1 + (n > 0) + (n < 3) for _, n, _ in UNITS) + 2 * nu
            with dve.Fori(0, 4) as i:
                steps.begin(i, per)
                dve.wait_ge(s["att_out"], nu * i + nu)
                steps(nc.vector.tensor_copy(q_st[:, :, :], q_t[:, bass.ds(2 * i, 2), :]))
                steps(nc.vector.tensor_copy(k_st[:, :].unsqueeze(1), k_dup[:, bass.ds(i, 1), :]))
                steps(nc.vector.tensor_copy(v_st[:, :, :], v_tok[:, :, bass.ds(HEAD * i, HEAD)]))
                steps.wait()
                dve.sem_inc(s["att_in"], 1)
                for u in range(nu + 1):
                    if u < nu:
                        c2, n, par = UNITS[u]
                        v, w = u % ATT_BUFS, att_lat(n)[1] * P
                        sc = pair_ps[u % 2]
                        dve.wait_ge(s["scores"], nu * i + u + 1)
                        if n > 0:
                            steps(nc.vector.tensor_tensor(sc[:, S:S + P], sc[:, S:S + P], at_or_after[:, :], ALU.add))
                        if n < 3:
                            steps(nc.vector.tensor_tensor(sc[:, S + w - P:S + w], sc[:, S + w - P:S + w],
                                                          at_or_before[:, :], ALU.add))
                        steps.wait()
                        steps(nc.vector.tensor_reduce(sm[:, v, 0:1], sc[:, CTX:S + w], AX.X, ALU.max))
                        steps.wait()
                        head = 2 * c2 + par
                        nc.vector.tensor_scalar(sm[:, v, 1:2], sm[:, v, 0:1], -ATT_SCALE,
                                                neg_sink[:, bass.ds(4 * i + head, 1)], ALU.mult, ALU.min)\
                          .then_inc(s["nmax"], 1)
                    if u >= 1:
                        v = (u - 1) % ATT_BUFS
                        w = att_lat(UNITS[u - 1][1])[1] * P
                        dve.wait_ge(s["exps"], 2 * nu * i + 2 * u)
                        steps(nc.vector.tensor_tensor(sm[:, v, 4:5], sm[:, v, 2:3], sm[:, v, 3:4], ALU.add))
                        steps.wait()
                        steps(nc.vector.reciprocal(sm[:, v, 5:6], sm[:, v, 4:5]))
                        steps.wait()
                        nc.vector.tensor_scalar(p_sb[:, v, 0:CTX + w], p_sb[:, v, 0:CTX + w], sm[:, v, 5:6], None,
                                                ALU.mult).then_inc(s["probs"], 1)
                    if u in (12, nu):
                        c2 = 0 if u < nu else 1
                        dve.wait_ge(s["att_out"], nu * i + nu + 8 * (c2 + 1))
                        g_k = g_t[:, bass.ds(2 * i + c2, 1), :]
                        nc.vector.tensor_tensor(g_k, bank(2 + c2)[:, :].unsqueeze(1), g_k, ALU.mult)\
                          .then_inc(s["att_o"], 1)
                steps.end(4)
            for k in range(KC):
                dve.wait_ge(s["op_hi"], OP_DONE["l1"] + k + 1)
                if k == 0:
                    dve.wait_ge(s["att_o"], 8)
                nc.vector.tensor_tensor(op_lo[:, k, 0:S], g_t[:, k, :], op_hi[:, k, 0:S].bitcast(F32), ALU.subtract)\
                  .then_inc(s["op_ready"], 1)
            add_gated("wo_c", 1, False, "final")
            all_evacuated(dve, "wo_c")
            norm_rstd("final")
            for k in range(KC):
                src, c0, n, gain, _ = norm_sources("final", k)[0]
                nc.vector.scalar_tensor_tensor(src, src, gain, rstd_rows("final", c0, n), ALU.mult, ALU.mult)\
                  .then_inc(s["norm_done"], 1)
            dve.wait_ge(s["norm_done"], 8)
            norm_adds("pre")
            norm_rstd("pre")
            norm_operand("pre")
            steps(nc.vector.memset(xbc[:, :, 0:PAD], 0.0))
            steps(nc.vector.memset(prev[:, :], 0.0))
            b0 = BLOCK0["xbc"]
            taps = 4
            with dve.Fori(0, XC // 2) as i:
                steps.begin(i, 2 * (taps - 1))
                for j in range(2):
                    xk = xbc[:, bass.ds(2 * i + j, 1), :]

                    def w_col(k):
                        return cols[:, 1, bass.ds(2 * i + (j + XC * k), 1)]

                    dve.wait_ge(s_evac[(b0 + j) % 2], 2 + (b0 + j) // 2 + i)
                    dve.wait_ge(s["conv_done"], 2 * i + j + 1)
                    steps(nc.vector.tensor_scalar(conv[:, j:j + 1, :], xk[:, :, PAD:TP], w_col(taps - 1),
                                                  cols[:, 1, bass.ds(2 * i + (j + VEC_B["conv_b"]), 1)],
                                                  ALU.mult, ALU.add))
                    for k in range(1, taps):
                        steps.wait()
                        o = conv[:, j:j + 1, k:T2]
                        ins = nc.vector.scalar_tensor_tensor(o, xk[:, :, PAD:TP - k], w_col(taps - 1 - k), o,
                                                             ALU.mult, ALU.add)
                        if k < taps - 1:
                            steps(ins)
                        else:
                            ins.then_inc(s["conv_in"], 1)
                steps.end(XC // 2)
            all_evacuated(dve, "dt")
            dtr = xbc[0:16, XC, PAD:TP]
            dve.wait_ge(s["small_in"], SMALL)
            steps(nc.vector.tensor_scalar(dtm[0:16, 0, :], dtr, dt_bias[0:16, 0:1], None, ALU.add))
            steps.wait()
            steps(nc.vector.tensor_scalar(dtm[0:16, 2, :], dtm[0:16, 0, :], 0.0, -2.0, ALU.max, ALU.mult))
            steps.wait()
            nc.vector.tensor_tensor(dtm[0:16, 1, :], dtm[0:16, 0, :], dtm[0:16, 2, :], ALU.add)\
              .then_inc(s["dt_e"], 1)
            dve.wait_ge(s["dt_l"], 1)
            steps(nc.vector.scalar_tensor_tensor(dtr, dtm[0:16, 0, :], 0.0, dtm[0:16, 1, :], ALU.max, ALU.add))
            steps(nc.vector.tensor_scalar(neg_a[:, :], neg_a[:, :], -1.0, None, ALU.mult))
            steps.wait()
            dve.wait_ge(s["conv_done"], XC + 2)
            dve.sem_inc(s["dt_ready"], 1)
            dve.sem_inc(s["ssd_used"], 1)
            H = 16
            with dve.Fori(0, NT) as t:
                steps.begin(t, 14)
                back = bass.ds(t * P, P)
                steps.wait()

                def by_head(ap, n):
                    return ap.unsqueeze(2).to_broadcast([P, H, n])

                dve.wait_ge(s["chunk_turned"], t + 1)
                steps(nc.vector.tensor_copy(dt_k[:, :], pair_ps[1][:, 2 * P:2 * P + H]))
                nc.vector.tensor_copy(b_tok[:, :], pair_ps[1][:, 0:2 * P]).then_inc(s["chunk_b"], 1)
                steps.wait()
                steps(nc.vector.tensor_tensor(adt[:, :], dt_k[:, :], neg_a[:, :], ALU.mult))
                steps(nc.vector.tensor_tensor(xdt[:, :].rearrange("p (h d) -> p h d", h=H),
                                              pair_ps[0][:, :].rearrange("p (h d) -> p h d", h=H),
                                              by_head(dt_k[:, :], HEAD), ALU.mult))
                steps.wait()
                dve.sem_inc(s["chunk_scaled"], 1)
                dve.wait_ge(s["chunk_acs"], 2 * t + 1)
                a_ps = pair_ps[1][:, S:S + 2 * H]
                a_ps_cb = pair_ps[1][:, S + P:S + 3 * P].rearrange("p (g l) -> p g l", g=2)
                steps(nc.vector.tensor_copy(acs[:, :], a_ps))
                steps.wait()
                steps(nc.vector.tensor_tensor(cb[:, :, :], a_ps_cb, tri[:, :].unsqueeze(1).to_broadcast([P, 2, P]),
                                              ALU.mult))
                for g in range(2):
                    seg_g = seg[:, 8 * g:8 * g + 8, :]
                    dve.wait_ge(s["chunk_acs"], 2 * t + g + 1)
                    dve.wait_ge(s["chunk_e"], 2 * t + g + 1)
                    nc.vector.tensor_tensor(seg_g, bank(2, 2).rearrange("p (h l) -> p h l", h=8),
                                            acs[:, 8 * g:8 * g + 8].unsqueeze(2).to_broadcast([P, 8, P]),
                                            ALU.subtract).then_inc(s["seg_sub"], 1)
                    dve.wait_ge(s["seg_sub"], 2 * t + g + 1)
                    nc.vector.tensor_scalar(seg_g, seg_g, 0.0, None, ALU.min).then_inc(s["seg_ready"], 1)
                    c_g = cexp[:, 8 * g:8 * g + 8, :]
                    steps(nc.vector.tensor_tensor(c_g, c_g, xst[:, 10 + g:11 + g, :].to_broadcast([P, 8, P]),
                                                  ALU.mult))
                steps(nc.vector.tensor_tensor(acs[:, 0:H], acs[:, H:2 * H], acs[:, 0:H], ALU.subtract))
                steps.wait()
                dve.sem_inc(s["dec_in"], 1)
                steps(nc.vector.tensor_tensor(xst[:, 0:KC, :], xst[:, 0:KC, :],
                                              skip[:, :].unsqueeze(2).to_broadcast([P, KC, P]), ALU.mult))
                for g in range(2):
                    l_g = seg[:, 8 * g:8 * g + 8, :]
                    dve.wait_ge(s["seg_e"], 2 * t + g + 1)
                    steps(nc.vector.tensor_tensor(l_g, l_g, cb[:, g:g + 1, :].to_broadcast([P, 8, P]), ALU.mult))
                dve.wait_ge(s["dec_ready"], t + 1)
                steps(nc.vector.tensor_tensor(xdd[:, :].rearrange("p (h d) -> p h d", h=H),
                                              xdt[:, :].rearrange("p (h d) -> p h d", h=H),
                                              by_head(dec[:, 0:H], HEAD), ALU.mult))
                steps.wait()
                dve.sem_inc(s["ssd_operands"], 1)
                dve.wait_ge(s["ssd_y"], t + 1)
                steps(nc.vector.tensor_tensor(xbc[:, 0:KC, back], xst[:, 0:KC, :],
                                              pair_ps[0][:, :].rearrange("p (k l) -> p k l", k=KC), ALU.add))
                pv = prev[:, :].rearrange("p (h d) -> p h d", h=H)
                steps(nc.vector.tensor_tensor(pv, pv, by_head(dec[:, H:2 * H], HEAD), ALU.mult))
                steps.wait()
                dve.wait_ge(s["ssd_state"], t + 1)
                nc.vector.tensor_tensor(prev[:, :], prev[:, :], pair_ps[1][:, :], ALU.add).then_inc(s["ssd_used"], 1)
                steps.end(NT)
            steps.wait()
            dve.wait_ge(s["z_silu"], 1)
            for k in range(KC):
                z_k = zs[:, k, PAD:TP]
                nc.vector.tensor_tensor(z_k, z_k, xbc[:, k, PAD:TP], ALU.mult).then_inc(s["gated"], 1)
            norm_adds("ssd")
            norm_rstd("ssd")
            nc.vector.tensor_copy(rstd_ssd[:, :], rstd_rows("ssd", 0, T2)).then_inc(s["rows_kept"], 1)
            dve.wait_ge(s["ssd_used"], NT + 1)

            dve.wait_ge(s["rows_kept"], 1)

            def sb_iteration(i):
                for u in range(SBN + SB_SKEW):
                    if u + 1 in SB_NORM:
                        j = SB_NORM.index(u + 1)
                        nc.vector.scalar_tensor_tensor(hp_ssd[:, j:j + 1, :], zs[:, bass.ds(2 * i + j, 1), PAD:TP],
                                                       cols[:, 0, bass.ds(2 * i + (COL["ssd_norm"] + j), 1)],
                                                       rstd_ssd[:, :].unsqueeze(1), ALU.mult, ALU.mult)\
                          .then_inc(s["hp"], 1)
                    if u - 1 in SB_NORM:
                        j = SB_NORM.index(u - 1)
                        dve.wait_ge(s["op_hi"], OP_DONE["pre"] + j + 1 + 2 * i)
                        nc.vector.tensor_tensor(ys_lo[:, bass.ds(2 * i + j, 1), :], hp_ssd[:, j:j + 1, :],
                                                ys_hi[:, bass.ds(2 * i + j, 1), :].bitcast(F32), ALU.subtract)\
                          .then_inc(s["op_ready"], 1)
                    if u >= SB_SKEW and sb_outputs(u - SB_SKEW):
                        m, par, blk, nq, q0, nk, buf = sb_unit(u - SB_SKEW)
                        n = P if blk else META
                        h = sb_out(u - SB_SKEW)
                        dve.wait_ge(s["sb_o"], 2 * NT * i + h + 1)
                        o = sb_bank(u - SB_SKEW)[:, 0:n].unsqueeze(1)
                        nc.vector.tensor_copy(ysb[:, bass.ds(2 * i + m, 1), q0:q0 + n], o).then_inc(s["sb_y"], 1)
                    if 1 <= u <= SBN:
                        m, par, blk, nq, q0, nk, buf = sb_unit(u - 1)
                        relu, neg, total = (a[0:nq, buf, :] for a in (sb_relu, sb_neg, sb_sum))
                        z_ps = sb_bank(u - 1)[0:nq, sb_key0(u - 1):sb_key0(u - 1) + nk]
                        if u > SB_BUFS:
                            dve.wait_ge(s["sb_wt"], SBN * i + u - SB_BUFS)
                        dve.wait_ge(s["sb_l"], 2 * SBN * i + 2 * u)
                        steps(nc.vector.tensor_tensor_scan(total[:, nk - 1::-1], relu[:, nk - 1::-1],
                                                           neg[:, nk - 1::-1], 0.0, ALU.add, ALU.add))
                        steps.wait()
                        nc.vector.tensor_tensor(total[:, 0:nk], z_ps, total[:, 0:nk], ALU.subtract)\
                          .then_inc(s["sb_d"], 1)
                    if u < SBN:
                        m, par, blk, nq, q0, nk, buf = sb_unit(u)
                        relu, neg = (a[0:nq, buf, 0:nk] for a in (sb_relu, sb_neg))
                        z_ps = sb_bank(u)[0:nq, sb_key0(u):sb_key0(u) + nk]
                        own, mask = (z_ps[:, nk - P:nk], before) if blk else (z_ps, before_meta)
                        dve.wait_ge(s["sb_scores"], SBN * i + u + 1)
                        steps(nc.vector.tensor_tensor(own, own, mask[0:nq, :], ALU.add))
                        steps.wait()
                        steps(nc.vector.tensor_scalar(relu, z_ps, 0.0, None, ALU.max))
                        steps.wait()
                        nc.vector.scalar_tensor_tensor(neg, relu, -2.0, z_ps, ALU.mult, ALU.add)\
                          .then_inc(s["sb_in"], 1)
                    if u % len(SBU) == 0 and u < SBN:
                        m = u // len(SBU)
                        dve.wait_ge(s["sb_vt"], 2 * i + m + 1)
                        steps(nc.vector.tensor_copy(v_sb[0:META, m, 0, :], gemm_ps[0][0:META, 0:P]))
                        steps(nc.vector.tensor_copy(v_sb[:, m, 1:NT, :].rearrange("p t n -> p (t n)"),
                                                    gemm_ps[0][:, P:NT * P]))
                        steps.wait()
                        dve.sem_inc(s["sb_v"], 1)

            with dve.Fori(0, SB_PAIRS // 2) as i:
                steps.begin(i, 2 * (2 + 3 * len(SBU)))
                sb_iteration(i)
                steps.end(SB_PAIRS // 2)
            dve.wait_ge(s["sb_y"], SB_PAIRS * NT + 1)
            norm_adds("sbn")
            norm_rstd("sbn")
            dve.wait_ge(s["slab_done"], SLAB0["wo_2"])
            norm_operand("sbn")

            def add_normed(name, operand=None):
                _, _, _, _, hp = NORMS[name]
                norm_rstd(name)
                n0 = 8 * (NORMS[name][0] == 6) + 16 * (NORMS[name][0] == 8)
                for k in range(KC + 3):
                    if k < KC:
                        src, c0, n, gain, _ = norm_sources(name, k)[0]
                        if k >= 3:
                            dve.wait_ge(s["norm_done"], n0 + k - 2)
                        nc.vector.scalar_tensor_tensor(hp[:, k % 3, 0:n], src, gain, rstd_rows(name, c0, n),
                                                       ALU.mult, ALU.mult).then_inc(s["normed"], 1)
                    if 1 <= k <= KC:
                        dve.wait_ge(s["normed"], n0 - 8 + k)
                        nc.vector.tensor_tensor(xT[:, k - 1, :], xT[:, k - 1, :], hp[:, (k - 1) % 3, 0:T2], ALU.add)\
                          .then_inc(s["norm_done"], 1)
                    if operand and 3 <= k:
                        operand(k - 3)

            def ffn_lo(k):
                dve.wait_ge(s["op_hi"], OP_DONE["sbn"] + k + 1)
                nc.vector.scalar_tensor_tensor(u_lo[:, k, :], xT[:, k, :], col("ffn_pre", k), u_hi[:, k, :].bitcast(F32),
                                               ALU.mult, ALU.subtract).then_inc(s["op_ready"], 1)

            stream_adds("post")
            add_normed("post", ffn_lo)
            norm_adds("ffn")
            norm_rstd("ffn")
            steps(nc.vector.tensor_copy(rstd_ffn[:, :], rstd_rows("ffn", 0, T2)))
            steps(nc.vector.memset(gp[:, 0:2], 0.0))
            steps.wait()
            g0, b0 = SLAB0["up"], BLOCK0["up"]
            with dve.Fori(0, FC) as i:
                steps.begin(i, 4)

                def w_col(k):
                    return cols[:, 2, bass.ds(i + FC * k, 1)]

                dve.wait_ge(s["slab_done"], g0 + 1 + 2 * i)
                steps.wait()
                nc.vector.tensor_tensor(two(gp[:, 2:2 + T2]), seg2(gemm_ps[b0 % 2]), two(rstd_ffn[:, :]), ALU.mult)\
                  .then_inc(s_evac[b0 % 2], 1)
                dve.wait_ge(s_evac[b0 % 2], 2 + b0 // 2 + i)
                steps(nc.vector.tensor_scalar(gacc[:, :], gp[:, 2:2 + T2], w_col(2),
                                              cols[:, 1, bass.ds(i + VEC_B["ffn_b"], 1)], ALU.mult, ALU.add))
                steps.wait()
                steps(nc.vector.scalar_tensor_tensor(gacc[:, :], gp[:, 1:1 + T2], w_col(1), gacc[:, :],
                                                     ALU.mult, ALU.add))
                steps.wait()
                nc.vector.scalar_tensor_tensor(gacc[:, :], gp[:, 0:T2], w_col(0), gacc[:, :], ALU.mult, ALU.add)\
                  .then_inc(s["gate_conv"], 1)
                dve.wait_ge(s["gelu"], i + 1)
                steps(nc.vector.tensor_tensor(gacc[:, :], gacc[:, :], rstd_ffn[:, :], ALU.mult))
                steps.wait()
                dve.wait_ge(s["slab_done"], g0 + 2 + 2 * i)
                nc.vector.tensor_tensor(two(fgl[:, :]), seg2(gemm_ps[(b0 + 1) % 2]), two(gacc[:, :]), ALU.mult)\
                  .then_inc(s["ffn_f"], 1)
                dve.wait_ge(s["ffn_f"], i + 1)
                dve.sem_inc(s_evac[(b0 + 1) % 2], 1)
                dve.wait_ge(s["ffn_hi"], i + 1)
                steps(nc.vector.tensor_tensor(f_lo[:, bass.ds(i, 1), :], fgl[:, :].unsqueeze(1),
                                              f_hi[:, bass.ds(i, 1), :].bitcast(F32), ALU.subtract))
                steps.wait()
                dve.sem_inc(s["op_ready"], 1)
                steps.end(FC)
            dve.wait_ge(s["op_ready"], OP_DONE["ffn"] + FC)
            stream_adds("fin")
            add_normed("fin")
            for t in range(S // P):
                dve.wait_ge(s["out_turned"], t + 1)
                nc.vector.tensor_copy(y_out[:, t, :], gemm_ps[t % 2][:, :]).then_inc(s["out_ready"], 1)

        @block.tensor
        def _(pe):
            mm = nc.tensor.matmul

            def sums_end(name):
                k0, tiles, _, sq, _ = NORMS[name]
                o = pair_ps[1]
                mm(o[:, 0:len(tiles)], zeros[:, :], zeros[:, 0:len(tiles)], start=True, stop=True)
                pe.wait_ge(s["sq_used"], 8 * k0 + 8)
                for t, (c0, n) in enumerate(tiles):
                    ins = mm(o[0:n, t:t + 1], sq[:, 2, c0:c0 + n], ones[:, 0:1], start=False, stop=True,
                             skip_group_check=True)
                ins.then_inc(s["ssq"], 1)
                sums_rows(name)

            def sums_rows(name):
                k0, tiles, _, _, _ = NORMS[name]
                pe.wait_ge(s["rstd"], k0 + 1)
                for t, (c0, n) in enumerate(tiles):
                    ins = mm(rstd_rows(name, c0, n), rstd[0:n, t:t + 1].to_broadcast([n, P]), ident[0:n, 0:n],
                             start=True, stop=True)
                ins.then_inc(s["rstd_rows"], 1)

            def products(o, hi, lo, w_h, w_l, kn, k0, segs, first, last, slab_end=True, ready=None):
                for k in range(kn):
                    if ready is not None:
                        pe.wait_ge(s["op_ready"], ready + k0 + k + 1)
                    a, z = first and k == 0, last and k == kn - 1
                    for b, (c0, n) in enumerate(segs):
                        mm(o[:, 512 * b:512 * b + n], w_h[:, k, :], hi[:, k0 + k, c0:c0 + n], start=a, stop=False)
                        mm(o[:, 512 * b:512 * b + n], w_h[:, k, :], lo[:, k0 + k, c0:c0 + n], start=False, stop=False)
                    for b, (c0, n) in enumerate(segs):
                        ins = mm(o[:, 512 * b:512 * b + n], w_l[:, k, :], hi[:, k0 + k, c0:c0 + n], start=False,
                                 stop=z)
                if slab_end:
                    ins.then_inc(s["slab_done"], 1)

            def gemm(name, hi, lo, segs, ready=None, cuts=((0, KC),), beside=None):
                per, g0, b0 = PER[name], SLAB0[name], BLOCK0[name]
                n = SLABS[name] // per
                u = 2 if n % 2 == 0 else 1

                def body(i, ready=None):
                    for jb in range(u):
                        b = b0 + jb
                        pe.wait_ge(s_evac[b % 2], 1 + b // 2 + (i if u == 2 else 0))
                        for h, (k0, kn) in enumerate(cuts):
                            j = jb * per + h
                            slot = (g0 + j) % 2
                            pe.wait_ge(s["split"], g0 + j + 1 + u * per * i)
                            products(gemm_ps[b % 2], hi, lo, w_hi[:, slot, :, :], w_lo[:, slot, :, :], kn, k0, segs,
                                     h == 0, h == per - 1, ready=ready if jb == 0 else None)

                body(0, ready)
                if beside:
                    beside()
                if n > u:
                    with pe.Fori(1, n // u) as i:
                        body(i)

            def turn_cols(v, o):
                r = VEC_ROWS[v]
                nc.tensor.transpose(o[:, 0:r], vec_in[0:r, v, :], ident[0:r, 0:r]).then_inc(s["vec_turned"], 1)

            pe.wait_ge(s["vec_in"], 16 * 9)
            pe.wait_ge(s["consts_in"], 16)
            turn_cols(0, bank(0))

            def ada_rows(j):
                pe.wait_ge(s_ada_first[j], 16)
                if j >= 2:
                    pe.wait_ge(s["rows_taken"], j - 1)
                for k in range(KC):
                    ins = mm(ada_rows_at(j), cond[:, k, :], ada_first[:, j % 3, k, :], start=(k == 0),
                             stop=(k == KC - 1))
                ins.then_inc(s["ada_rows"], 1)

            pe.wait_ge(s["cond_ready"], 2)
            ada_rows(0)
            pe.wait_ge(s["x_in"], 16 * 3)
            for k in range(KC):
                if k >= 4:
                    pe.wait_ge(s["x_ready"], k - 3)
                for t in range(S // P):
                    ins = nc.tensor.transpose(bank(k % 4)[:, t * P:(t + 1) * P], x_in[:, t, k * P:(k + 1) * P],
                                              ident[:, :])
                ins.then_inc(s["x_turned"], 1)
            for k in range(0, KC, 2):
                pe.wait_ge(s["x_ready"], 5 + k // 2)
                for a in range(2):
                    for t in range(CTX // P):
                        ins = nc.tensor.transpose(bank(k // 2 % 4)[:, a * CTX + t * P:a * CTX + (t + 1) * P],
                                                  ctx_in[:, t, (k + a) * P:(k + a + 1) * P], ident[:, :])
                ins.then_inc(s["x_turned"], 1)
            pe.wait_ge(s["x_ready"], 9)
            for k in range(KC):
                ins = nc.tensor.transpose(bank(0)[:, k * META:(k + 1) * META], meta_in[:, k * P:(k + 1) * P],
                                          ident[0:META, 0:META])
            ins.then_inc(s["x_turned"], 1)
            pe.wait_ge(s["x_ready"], 13)
            ada_rows(1)
            pe.wait_ge(s["fill_ready"], 3)
            sums_end("l0")
            ada_rows(2)
            ada_rows(3)
            pe.wait_ge(s["rows_taken"], ADA_FIRST)
            for n in range(2 * KC):
                ins = nc.tensor.transpose(bank(2)[:, 2 * n:2 * n + 2], m_rows[:, n * P:(n + 1) * P], ident[0:2, 0:2])
            ins.then_inc(s["rows_turned"], 1)
            pe.wait_ge(s["vec2_in"], 16 * 7)
            for v in range(1, 3):
                turn_cols(v, bank(7)[:, (v - 1) * P:v * P])
            pe.wait_ge(s["mod_ready"], 1)
            gemm("uv", op_hi, op_lo, SEG_XC, ready=0)
            gemm("ga", op_hi, op_lo, SEG_XC)
            gemm("xb", op_hi, op_lo, SEG_XC)
            gemm("gb", op_hi, op_lo, SEG_XC)
            all_evacuated(pe, "gb")
            pe.wait_ge(s["ada_acc"], ADA_RING + ADA_L0)
            for a in range(ADA_L0):
                for c_ in range(2):
                    ins = mm(bank(2)[:, 2 * a + c_:2 * a + c_ + 1], ada_acc[:, a, c_, :], ones[:, 0:1], start=True,
                             stop=True)
            ins.then_inc(s["ada_sums"], 1)
            pe.wait_ge(s["cols_ready"], 3)
            pe.wait_ge(s["dft_in"], 16 * 2)

            def turn_v(t):
                if t:
                    pe.wait_ge(s["v_ready"], t)
                for h in range(4):
                    ins = nc.tensor.transpose(bank(7)[:, h * P:(h + 1) * P], zT[:, 4 + h, t * P:(t + 1) * P],
                                              ident[:, :])
                ins.then_inc(s["v_turned"], 1)

            for g in range(4):
                if g:
                    pe.wait_ge(s["pq_ready"], g)
                for t in range(SX // P):
                    ins = mm(ps[:, 4 * 512 + t * 2 * P:4 * 512 + (t + 1) * 2 * P], zT[:, 12 + g, t * P:(t + 1) * P],
                             dft_ch[:, :], start=True, stop=True)
                ins.then_inc(s["ch_dft"], 1)
                if g < 3:
                    turn_v(2 * g)
                else:
                    pe.wait_ge(s["v_ready"], SX // P)
                    pe.wait_ge(s["sw_ready"], 1)
                    pe.wait_ge(s["pq_ready"], 4)
                    for h in range(4):
                        if h >= 2:
                            pe.wait_ge(s["ya_ready"], h - 1)
                        for t in range(SX // P):
                            ins = mm(pair_ps[h % 2][:, t * P:(t + 1) * P], vt[:, t, h * P:(h + 1) * P], swT[:, h, :],
                                     start=True, stop=True)
                        ins.then_inc(s["spatial"], 1)
                pe.wait_ge(s["pq_ready"], g + 1)
                if g == 1:
                    pe.wait_ge(s["mod1_ready"], 1)
                if g >= 2:
                    pe.wait_ge(s["yb_ready"], g - 1)
                o = gemm_ps[g % 2]
                nx = S // P
                for t in range(nx):
                    for r in range(2):
                        mm(o[:, 0:S], pq[:, t, r * P:(r + 1) * P], dft_seq[:, t, r, :], start=(t + r == 0),
                           stop=(t == nx - 1 and r == 1))
                for t in range(CTX // P):
                    for r in range(2):
                        ins = mm(o[:, S:SX], pq[:, nx + t, r * P:(r + 1) * P], dft_seq[:, t, r, 0:S:S // CTX],
                                 start=(t + r == 0), stop=(t == CTX // P - 1 and r == 1))
                ins.then_inc(s["seq_dft"], 1)
                if g < 3:
                    turn_v(2 * g + 1)
                if g == 2:
                    pe.wait_ge(s["small_in"], SMALL)
                    pe.wait_ge(s["v_ready"], SX // P)
                    for h in range(4):
                        ins = nc.tensor.transpose(bank(7)[:, h * P:(h + 1) * P], sw[:, h, :], ident[:, :])
                    ins.then_inc(s["sw_turned"], 1)
            pe.wait_ge(s["yb_ready"], 4)
            gemm("wo_ab", op_hi, op_lo, SEG_XC, ready=OP_DONE["l0"])
            sums_end("l1")
            gemm("q", op_hi, op_lo, SEG_X, ready=OP_DONE["y0"])
            gemm("kv", op_hi, op_lo, SEG_XC)
            gemm("gc", op_hi, op_lo, SEG_X)
            all_evacuated(pe, "kv")
            for t in range(SX // P):
                for k in range(2):
                    a = 4 * 512 + t * CTX + k * P
                    ins = nc.tensor.transpose(ps[:, a:a + P], kv_t[:, 2 + k, t * P:(t + 1) * P], ident[:, :])
            ins.then_inc(s["vtok_turned"], 1)
            pe.wait_ge(s["ada_acc"], ADA_RING + ADA_L0 + ADA_L1)
            for a in range(ADA_L1):
                for c_ in range(2):
                    ins = mm(bank(7)[:, 2 * a + c_:2 * a + c_ + 1], ada_acc1[:, a, c_, :], ones[:, 0:1], start=True,
                             stop=True)
            ins.then_inc(s["ada_sums"], 1)
            pe.wait_ge(s["vtok_ready"], 1)
            pe.wait_ge(s["gate1_ready"], 1)
            all_evacuated(pe, "gc")
            nu = len(UNITS)
            pe.sem_inc(s["att_out"], nu)
            with pe.Fori(0, 4) as i:
                pe.wait_ge(s["att_in"], i + 1)
                for u in range(nu + 3):
                    if u < nu:
                        c2, n, par = UNITS[u]
                        lo, nb = att_lat(n)
                        h = slice(HEAD * par, HEAD * par + HEAD)
                        sc = pair_ps[u % 2]
                        if u >= 2:
                            pe.wait_ge(s["exps"], 2 * nu * i + 2 * (u - 1))
                        q_u = q_st[h, c2, n * P:(n + 1) * P]
                        mm(sc[:, CTX:S], q_u, k_st[h, S:SX], start=True, stop=True)
                        mm(sc[:, S:S + nb * P], q_u, k_st[h, lo * P:(lo + nb) * P], start=True, stop=True)\
                            .then_inc(s["scores"], 1)
                    if 2 <= u < nu + 2:
                        nb = att_lat(UNITS[u - 2][1])[1] + CTX // P
                        pe.wait_ge(s["probs"], nu * i + u - 1)
                        if u >= 3:
                            pe.wait_ge(s["p_copied"], nu * i + u - 2)
                        for b in range(nb):
                            ins = nc.tensor.transpose(bank(0, 2)[:, b * P:(b + 1) * P],
                                                      p_sb[:, (u - 2) % ATT_BUFS, b * P:(b + 1) * P], ident[:, :])
                        ins.then_inc(s["p_turned"], 1)
                    if u >= 3:
                        c2, n, par = UNITS[u - 3]
                        lo, nb = att_lat(n)
                        pe.wait_ge(s["p_copied"], nu * i + u - 2)
                        o = bank(2 + c2)[HEAD * par:HEAD * par + HEAD, n * P:(n + 1) * P]
                        tiles = [S // P, S // P + 1] + list(range(lo, lo + nb))
                        for b, t in enumerate(tiles):
                            ins = mm(o, v_st[:, t, :], pT[:, (u - 3) % 2, b * P:(b + 1) * P], start=(b == 0),
                                     stop=(b == len(tiles) - 1))
                        ins.then_inc(s["att_out"], 1)
            pe.wait_ge(s["op_ready"], OP_DONE["y1"])
            gemm("wo_c", op_hi, op_lo, SEG_X)
            sums_end("final")
            pe.wait_ge(s["norm_done"], 8)
            sums_end("pre")
            gemm("xbc", xn_hi, xn_lo, SEG_2, ready=OP_DONE["y1"])
            gemm("dt", xn_hi, xn_lo, SEG_2)
            all_evacuated(pe, "dt")

            def slab_chunk(slot, k):
                products(gemm_ps[0], xn_hi, xn_lo, w_hi[:, slot, k:k + 1, :], w_lo[:, slot, k:k + 1, :], 1, k,
                         SEG_2, k == 0, k == KC - 1, k == KC - 1)

            g0z = SLAB0["z"]

            def z_chunks(t, j, k0, k1):
                for k in range(k0, k1):
                    if k == 0:
                        pe.wait_ge(s["split"], g0z + j + 1 + 2 * t)
                        pe.wait_ge(s["z_evac"], j + 1 + 2 * t)
                    slab_chunk((g0z + j) % 2, k)

            H = 16

            def chunk(t, with_z):
                pe.wait_ge(s["chunk_in"], 2 * t + 2)
                for k in range(KC):
                    nc.tensor.transpose(pair_ps[0][:, k * P:(k + 1) * P], xst[:, k, :], ident[:, :])
                for g in range(2):
                    nc.tensor.transpose(pair_ps[1][:, g * P:(g + 1) * P], xst[:, KC + g, :], ident[:, :])
                for g in range(2):
                    mm(pair_ps[1][:, S + P + g * P:S + 2 * P + g * P], xst[:, KC + g, :], xst[:, KC + 2 + g, :],
                       start=True, stop=True)
                nc.tensor.transpose(pair_ps[1][:, 2 * P:2 * P + H], dt_t[0:H, :], ident[0:H, 0:H])\
                    .then_inc(s["chunk_turned"], 1)
                if with_z:
                    z_chunks(t, 0, 0, 4)
                pe.wait_ge(s["chunk_scaled"], t + 1)
                mm(pair_ps[1][:, S:S + H], tri[:, :], adt[:, :], start=True, stop=True)
                mm(pair_ps[1][:, S + H:S + 2 * H], ones[:, :], adt[:, :], start=True, stop=True)
                for g in range(2):
                    if g:
                        pe.wait_ge(s["seg_sub"], 2 * t + 1)
                    for h in range(8):
                        ins = mm(bank(2, 2)[:, h * P:(h + 1) * P], adt[:, 8 * g + h:8 * g + h + 1].to_broadcast([P, P]),
                                 tri[:, :], start=True, stop=True)
                    ins.then_inc(s["chunk_acs"], 1)
                    if with_z:
                        z_chunks(t, g, 4 * (1 - g), KC)
                pe.wait_ge(s["ssd_operands"], t + 1)
                pe.wait_ge(s["chunk_b"], t + 1)
                for h in range(H):
                    o = pair_ps[0][HEAD * (h % 2):HEAD * (h % 2) + HEAD, (h // 2) * P:(h // 2 + 1) * P]
                    mm(o, xdt[:, h * HEAD:(h + 1) * HEAD], seg[:, h, :], start=True, stop=False)
                    ins = mm(o, prev[:, h * HEAD:(h + 1) * HEAD], cexp[:, h, :], start=False, stop=True)
                ins.then_inc(s["ssd_y"], 1)
                for g in range(2):
                    ins = mm(pair_ps[1][:, g * S:(g + 1) * S], b_tok[:, g * P:(g + 1) * P],
                             xdd[:, g * S:(g + 1) * S], start=True, stop=True)
                ins.then_inc(s["ssd_state"], 1)

            with pe.Fori(0, NT - 1) as t:
                chunk(t, True)
            chunk(NT - 1, False)
            g0 = SLAB0["sb"]

            def sb_chunk(i, g, k):
                if k == 0:
                    pe.wait_ge(s["split"], g0 + 3 + g + 1 + 6 * i)
                    if g % 3:
                        pe.wait_ge(s["sb_evac"], 3 + g + 6 * i)
                    else:
                        pe.wait_ge(s["sb_v"], 1 + g // 3 + 2 * i)
                slab_chunk((g0 + 3 + g) % 2, k)

            pe.wait_ge(s["ssd_used"], NT + 1)
            pe.wait_ge(s["z_evac"], KC + 1)
            for g in range(-3, 0):
                for k in range(KC):
                    if k == 0:
                        pe.wait_ge(s["split"], g0 + 3 + g + 1)
                        if g > -3:
                            pe.wait_ge(s["sb_evac"], 3 + g)
                    slab_chunk((g0 + 3 + g) % 2, k)
            sums_end("ssd")
            pe.wait_ge(s["rows_kept"], 1)

            def sb_iteration(i, last):
                chunk = 0
                for u in range(SBN + 2):
                    if u < SBN:
                        m, par, blk, nq, q0, nk, buf = sb_unit(u)
                        pe.wait_ge(s["sb_evac"], 3 * m + 2 + 6 * i)
                        if not SB_HELD[u]:
                            pe.wait_ge(s["sb_y"], 2 * NT * i + 1)
                        for w in SB_HELD[u]:
                            if sb_outputs(w):
                                pe.wait_ge(s["sb_y"], 2 * NT * i + sb_out(w) + 2)
                            else:
                                pe.wait_ge(s["sb_wc"], SBN * i + w + 1)
                        z_ps = sb_bank(u)
                        if blk == 0:
                            pe.sem_inc(s["pe_gate"], 1)
                            for half in range(2):
                                h = slice(HEAD * half, HEAD * half + HEAD)
                                ins = mm(z_ps[32 * half:32 * half + 32, 0:META], qs[h, m, 0:32],
                                         ks[h, m, 0:META], start=True, stop=True)
                        else:
                            h = slice(HEAD * par, HEAD * par + HEAD)
                            q_u = qs[h, m, q0:q0 + nq]
                            if SB_BANKS[u][1] == 1:
                                ins = mm(z_ps[:, 0:nk], q_u, ks[h, m, 0:nk], start=True, stop=True)
                            else:
                                mm(z_ps[:, S - META:S], q_u, ks[h, m, 0:META], start=True, stop=True)
                                ins = mm(z_ps[:, S:S + blk * P], q_u, ks[h, m, META:nk], start=True, stop=True)
                        ins.then_inc(s["sb_scores"], 1)
                    if u % len(SBU) == 0 and u < SBN:
                        m = u // len(SBU)
                        pe.wait_ge(s["sb_evac"], 3 * m + 3 + 6 * i)
                        for t in range(NT):
                            n, c0 = (META, 0) if t == 0 else (P, META + (t - 1) * P)
                            ins = nc.tensor.transpose(gemm_ps[0][0:n, t * P:(t + 1) * P], vs[:, m, c0:c0 + n],
                                                      ident[:, :])
                        ins.then_inc(s["sb_vt"], 1)
                    if u < 9 or not last:
                        for _ in range(SB_CHUNKS.get(u, 0)):
                            sb_chunk(i, chunk // KC, chunk % KC)
                            chunk += 1
                    if 1 <= u <= SBN:
                        m, par, blk, nq, q0, nk, buf = sb_unit(u - 1)
                        o = sb_bank(u - 1)
                        pe.wait_ge(s["sb_wr"], SBN * i + u)
                        if blk == 0:
                            pe.sem_inc(s["pe_gate"], 1)
                        for t in range(blk + 1):
                            n, c0 = (META, 0) if t == 0 else (P, META + (t - 1) * P)
                            at_ = sb_tile(u - 1, t)
                            ins = nc.tensor.transpose(o[0:n, at_:at_ + nq], sb_sum[0:nq, buf, c0:c0 + n],
                                                      ident[0:nq, 0:nq])
                        ins.then_inc(s["sb_wt"], 1)
                    if u >= 2 and sb_outputs(u - 2):
                        m, par, blk, nq, q0, nk, buf = sb_unit(u - 2)
                        o = sb_bank(u - 2)
                        pe.wait_ge(s["sb_wc"], SBN * i + u - 1)
                        if blk == 0:
                            pe.wait_ge(s["sb_v"], 2 * i + m + 1)
                            pe.sem_inc(s["pe_gate"], 1)
                        for half in range(2):
                            h = slice(HEAD * half, HEAD * half + HEAD)
                            if blk == 0:
                                ins = mm(o[h, 0:META], v_sb[0:META, m, 0, h],
                                         sb_wT[0:META, buf, 0, 32 * half:32 * half + META], start=True, stop=True)
                                continue
                            wb = (buf + half - 1) % SB_BUFS
                            for t in range(blk + 1):
                                n = META if t == 0 else P
                                ins = mm(o[h, 0:P], v_sb[0:n, m, t, h], sb_wT[0:n, wb, t, 0:nq],
                                         start=(t == 0), stop=(t == blk))
                        ins.then_inc(s["sb_o"], 1)

            with pe.Fori(0, SB_PAIRS // 2 - 1) as i:
                sb_iteration(i, False)
            sb_iteration(SB_PAIRS // 2 - 1, True)
            pe.wait_ge(s["sb_y"], SB_PAIRS * NT + 1)
            g0, b0 = SLAB0["wo_2"], BLOCK0["wo_2"]

            def half(i, h, jb, ready=None):
                b, j = b0 + jb, 2 * h + jb
                if h == 0:
                    pe.wait_ge(s_evac[b % 2], 1 + b // 2 + i)
                pe.wait_ge(s["split"], g0 + j + 1 + 4 * i)
                hi, lo = ((ys_hi, ys_lo), (xn_hi, xn_lo))[h]
                slot = (g0 + j) % 2
                products(gemm_ps[b % 2], hi, lo, w_hi[:, slot, :, :], w_lo[:, slot, :, :], KC, 0, SEG_2, h == 0, h == 1,
                         ready=ready)

            pe.wait_ge(s["op_ready"], OP_DONE["ssd"])
            half(0, 0, 0)
            half(0, 0, 1)
            sums_end("sbn")
            half(0, 1, 0, ready=OP_DONE["ssd"])
            half(0, 1, 1)
            with pe.Fori(1, KC // 2) as i:
                for j in range(4):
                    half(i, j // 2, j % 2)
            sums_end("post")
            gemm("up", u_hi, u_lo, SEG_2, ready=OP_DONE["sbn"], beside=lambda: sums_end("ffn"))
            gemm("down", f_hi, f_lo, SEG_2, ready=OP_DONE["ffn"], cuts=DOWN)
            sums_end("fin")
            pe.wait_ge(s["norm_done"], 24)
            for t in range(S // P):
                if t >= 2:
                    pe.wait_ge(s["out_ready"], t - 1)
                for k in range(KC):
                    ins = nc.tensor.transpose(gemm_ps[t % 2][:, k * P:(k + 1) * P],
                                              xT[:, k, META + t * P:META + (t + 1) * P], ident[:, :])
                ins.then_inc(s["out_turned"], 1)


INPUTS = ["x", "c", "ctx", "c_ctx", "norm_g", "ada_w", "ada_b", "w_in_ab", "v_norm_g", "spatial_w", "spatial_b",
          "w_out_ab", "w_in_c", "sink_logit", "w_out_c", "final_g", "meta_tokens_2", "mix_pre_g_2", "w_in_2",
          "ssd_conv_w_2", "ssd_conv_b_2", "ssd_dt_bias_2", "ssd_a_log_2", "ssd_d_2", "ssd_norm_g_2",
          "sb_norm_g_2", "w_out_2", "mix_post_g_2", "ffn_pre_g_2", "w_up_2", "ffn_conv_w_2", "ffn_conv_b_2",
          "w_down_2", "ffn_post_g_2"]
FLAT = {"c", "c_ctx", "norm_g", "ada_b", "v_norm_g", "spatial_b", "sink_logit", "final_g", "mix_pre_g_2",
        "ssd_conv_w_2", "ssd_conv_b_2", "ssd_dt_bias_2", "ssd_a_log_2", "ssd_d_2", "ssd_norm_g_2", "sb_norm_g_2",
        "mix_post_g_2", "ffn_pre_g_2", "ffn_conv_w_2", "ffn_conv_b_2", "ffn_post_g_2"}


def kernel(**inputs):
    import concourse.bacc as bacc
    from concourse.bass_utils import run_bass_kernel_spmd

    nc = bacc.Bacc("TRN2", target_bir_lowering=False, num_devices=1)
    nc, arrays = build(nc, inputs)
    r = run_bass_kernel_spmd(nc, [arrays], core_ids=[0])
    return r.results[0]["out_dram"].reshape(1, S, D)


def build(nc, inputs):
    arrays, args = {}, []
    for name in INPUTS:
        a = np.ascontiguousarray(inputs[name])
        if name in FLAT:
            a = a.reshape(-1)
        elif name not in ("ada_w", "meta_tokens_2"):
            a = a.reshape(a.shape[1:])
        arrays[f"in_{name}"] = a
        args.append(nc.dram_tensor(f"in_{name}", a.shape, F32, kind="ExternalInput").ap())
    arrays["consts"] = shape_constants()[0]
    args.append(nc.dram_tensor("consts", arrays["consts"].shape, F32, kind="ExternalInput").ap())
    args.append(nc.dram_tensor("out_dram", (S, D), F32, kind="ExternalOutput").ap())
    two_blocks(nc, *args)
    return nc, arrays
```

```python
from contextlib import ExitStack

import numpy as np

import concourse.bass as bass
from concourse import mybir

ALU = mybir.AluOpType
ACT = mybir.ActivationFunctionType
AX = mybir.AxisListType
F32 = mybir.dt.float32
F32R = mybir.dt.float32r

P = 128
D = 1024
KC = D // P
S = 512
CTX = 256
META = 16
SX = S + CTX
T2 = META + S
PAD = P - META
TP = PAD + T2
NT = TP // P
HALF = T2 // 2
GRID_W = 64
EPS = 1e-6
NEG = -1e30
FF = 2816
FC = FF // P
AB_IN = 2560
HEAD = 64
ATT_SCALE = HEAD ** -0.5
ROPE_BASE = 10000.0
XBC = 1536
XC = XBC // P
OFF_XBC, OFF_DT = 1024, 2560
OFF_Q, OFF_K, OFF_V = 2576, 3600, 4624
ADA_FIRST = 4
ADA_RING = 4
ADA_L0, ADA_L1 = 28, 4
ATT_BUFS = 4
SB_BUFS = 3
DOWN = [(0, 8), (8, 8), (16, 6)]

STREAM = [("uv", 8, 1), ("ga", 4, 1), ("xb", 4, 1), ("gb", 4, 1), ("wo_ab", 8, 1),
          ("q", 8, 1), ("kv", 4, 1), ("gc", 8, 1), ("wo_c", 8, 1),
          ("dt", 1, 1), ("xbc", 12, 1), ("z", 8, 1), ("sb", 24, 1),
          ("wo_2", 16, 2), ("up", 44, 1), ("down", 24, 3)]
SLAB0, BLOCK0, SLABS, PER = {}, {}, {}, {}
_g = _b = 0
for _name, _n, _per in STREAM:
    SLAB0[_name], BLOCK0[_name], SLABS[_name], PER[_name] = _g, _b, _n, _per
    _g += _n
    _b += 0 if _name in ("z", "sb") else _n // _per

VEC_A = {"norm_g": 0, "ada_b": 16, "c": 64, "c_ctx": 72, "final_g": 80, "mix_pre": 88,
         "ssd_norm": 96, "sb_norm": 104, "mix_post": 112}
VEC_B = {"conv_w": 0, "conv_b": 48, "ffn_b": 60, "ffn_pre": 82, "ffn_post": 90, "v_norm": 98}
COL = {**VEC_A, **{k: 128 + v for k, v in VEC_B.items()}, "ffn_w": 256}
VEC_ROWS = (120, 102, 66)

OP_DONE = {"l0": 8, "y0": 16, "l1": 24, "y1": 32, "pre": 40, "ssd": 48, "sbn": 56, "ffn": 64}


class Steps:

    def __init__(self, eng, sem):
        self.eng, self.sem, self.n, self.i, self.per = eng, sem, 0, None, 0

    def __call__(self, ins):
        self.n += 1
        ins.then_inc(self.sem, 1)

    def wait(self, but=0):
        n = self.n - but
        self.eng.wait_ge(self.sem, n if self.i is None else n + self.i * self.per)

    def begin(self, i, per):
        self.i, self.per, self.at = i, per, self.n

    def end(self, count):
        assert self.n - self.at == self.per, (self.n - self.at, self.per)
        self.n = self.at + count * self.per
        self.i = None


def shape_constants():
    r = np.arange(P)
    ident = np.eye(P)
    tri = (r[:, None] <= r[None, :]) * 1.0
    at_or_after = np.where(r[None, :] >= r[:, None], 0.0, NEG)
    at_or_before = np.where(r[None, :] <= r[:, None], 0.0, NEG)
    before = np.where(r[None, :] < r[:, None], 0.0, NEG)
    before_meta = np.where(r[None, :META] < r[:, None] % 32, 0.0, NEG)
    t = np.arange(S)
    d = r % HEAD
    nf = HEAD // 4
    inv = np.float32(ROPE_BASE) ** (-np.arange(nf, dtype=np.float32) / np.float32(nf))
    place = np.where((d // 32)[:, None] == 0, (t // GRID_W)[None, :], (t % GRID_W)[None, :]).astype(np.float32)
    ang = (place * inv[d % nf][:, None].astype(np.float32)).astype(np.float64)
    sign = np.where(d % 32 < nf, -1.0, 1.0)[:, None]
    a = 2 * np.pi * np.outer(r, r) / P
    b = 2 * np.pi * (np.outer(t, t) % S) / S
    seq = np.stack([np.cos(b), -np.sin(b)], 1) / np.sqrt(S)
    seq = seq.reshape(S // P, P, 2, S).transpose(1, 0, 2, 3).reshape(P, -1)
    parts = {"ident": ident, "tri": tri, "at_or_after": at_or_after, "at_or_before": at_or_before,
             "before": before, "before_meta": before_meta, "cos": np.cos(ang), "sin": np.sin(ang) * sign,
             "dft_ch": np.concatenate([np.cos(a), np.sin(a)], 1) / np.sqrt(P), "dft_seq": seq}
    first, n = {}, 0
    for name, v in parts.items():
        first[name] = n
        n += v.shape[1]
    return np.ascontiguousarray(np.concatenate(list(parts.values()), 1).astype(np.float32)), first


CONST_FIRST = shape_constants()[1]


def two_blocks(nc, x, c, ctx, c_ctx, norm_g, ada_w, ada_b, w_in_ab, v_norm_g, spatial_w, spatial_b,
               w_out_ab, w_in_c, sink_logit, w_out_c, final_g, meta_tokens_2, mix_pre_g_2, w_in_2,
               ssd_conv_w_2, ssd_conv_b_2, ssd_dt_bias_2, ssd_a_log_2, ssd_d_2, ssd_norm_g_2, sb_norm_g_2,
               w_out_2, mix_post_g_2, ffn_pre_g_2, w_up_2, ffn_conv_w_2, ffn_conv_b_2, w_down_2,
               ffn_post_g_2, consts, out):
    stack = ExitStack()
    with stack:
        cursor = [(nc.sbuf_base + 63) // 64 * 64]

        def at(name, shape, offset, dt=F32):
            return nc.alloc_sbuf_tensor_at(name, shape, dt, offset=offset)

        def size(shape):
            return (int(np.prod(shape[1:])) * 4 + 31) // 32 * 32

        def sb(name, shape, dt=F32):
            t = at(name, shape, cursor[0], dt)
            cursor[0] += size(shape)
            return t

        raw = sb("raw", [P, 2, KC, P])
        w_hi = sb("w_hi", [P, 2, KC, P], F32R)
        w_lo = sb("w_lo", [P, 2, KC, P], F32R)
        xT = sb("xT", [P, KC, T2])
        cols = sb("cols", [P, 3, P])
        mod = sb("mod", [P, 48, 2])
        modg = sb("modg", [P, 2, 2, KC])
        ident = sb("ident", [P, P])
        tri = sb("tri", [P, P])
        at_or_after = sb("at_or_after", [P, P])
        at_or_before = sb("at_or_before", [P, P])
        before = sb("before", [P, P])
        before_meta = sb("before_meta", [P, META])
        ones = sb("ones", [P, P])
        zeros = sb("zeros", [P, P])
        eps = sb("eps", [P, 8])
        stat = sb("stat", [P, 8])
        rstd = sb("rstd", [P, 8])
        cond = sb("cond", [P, KC, 2])
        bn = sb("bn", [P, 8])
        mv = sb("mv", [P, 8])
        sink = sb("sink", [P, 16])
        neg_sink = sb("neg_sink", [P, 16])
        neg_a = sb("neg_a", [P, 16])
        a_log = sb("a_log", [P, 16])
        skip = sb("skip", [P, KC])
        dt_bias = sb("dt_bias", [P, 8])
        sm = sb("sm", [P, ATT_BUFS, 8])
        stage0 = cursor[0]

        def plan(*items, start=None):
            at_ = stage0 if start is None else start
            made = []
            for name, shape, *dt in items:
                made.append(at(name, shape, at_, *dt))
                at_ += size(shape)
            assert at_ <= nc.sbuf_usable_end, (items[-1][0], at_, nc.sbuf_usable_end)
            return made

        ctxT, op_hi, op_lo = plan(("ctxT", [P, KC, CTX]), ("op_hi", [P, KC, SX], F32R),
                                  ("op_lo", [P, KC, SX], F32R))
        layer0 = stage0 + size([P, KC, CTX]) + 2 * size([P, KC, SX])
        zT, dft_ch, dft_seq, sw, swT, s_bias, vt, pq = plan(
            ("zT", [P, 20, SX]), ("dft_ch", [P, 2 * P]), ("dft_seq", [P, S // P, 2, S]),
            ("sw", [P, 4, P]), ("swT", [P, 4, P]), ("s_bias", [P, 4, P]),
            ("vt", [P, SX // P, S]), ("pq", [P, SX // P, 2 * P]), start=layer0)
        x_in, ctx_in, meta_in, vec_in = plan(
            ("x_in", [P, S // P, D]), ("ctx_in", [P, CTX // P, D]), ("meta_in", [META, D]),
            ("vec_in", [P, 3, P]), start=layer0)
        ada_first, m_rows, sq0, hp0 = plan(
            ("ada_first", [P, ADA_FIRST - 1, KC, 4 * P]), ("m_rows", [2, ADA_FIRST * 4 * P]), ("sq0", [P, 3, SX]),
            ("hp0", [P, 3, SX]),
            start=layer0 + sum(size(s) for s in ([P, S // P, D], [P, CTX // P, D], [META, D], [P, 3, P])))
        ada_ring, = plan(("ada_ring", [P, ADA_RING, KC, P]), start=layer0 + size([P, 20, SX]))
        ada_acc, = plan(("ada_acc", [P, ADA_L0, 2, P]), start=(nc.sbuf_usable_end - size([P, ADA_L0, 2, P])) // 32 * 32)
        tail0 = layer0 + sum(size(s) for s in ([P, 20, SX], [P, 2 * P], [P, S // P, 2, S], [P, 4, P],
                                               [P, 4, P], [P, 4, P]))
        gmlp, = plan(("gmlp", [P, SX]), start=tail0 + size([P, SX // P, S]) + size([P, SX // P, 2 * P]))
        att_plan = (
            ("q_t", [P, KC, S]), ("kv_t", [P, 4, SX]), ("g_t", [P, KC, S]), ("k_st", [P, 2, 2, SX], F32R),
            ("v_tok", [P, SX // P, CTX]), ("cos", [P, S]), ("sin", [P, S]), ("q_st", [P, 2, 4, S], F32R),
            ("rot", [P, 2, S]), ("v_st", [P, 2, SX // P, HEAD]), ("p_sb", [P, ATT_BUFS, 640]), ("pT", [P, 2, 640]))
        q_t, kv_t, g_t, k_st, v_tok, cos, sin, q_st, rot, v_st, p_sb, pT = plan(*att_plan, start=layer0)
        masks, ident_r = plan(("masks", [P, 2, P], F32R), ("ident_r", [P, P], F32R),
                              start=layer0 + sum(size(item[1]) for item in att_plan[:8]))
        ada_ring1, = plan(("ada_ring1", [P, ADA_RING, KC, P]),
                          start=layer0 + sum(size(item[1]) for item in att_plan[:7]))
        ada_acc1, = plan(("ada_acc1", [P, ADA_L1, 2, P]), start=layer0 + sum(size(item[1]) for item in att_plan[:11]))
        sq1, hp1 = plan(("sq1", [P, 3, SX]), ("hp1", [P, 3, SX]),
                        start=layer0 + 2 * size([P, KC, S]) + size([P, 4, SX]))
        xn_hi, xn_lo, zs, xbc = plan(("xn_hi", [P, KC, T2], F32R), ("xn_lo", [P, KC, T2], F32R),
                                     ("zs", [P, KC, TP]), ("xbc", [P, XC + 1, TP]))
        ys_hi, ys_lo = plan(("ys_hi", [P, KC, T2], F32R), ("ys_lo", [P, KC, T2], F32R),
                            start=stage0 + 2 * size([P, KC, T2]) + size([P, KC, TP]))
        mixer = stage0 + 4 * size([P, KC, T2]) + size([P, KC, TP])
        assert size([P, XC + 1, TP]) <= 2 * size([P, KC, T2])
        ssd_plan = (
            ("xst", [P, XC, P]), ("b_tok", [P, 2, 2 * P]), ("xdt", [P, D]), ("xdd", [P, D]),
            ("seg", [P, 16, P]), ("cexp", [P, 16, P]), ("prev", [P, D]),
            ("dt_t", [P, P]), ("dt_k", [P, 16]), ("adt", [P, 16]), ("acs", [P, 32]), ("dec", [P, 32]), ("cb", [P, 2, P]))
        xst, b_tok, xdt, xdd, seg, cexp, prev, dt_t, dt_k, adt, acs, dec, cb = plan(*ssd_plan, start=mixer)
        ssd_odd = mixer + sum(size(shape) for _, shape in ssd_plan)
        xst_odd, xdt_odd = plan(("xst_odd", [P, XC, P]), ("xdt_odd", [P, D]), start=ssd_odd)
        conv, dtm, ysb, hp_ssd, rstd_ssd = plan(
            ("conv", [P, 2, T2]), ("dtm", [P, 3, T2]), ("ysb", [P, KC, T2]), ("hp_ssd", [P, 2, T2]),
            ("rstd_ssd", [P, T2]), start=ssd_odd)
        assert size([P, XC, P]) + size([P, D]) <= size([P, 2, T2]) + size([P, 3, T2])
        xst, xdt = (xst, xst_odd), (xdt, xdt_odd)
        qs, ks = plan(("qs", [P, 2, T2]), ("ks", [P, 2, T2]), start=ssd_odd)
        vs, = plan(("vs", [P, 2, T2]), start=ssd_odd + sum(
            size(shape) for shape in ([P, 2, T2], [P, 3, T2], [P, KC, T2], [P, 2, T2], [P, T2])))
        v_sb, sb_relu, sb_neg, sb_sum, sb_wT = plan(
            ("v_sb", [P, 2, NT, P]), ("sb_relu", [P, SB_BUFS, T2]), ("sb_neg", [P, SB_BUFS, T2]),
            ("sb_sum", [P, SB_BUFS, T2]), ("sb_wT", [P, SB_BUFS, NT, P]), start=mixer)
        mixT, sq2, hp2 = plan(("mixT", [P, KC, T2]), ("sq2", [P, 3, T2]), ("hp2", [P, 3, T2]), start=mixer)
        u_hi, u_lo, f_hi, f_lo, gp, gacc, fgl, fT = plan(
            ("u_hi", [P, KC, T2], F32R), ("u_lo", [P, KC, T2], F32R), ("f_hi", [P, FC, T2], F32R),
            ("f_lo", [P, FC, T2], F32R), ("gp", [P, T2 + 8]), ("gacc", [P, T2]), ("fgl", [P, T2]),
            ("fT", [P, KC, T2]))
        ffn_tail = stage0 + 2 * size([P, FC, T2]) + 2 * size([P, KC, T2]) + size([P, T2 + 8]) + 2 * size([P, T2])
        sq3, hp3 = plan(("sq3", [P, 3, T2]), ("hp3", [P, 3, T2]), start=ffn_tail)
        rstd_ffn, = plan(("rstd_ffn", [P, T2]), start=ffn_tail + size([P, KC, T2]))
        sq4, hp4 = plan(("sq4", [P, 3, T2]), ("hp4", [P, 3, T2]), start=stage0 + size([P, S // P, D]))
        y_out, = plan(("y_out", [P, S // P, D]), start=stage0)

        ps = stack.enter_context(nc.psum_tensor("ps", [P, 8 * 512], F32))

        def bank(b, n=1):
            return ps[:, 512 * b:512 * (b + n)]

        gemm_ps = [bank(0, 2), bank(2, 2)]
        pair_ps = [bank(4, 2), bank(6, 2)]

        def sem(name):
            return stack.enter_context(nc.semaphore(name))

        names = """vec_in x_in consts_in small_in dft_in vec_turned cols_ready cond_ready x_turned x_ready
            vec2_in ada_rows rows_taken rows_turned ada1_in ada_acc ada_sums mod_ready mod1_ready gate1_ready fill_ready raw0 raw1 split slab_done evac0 evac1 slab_taken
            sq sq_used ssq std rstd rstd_rows hp op_hi op_ready norm_done
            v_turned v_stat v_std v_ready sw_turned sw_ready spatial ya_ready ch_dft pq_ready seq_dft yb_ready
            rope_ready vtok_turned vtok_ready att_in scores nmax exps probs p_turned p_copied att_out att_o
            conv_in conv_done dt_e dt_l dt_ready chunk_in chunk_turned chunk_sums chunk_scaled chunk_b chunk_acs dec_in dec_ready
            chunk_e seg_ready seg_e ssd_operands ssd_y ssd_state ssd_used
            z_evac seg_sub z_silu gated rows_kept sb_evac sb_vt sb_v sb_scores sb_in sb_l sb_d sb_wr sb_wt sb_wc sb_o sb_y
            normed gate_conv gelu ffn_f ffn_hi out_turned out_ready out_ready_act stored
            pe_gate act_gate act_steps dve_steps pool_steps""".split()
        s = {n: sem("s_" + n) for n in names}
        s_ada_first = [sem(f"s_ada_first{j}") for j in range(ADA_FIRST)]
        s_ada_in = [sem(f"s_ada_in{j}") for j in range(ADA_RING)]
        s_raw = [s["raw0"], s["raw1"]]
        s_evac = [s["evac0"], s["evac1"]]

        SMALL = 16 * 5

        def col(name, k, n=1):
            i = COL[name] + k
            return cols[:, i // P, i % P:i % P + n]

        def ada_rows_at(j):
            return bank(7 if j % 2 == 0 else 3)[0:2, :]

        def block_done(name, n):
            return SLAB0[name] + n * PER[name]

        def all_evacuated(eng, name):
            last = BLOCK0[name] + SLABS[name] // PER[name]
            eng.wait_ge(s_evac[0], 1 + (last + 1) // 2)
            eng.wait_ge(s_evac[1], 1 + last // 2)

        def seg2(ap):
            return ap.rearrange("p (h n) -> p h n", h=2)[:, :, 0:HALF]

        def two(ap):
            return ap.rearrange("p (h n) -> p h n", h=2)

        SEG_X = [(0, S)]
        SEG_XC = [(0, S), (S, CTX)]
        SEG_2 = [(0, HALF), (HALF, HALF)]
        TILES_XC = [(t * P, P) for t in range(SX // P)]
        TILES_X = TILES_XC[:S // P]
        TILES_2 = [(0, META)] + [(META + t * P, P) for t in range(S // P)]

        def lat(k):
            return xT[:, k, META:T2]

        NORMS = {
            "l0": (0, TILES_XC, 0, sq0, hp0), "l1": (1, TILES_XC, 0, sq1, hp1),
            "final": (2, TILES_X, 0, sq1, hp1), "pre": (3, TILES_2, PAD, sq2, hp2),
            "ssd": (4, TILES_2, PAD, sq2, hp2), "sbn": (5, TILES_2, PAD, sq2, hp2),
            "post": (6, TILES_2, PAD, sq2, hp2), "ffn": (7, TILES_2, PAD, sq3, hp3),
            "fin": (8, TILES_2, PAD, sq4, hp4)}
        HP0 = {"l0": 0, "l1": 8, "pre": 16, "ssd": 24, "sbn": 32, "ffn": 40}

        def norm_sources(name, k):
            if name in ("l0", "l1"):
                layer = int(name[1])
                return [(lat(k), 0, S, modg[:, layer, 0, k:k + 1], mod[:, 24 * layer + k, 0:1]),
                        (ctxT[:, k, :], S, CTX, modg[:, layer, 1, k:k + 1], mod[:, 24 * layer + k, 1:2])]
            if name == "final":
                return [(lat(k), 0, S, col("final_g", k), None)]
            src, gain = {"pre": (xT[:, k, :], "mix_pre"), "ssd": (zs[:, k, PAD:TP], "ssd_norm"),
                         "sbn": (ysb[:, k, :], "sb_norm"), "post": (mixT[:, k, :], "mix_post"),
                         "ffn": (xT[:, k, :], "ffn_pre"), "fin": (fT[:, k, :], "ffn_post")}[name]
            return [(src, 0, T2, col(gain, k), None)]

        OPERAND = {"l0": (op_hi, op_lo, 0), "l1": (op_hi, op_lo, 0), "pre": (xn_hi, xn_lo, 0),
                   "ssd": (ys_hi, ys_lo, 0), "sbn": (xn_hi, xn_lo, 0), "ffn": (u_hi, u_lo, 0)}

        def rstd_rows(name, c0, n):
            base = NORMS[name][2]
            return pair_ps[0][:, base + c0:base + c0 + n]

        def y0_chunk(k):
            return zT[:, k if k < 4 else 8 + k, :]

        def att_lat(n):
            lo, hi = max(n - 1, 0), min(n + 1, S // P - 1)
            return lo, hi - lo + 1

        UNITS = [(j, c2, n, par) for j in range(2) for c2 in range(2) for n in range(S // P) for par in range(2)]
        SBU = [(0, 0)] + [(par, blk) for blk in range(1, NT) for par in range(2)]
        SBN = 2 * len(SBU)
        SB_PAIRS = 8
        SB_SKEW = 3

        def sb_unit(u):
            m, v = divmod(u, len(SBU))
            par, blk = SBU[v]
            if blk == 0:
                return m, par, blk, 2 * 32, 0, META, u % SB_BUFS
            return m, par, blk, P, META + (blk - 1) * P, META + blk * P, u % SB_BUFS

        def sb_out(u):
            m, v = divmod(u, len(SBU))
            return NT * m + (v + 1) // 2

        def sb_outputs(u):
            return u % len(SBU) % 2 == 0

        SB_CHUNKS = {0: 4, 2: 3, 3: 3, 4: 2, 5: 3, 6: 3, 7: 2, 8: 4, 9: 4,
                     11: 3, 12: 3, 13: 2, 14: 3, 15: 3, 16: 2, 17: 4}
        SB_TAKE = {0: (0, 2, -1), 4: (1, 0, 0), 7: (1, 1, 1), 9: (1, 2, 2), 13: (0, 0, 3), 16: (0, 1, 4)}

        SB_NORM = [6, 15]

        SB_GAPS = (12, 14)
        SB_BANKS, SB_HELD = [], [[] for _ in range(SBN)]
        _turn, _holder = 0, {}
        for _u in range(2 * SBN):
            _n = 1 if sb_unit(_u)[5] <= 512 else 2
            _turn += _u % SBN in SB_GAPS
            assert _turn % 6 + _n <= 6
            SB_BANKS.append((2 + _turn % 6, _n))
            _held = [(_turn + _j) % 6 for _j in range(_n)]
            SB_HELD[_u % SBN] = sorted({_holder[_j] - _u // SBN * SBN for _j in _held if _j in _holder})
            _holder.update({_j: _u for _j in _held})
            _turn += _n
        assert _turn % 6 == 0

        def sb_bank(u):
            return bank(*SB_BANKS[u % SBN])

        def sb_key0(u):
            return S - META if SB_BANKS[u % SBN][1] == 2 else 0

        def sb_tile(u, t):
            return t * P if t == 0 or SB_BANKS[u % SBN][1] == 1 else S + (t - 1) * P

        def sb_live(i, u):
            return u < SBN and not (u < 0 and isinstance(i, int) and i == 0)

        def sb_wait(eng, what, per, i, n):
            if not isinstance(i, int) or per * i + n > 0:
                eng.wait_ge(s[what], n + per * i)

        def sb_scored(u, last):
            return u < SBN or u == SBN and not last

        def sb_steps(last):
            return SBN + (SB_SKEW if last else 0)

        block = stack.enter_context(nc.Block())

        @block.sync
        def _(sp):
            for tile, rows in ((0, [(norm_g, "norm_g"), (ada_b, "ada_b"), (c, "c"), (c_ctx, "c_ctx"),
                                    (final_g, "final_g"), (mix_pre_g_2, "mix_pre"), (ssd_norm_g_2, "ssd_norm"),
                                    (sb_norm_g_2, "sb_norm"), (mix_post_g_2, "mix_post")]),
                               (1, [(ssd_conv_w_2, "conv_w"), (ssd_conv_b_2, "conv_b"), (ffn_conv_b_2, "ffn_b"),
                                    (ffn_pre_g_2, "ffn_pre"), (ffn_post_g_2, "ffn_post"), (v_norm_g, "v_norm")]),
                               (2, [(ffn_conv_w_2, "ffn_w")])):
                if tile == 1:
                    sp.dma_start(ident[:, :], consts[:, 0:P]).then_inc(s["consts_in"], 16)
                    ada0 = ada_w[0].rearrange("(k p) n -> p k n", p=P)

                    def ada_slab(j):
                        sp.dma_start(ada_first[:, j % 3, :, :], ada0[:, :, j * 4 * P:(j + 1) * 4 * P])\
                          .then_inc(s_ada_first[j], 16)

                    ada_slab(0)
                    sp.dma_start(x_in[:, :, :], x.rearrange("(t p) d -> p t d", p=P)).then_inc(s["x_in"], 16)
                    sp.dma_start(ctx_in[:, :, :], ctx.rearrange("(t p) d -> p t d", p=P)).then_inc(s["x_in"], 16)
                    sp.dma_start(meta_in[:, :], meta_tokens_2).then_inc(s["x_in"], 16)
                    ada_slab(1)
                    ada_slab(2)
                    sp.wait_ge(s["ada_rows"], 1)
                    ada_slab(3)
                for src, name in rows:
                    n = src.shape[0] // P
                    r = COL[name] - P * tile
                    flat = src.rearrange("(k p) -> k p", p=P)
                    sp.dma_start(vec_in[r:r + n, tile, :], flat).then_inc(s["vec2_in" if tile else "vec_in"], 16)
            for name, dst in (("tri", tri), ("at_or_after", at_or_after),
                              ("at_or_before", at_or_before), ("before", before), ("before_meta", before_meta)):
                f = CONST_FIRST[name]
                sp.dma_start(dst[:, :], consts[:, f:f + dst.shape[1]]).then_inc(s["consts_in"], 16)
            sp.dma_start(sink[:, :], sink_logit.partition_broadcast(P)).then_inc(s["small_in"], 16)
            sp.dma_start(a_log[:, :], ssd_a_log_2.partition_broadcast(P)).then_inc(s["small_in"], 16)
            sp.dma_start(dt_bias[0:16, 0:1], ssd_dt_bias_2.rearrange("(h o) -> h o", o=1),
                         allow_slow_non_contiguous=True).then_inc(s["small_in"], 16)
            d_by_half = ssd_d_2.rearrange("(k h) -> h k", h=2)
            for h in range(2):
                sp.dma_start(skip[HEAD * h:HEAD * h + HEAD, :], d_by_half[h].partition_broadcast(HEAD),
                             allow_slow_non_contiguous=True).then_inc(s["consts_in"], 16)

            def cols_of(w):
                return w.rearrange("(k p) n -> p k n", p=P)

            def stream(name, src, begin=0, end=None, beside=None):
                u = 2 if SLABS[name] % 2 == 0 else 1
                g0 = SLAB0[name]

                def load(i, j):
                    if not (isinstance(i, int) and g0 + j + u * i < 2):
                        sp.wait_ge(s["split"], g0 + j - 1 + u * i)
                    sp.dma_start(raw[:, (g0 + j) % 2, :, :], src(i, j)).then_inc(s_raw[(g0 + j) % 2], 16)

                def step(i):
                    for j in range(u):
                        load(i, j)
                    if beside:
                        beside(i)

                end = SLABS[name] // u if end is None else end
                if end - begin == 1:
                    step(begin)
                    return
                with sp.Fori(begin, end) as i:
                    step(i)

            def plain(w, c0):
                return lambda i, j: cols_of(w)[:, :, bass.ds(i * 2 * P + (j * P + c0), P)]

            def ada_beside(layer, c0, it0, ring, dma_sems):
                w = ada_w[layer].rearrange("(k p) n -> p k n", p=P)

                def load(i):
                    for j in range(ADA_RING):
                        sp.wait_ge(s["ada_acc"], ADA_RING * it0 + j + 1 + ADA_RING * i)
                        sp.dma_start(ring[:, j, :, :], w[:, :, bass.ds(i * ADA_RING * P + (c0 + j * P), P)])\
                          .then_inc(dma_sems[j], 16)

                return load

            stream("uv", plain(w_in_ab, 0), 0, 1)
            sp.wait_ge(s["mod_ready"], 1)
            stream("uv", plain(w_in_ab, 0), 1, 3, ada_beside(0, 2 * D - ADA_RING * P, -1, ada_ring, s_ada_in))
            stream("uv", plain(w_in_ab, 0), 3, 4, ada_beside(1, -3 * ADA_RING * P, -1, ada_ring, s_ada_in))
            stream("ga", plain(w_in_ab, 1024), beside=ada_beside(1, ADA_RING * P, 3, ada_ring, s_ada_in))
            stream("xb", plain(w_in_ab, 1536), beside=ada_beside(1, 3 * ADA_RING * P, 5, ada_ring, s_ada_in))
            stream("gb", plain(w_in_ab, 2048))
            sp.wait_ge(s["ada_acc"], ADA_RING + ADA_L0)
            f = CONST_FIRST["dft_ch"]
            sp.dma_start(dft_ch[:, :], consts[:, f:f + 2 * P]).then_inc(s["dft_in"], 16)
            f = CONST_FIRST["dft_seq"]
            sp.dma_start(dft_seq[:, :, :, :].rearrange("p a b n -> p (a b n)"),
                         consts[:, f:f + 2 * S * S // P]).then_inc(s["dft_in"], 16)
            sp.wait_ge(s["ada_sums"], 1)
            sp.dma_start(sw[:, :, :], spatial_w.rearrange("h q p -> q h p")).then_inc(s["small_in"], 16)
            sp.dma_start(s_bias[:, :, :], spatial_b.partition_broadcast(P)).then_inc(s["small_in"], 16)
            stream("wo_ab", plain(w_out_ab, 0))
            def second_layer(i):
                sp.wait_ge(s["op_ready"], OP_DONE["l1"])
                w = ada_w[1].rearrange("(k p) n -> p k n", p=P)
                sp.dma_start(ada_ring1[:, bass.ds(i, 1), :, :].rearrange("p a k n -> p (a k) n"),
                             w[:, :, bass.ds(i * P + (ADA_L0 - KC) * P, P)]).then_inc(s["ada1_in"], 16)

            stream("q", plain(w_in_c, 0), beside=second_layer)
            for name, dst in (("cos", cos), ("sin", sin)):
                f = CONST_FIRST[name]
                sp.dma_start(dst[:, :], consts[:, f:f + S]).then_inc(s["consts_in"], 16)
            stream("kv", plain(w_in_c, 1024))
            stream("gc", plain(w_in_c, 1536))
            stream("wo_c", plain(w_out_c, 0))
            stream("dt", lambda i, j: cols_of(w_in_2)[:, :, OFF_DT:OFF_DT + P])
            stream("xbc", plain(w_in_2, OFF_XBC))
            stream("z", plain(w_in_2, 0))
            g0 = SLAB0["sb"]
            with sp.Fori(0, 4) as i:
                for j in range(6):
                    sp.wait_ge(s["split"], g0 + j - 1 + 6 * i)
                    c0 = (OFF_Q, OFF_K, OFF_V)[j % 3] + (j // 3) * P
                    sp.dma_start(raw[:, (g0 + j) % 2, :, :], cols_of(w_in_2)[:, :, bass.ds(i * 2 * P + c0, P)])\
                      .then_inc(s_raw[(g0 + j) % 2], 16)
            wo2 = w_out_2.rearrange("(h k p) n -> p h k n", h=2, p=P)
            g0 = SLAB0["wo_2"]
            with sp.Fori(0, KC // 2) as i:
                for j in range(4):
                    sp.wait_ge(s["split"], g0 + j - 1 + 4 * i)
                    sp.dma_start(raw[:, (g0 + j) % 2, :, :], wo2[:, j // 2, :, bass.ds(i * 2 * P + j % 2 * P, P)])\
                      .then_inc(s_raw[(g0 + j) % 2], 16)
            g0 = SLAB0["up"]
            with sp.Fori(0, FC) as i:
                for h in range(2):
                    sp.wait_ge(s["split"], g0 + h - 1 + 2 * i)
                    sp.dma_start(raw[:, (g0 + h) % 2, :, :], cols_of(w_up_2)[:, :, bass.ds(i * P + h * FF, P)])\
                      .then_inc(s_raw[(g0 + h) % 2], 16)
            wd = w_down_2.rearrange("(k p) n -> p k n", p=P)
            g0 = SLAB0["down"]
            with sp.Fori(0, KC // 2) as i:
                for j in range(2 * len(DOWN)):
                    k0, n = DOWN[j % len(DOWN)]
                    sp.wait_ge(s["split"], g0 + j - 1 + 2 * len(DOWN) * i)
                    sp.dma_start(raw[:, (g0 + j) % 2, 0:n, :],
                                 wd[:, k0:k0 + n, bass.ds(i * 2 * P + j // len(DOWN) * P, P)])\
                      .then_inc(s_raw[(g0 + j) % 2], 16)
            for t in range(S // P):
                sp.wait_ge(s[("out_ready", "out_ready_act")[t % 2]], t // 2 + 1)
                sp.dma_start(out[t * P:(t + 1) * P, :], y_out[:, t, :]).then_inc(s["stored"], 16)
            sp.wait_ge(s["stored"], 16 * (S // P))

        @block.gpsimd
        def _(pool):
            steps = Steps(pool, s["pool_steps"])
            nc.gpsimd.memset(ones[:, :], 1.0).then_inc(s["fill_ready"], 1)
            nc.gpsimd.memset(zeros[:, :], 0.0).then_inc(s["fill_ready"], 1)
            nc.gpsimd.memset(eps[:, :], EPS).then_inc(s["fill_ready"], 1)

            def split(r, hi, lo):
                pool.sem_inc(s["slab_taken"], 1)
                steps(nc.gpsimd.tensor_scalar(hi, r, 1.0, 0.0, ALU.mult, ALU.add))
                steps.wait()
                nc.gpsimd.tensor_tensor(lo, r, hi.bitcast(F32), ALU.subtract).then_inc(s["split"], 1)

            def slab(i, j, before_it):
                pool.wait_ge(s_raw[j], 16 * i + 16)
                if before_it:
                    pool.wait_ge(s["slab_done"], 2 * i + j - 1)
                split(raw[:, j, :, :], w_hi[:, j, :, :], w_lo[:, j, :, :])

            def slab_pairs(begin, end):
                with pool.Fori(begin, end) as i:
                    steps.begin(i - begin, 2)
                    for j in range(2):
                        slab(i, j, True)
                    steps.end(end - begin)

            def staged(ins):
                steps(ins)
                steps.wait()

            def halves_of(r, hi, lo):
                staged(nc.gpsimd.tensor_scalar(hi, r, 1.0, 0.0, ALU.mult, ALU.add))
                staged(nc.gpsimd.tensor_tensor(lo, r, hi.bitcast(F32), ALU.subtract))

            for j in range(2):
                slab(0, j, False)
            slab_pairs(1, SLAB0["wo_c"] // 2)
            pool.wait_ge(s["rope_ready"], 1)
            pool.wait_ge(s["consts_in"], 16 * 10)
            for r, copy in ((at_or_after, masks[:, 0, :]), (at_or_before, masks[:, 1, :]), (ident, ident_r[:, :])):
                staged(nc.gpsimd.tensor_scalar(copy, r[:, :], 1.0, 0.0, ALU.mult, ALU.add))
            for g in range(4):
                pool.wait_ge(s["att_out"], len(UNITS) // 2 * (g + 1))
                j = g % 2
                a, b = slice(HEAD * j, HEAD * j + HEAD), slice(HEAD * (1 - j), HEAD * (2 - j))
                halves_of(kv_t[a, g // 2, :], k_st[a, j, 0, :], k_st[a, j, 1, :])
                for part in range(2):
                    staged(nc.gpsimd.tensor_copy(k_st[b, j, part, :], k_st[a, j, part, :]))
                for c2 in range(2):
                    for par in range(2):
                        a, b = slice(HEAD * par, HEAD * par + HEAD), slice(HEAD * (1 - par), HEAD * (2 - par))
                        h = 2 * c2 + par
                        halves_of(q_t[a, 2 * g + c2, :], q_st[a, j, h, :], q_st[b, j, h, :])
                    pool.sem_inc(s["att_in"], 1)
                    if c2 == 0:
                        pool.wait_ge(s["vtok_ready"], 1)
                        staged(nc.gpsimd.tensor_copy(v_st[:, j, :, :], v_tok[:, :, HEAD * g:HEAD * g + HEAD]))
                        pool.sem_inc(s["att_in"], 1)
            last = SLAB0["down"] + SLABS["down"]
            slab_pairs(SLAB0["wo_c"] // 2, last // 2)
            if last % 2:
                slab(last // 2, 0, True)

        @block.scalar
        def _(act):
            steps = Steps(act, s["act_steps"])

            def norm_std(name):
                k0, tiles, _, _, _ = NORMS[name]
                act.wait_ge(s["ssq"], k0 + 1)
                nc.scalar.activation(stat[:, 0:len(tiles)], pair_ps[1][:, 0:len(tiles)], ACT.Sqrt,
                                     bias=eps[:, 0:1], scale=1.0 / D).then_inc(s["std"], 1)

            def norm_squares(name, chunk_ready=None):
                k0, tiles, base, sq, hp = NORMS[name]
                depth = 2
                for k in range(KC):
                    if chunk_ready:
                        act.wait_ge(chunk_ready, k + 1)
                    if k >= depth or k0:
                        act.wait_ge(s["sq_used"], 8 * k0 + max(k - depth + 1, 0))
                    for src, c0, n, _, _ in norm_sources(name, k):
                        ins = nc.scalar.activation(sq[:, k % depth, c0:c0 + n], src, ACT.Square)
                    ins.then_inc(s["sq"], 1)
                norm_std(name)

            def block_squares(name, i, parts, gemm_name=None):
                k0, _, _, sq, _ = NORMS[name]
                for j in range(2):
                    if gemm_name:
                        b = BLOCK0[gemm_name] + j
                        act.wait_ge(s_evac[b % 2], 2 + b // 2 + i)
                    act.wait_ge(s["sq_used"], 8 * k0 + j - 1 + 2 * i)
                    act.sem_inc(s["act_gate"], 1)
                    for src, c0, n in parts(bass.ds(2 * i + j, 1)):
                        ins = nc.scalar.activation(sq[:, j:j + 1, c0:c0 + n], src, ACT.Square)
                    ins.then_inc(s["sq"], 1)

            def stream_squares(name, gemm_name, parts):
                with act.Fori(0, KC // 2) as i:
                    block_squares(name, i, parts, gemm_name)
                norm_std(name)

            def norm_hi(name):
                _, _, _, _, hp = NORMS[name]
                hi, _, c = OPERAND[name]
                for k in range(KC):
                    act.wait_ge(s["hp"], HP0[name] + k + 1)
                    for _, c0, n, _, shift in norm_sources(name, k):
                        if shift is None:
                            ins = nc.scalar.copy(hi[:, c + k, c0:c0 + n], hp[:, k % 3, c0:c0 + n])
                        else:
                            ins = nc.scalar.activation(hi[:, c + k, c0:c0 + n], hp[:, k % 3, c0:c0 + n],
                                                       ACT.Identity, bias=shift)
                    ins.then_inc(s["op_hi"], 1)

            def evacuate(name, dst, src, func, squares=None, late=0):
                n, b0 = SLABS[name] // PER[name], BLOCK0[name]
                u = 2 if n % 2 == 0 else 1
                if n == 1:
                    act.wait_ge(s["slab_done"], block_done(name, 1))
                    nc.scalar.activation(dst(0), src(gemm_ps[b0 % 2]), func).then_inc(s_evac[b0 % 2], 1)
                    return
                with act.Fori(0, n // u) as i:
                    for j in range(u):
                        act.wait_ge(s["slab_done"], block_done(name, j + 1) + (late if j == 0 else 0) + u * PER[name] * i)
                        nc.scalar.activation(dst(i * u + j), src(gemm_ps[(b0 + j) % 2]), func)\
                          .then_inc(s_evac[(b0 + j) % 2], 1)
                    if squares:
                        norm, buf = squares
                        for j in range(2):
                            act.wait_ge(s_evac[(b0 + j) % 2], 2 + (b0 + j) // 2 + i)
                        block_squares(norm, i, lambda k: [(buf[:, k, :], 0, T2)])
                if squares:
                    norm_std(squares[0])

            act.sem_inc(s_evac[0], 1)
            act.sem_inc(s_evac[1], 1)
            act.sem_inc(s["ada_acc"], ADA_RING)
            act.sem_inc(s["conv_done"], 2)
            act.sem_inc(s["z_evac"], 1)
            act.sem_inc(s["sb_y"], 1)
            act.wait_ge(s["cols_ready"], 1)
            for k, name in enumerate(("c", "c_ctx")):
                nc.scalar.activation(cond[:, :, k], col(name, 0, KC), ACT.Silu).then_inc(s["cond_ready"], 1)
            def take_rows(j):
                act.wait_ge(s["ada_rows"], j + 1)
                nc.scalar.copy(m_rows[:, j * 4 * P:(j + 1) * 4 * P], ada_rows_at(j)).then_inc(s["rows_taken"], 1)

            take_rows(0)
            act.wait_ge(s["x_ready"], 13)
            act.wait_ge(s["fill_ready"], 3)
            norm_squares("l0")
            for j in range(1, ADA_FIRST):
                take_rows(j)
            act.wait_ge(s["mod_ready"], 1)
            norm_hi("l0")

            def wide(ps_):
                return ps_[:, 0:SX].unsqueeze(1)

            def zdst(b0):
                return lambda b: zT[:, bass.ds(b + b0, 1), :]

            evacuate("uv", zdst(0), wide, ACT.Copy)
            evacuate("ga", zdst(8), wide, ACT.Silu)
            evacuate("xb", zdst(12), wide, ACT.Copy)
            evacuate("gb", zdst(16), wide, ACT.Silu)
            def v_std(t):
                act.wait_ge(s["v_stat"], t + 1)
                nc.scalar.activation(mv[:, 2:3], mv[:, 1:2], ACT.Sqrt, bias=eps[:, 0:1]).then_inc(s["v_std"], 1)

            for g in range(4):
                act.wait_ge(s["ch_dft"], g + 1)
                if g:
                    act.wait_ge(s["seq_dft"], g)
                nc.scalar.copy(pq[:, :, :], ps[:, 4 * 512:7 * 512].rearrange("p (t n) -> p t n", t=SX // P))\
                  .then_inc(s["pq_ready"], 1)
                if g < 3:
                    v_std(2 * g)
                    v_std(2 * g + 1)
            for k in range(KC):
                if k == 0:
                    act.wait_ge(s["slab_done"], SLAB0["wo_ab"])
                if k < 4:
                    act.wait_ge(s["ya_ready"], k + 1)
                else:
                    act.wait_ge(s["yb_ready"], k - 3)
                nc.scalar.copy(op_hi[:, k, :], y0_chunk(k)).then_inc(s["op_hi"], 1)
            stream_squares("l1", "wo_ab", lambda k: [(xT[:, k, META:T2], 0, S), (ctxT[:, k, :], S, CTX)])
            norm_hi("l1")

            def narrow(ps_):
                return ps_[:, 0:S].unsqueeze(1)

            evacuate("q", lambda b: q_t[:, bass.ds(b, 1), :], narrow, ACT.Copy)
            evacuate("kv", lambda b: kv_t[:, bass.ds(b, 1), :], wide, ACT.Copy)
            evacuate("gc", lambda b: g_t[:, bass.ds(b, 1), :], narrow, ACT.Silu)
            nu = len(UNITS)
            with act.Fori(0, 2) as i:
                steps.begin(i, 0)
                for u in range(nu + 2):
                    if u >= 2:
                        n = UNITS[u - 2][2]
                        w = att_lat(n)[1] * P
                        if u >= 4:
                            act.wait_ge(s["att_out"], nu + nu * i + u - 3)
                        act.wait_ge(s["p_turned"], nu * i + u - 1)
                        nc.scalar.copy(pT[:, (u - 2) % 2, 0:CTX + w], bank(0, 2)[:, 0:CTX + w])\
                          .then_inc(s["p_copied"], 1)
                    if u < nu:
                        j, c2, n, par = UNITS[u]
                        v, w = u % ATT_BUFS, att_lat(n)[1] * P
                        act.wait_ge(s["nmax"], nu * i + u + 1)
                        head = 4 * j + 2 * c2 + par
                        if u >= ATT_BUFS:
                            act.wait_ge(s["p_turned"], nu * i + u - ATT_BUFS + 1)
                        nc.scalar.activation(p_sb[:, v, 0:CTX + w], pair_ps[u % 2][:, CTX:S + w], ACT.Exp,
                                             bias=sm[:, v, 1:2], scale=ATT_SCALE,
                                             accum_out=sm[:, v, 3:4]).then_inc(s["exps"], 1)
                        nc.scalar.activation(sm[:, v, 2:3], neg_sink[:, bass.ds(8 * i + head, 1)], ACT.Exp,
                                             bias=sm[:, v, 1:2], scale=-1.0).then_inc(s["exps"], 1)
                steps.end(2)
            for k in range(KC):
                act.wait_ge(s["att_o"], k + 1)
                nc.scalar.copy(op_hi[:, k, 0:S], g_t[:, k, :]).then_inc(s["op_hi"], 1)
            stream_squares("final", "wo_c", lambda k: [(xT[:, k, META:T2], 0, S)])
            norm_squares("pre", s["norm_done"])
            norm_hi("pre")

            def halves(ps_):
                return seg2(ps_)

            def conv_silu(b, j):
                act.wait_ge(s["conv_in"], b + 1)
                nc.scalar.activation(xbc[:, bass.ds(b, 1), PAD:TP], conv[:, j:j + 1, :], ACT.Silu)\
                  .then_inc(s["conv_done"], 1)

            g0, b0 = SLAB0["xbc"], BLOCK0["xbc"]

            def xbc_pair(i, silu):
                for j in range(2):
                    act.wait_ge(s["slab_done"], g0 + j + 1 + 2 * i)
                    nc.scalar.copy(two(xbc[:, bass.ds(2 * i + j, 1), PAD:TP].rearrange("p a n -> p (a n)")),
                                   halves(gemm_ps[(b0 + j) % 2])).then_inc(s_evac[(b0 + j) % 2], 1)
                    if silu:
                        conv_silu(2 * i + j - 2, j)

            evacuate("dt", lambda b: two(xbc[:, XC, PAD:TP]), halves, ACT.Copy)
            nc.scalar.preload_act_table_set("natural_log_exp_and_others")
            act.wait_ge(s["small_in"], SMALL)
            steps(nc.scalar.activation(neg_a[:, :], a_log[:, :], ACT.Exp))
            act.wait_ge(s["dt_e"], 1)
            steps(nc.scalar.activation(dtm[0:16, 2, :], dtm[0:16, 1, :], ACT.Exp))
            steps.wait()
            nc.scalar.activation(dtm[0:16, 1, :], dtm[0:16, 2, :], ACT.Ln, bias=1.0).then_inc(s["dt_l"], 1)
            nc.scalar.preload_act_table_set("silu_and_others")
            xbc_pair(0, False)
            with act.Fori(1, XC // 2) as i:
                xbc_pair(i, True)
            for j in range(2):
                conv_silu(XC - 2 + j, j)
            g0z = SLAB0["z"]

            def take_z(t, j):
                act.wait_ge(s["slab_done"], g0z + j + 1 + 2 * t)
                nc.scalar.copy(two(zs[:, bass.ds(2 * t + j, 1), PAD:TP].rearrange("p a n -> p (a n)")),
                               halves(gemm_ps[0])).then_inc(s["z_evac"], 1)

            g0 = SLAB0["sb"]

            def take(m, kind, done):
                act.wait_ge(s["slab_done"], done)
                dst, scale = ((qs, ATT_SCALE), (ks, 1.0), (vs, 1.0))[kind]
                nc.scalar.activation(two(dst[:, m, :]), seg2(gemm_ps[0]), ACT.Copy, scale=scale)\
                  .then_inc(s["sb_evac"], 1)

            def chunk_in(i, j):
                act.wait_ge(s["ssd_used"], max(j, 1) + 2 * i)
                back = bass.ds(i * 2 * P + j * P, P)
                nc.scalar.copy(xst[j % 2][:, :, :], xbc[:, 0:XC, back]).then_inc(s["chunk_in"], 1)
                nc.scalar.copy(dt_t[0:16, :], xbc[0:16, XC, back]).then_inc(s["chunk_in"], 1)

            def chunk(i, j, more):
                for g in range(2):
                    act.wait_ge(s["chunk_acs"], 2 * j + g + 1 + 4 * i)
                    nc.scalar.activation(cexp[:, 8 * g:8 * g + 8, :].rearrange("p h l -> p (h l)"), bank(2, 2),
                                         ACT.Exp).then_inc(s["chunk_e"], 1)
                    if g == 0 and more:
                        chunk_in(i, j + 1)
                if more:
                    take_z(2 * i + j, 0)
                else:
                    act.wait_ge(s["ssd_used"], NT)
                    take(0, 0, g0 + 1)
                act.wait_ge(s["dec_in"], j + 1 + 2 * i)
                nc.scalar.activation(dec[:, :], acs[:, :], ACT.Exp).then_inc(s["dec_ready"], 1)
                for g in range(2):
                    act.wait_ge(s["seg_ready"], 2 * j + g + 1 + 4 * i)
                    nc.scalar.activation(seg[:, 8 * g:8 * g + 8, :], seg[:, 8 * g:8 * g + 8, :], ACT.Exp)\
                      .then_inc(s["seg_e"], 1)
                if more:
                    take_z(2 * i + j, 1)
                else:
                    take(0, 1, g0 + 2)

            act.wait_ge(s["dt_ready"], 1)
            chunk_in(0, 0)
            nc.scalar.preload_act_table_set("natural_log_exp_and_others")
            with act.Fori(0, NT // 2) as i:
                for j in range(2):
                    chunk(i, j, True)
            chunk(NT // 2, 0, False)
            act.wait_ge(s["z_evac"], KC + 1)
            nc.scalar.activation(zs[:, :, PAD:TP], zs[:, :, PAD:TP], ACT.Silu).then_inc(s["z_silu"], 1)
            norm_squares("ssd", s["gated"])
            nc.scalar.preload_act_table_set("natural_log_exp_and_others")

            def sb_logs(i, u):
                m, par, blk, nq, q0, nk, buf = sb_unit(u)
                neg = sb_neg[0:nq, buf, 0:nk]
                act.wait_ge(s["sb_in"], SBN * i + u + 1)
                nc.scalar.activation(neg, neg, ACT.Exp).then_inc(s["sb_l"], 1)
                act.wait_ge(s["sb_l"], 2 * SBN * i + 2 * u + 1)
                nc.scalar.activation(neg, neg, ACT.Ln, bias=1.0).then_inc(s["sb_l"], 1)

            def sb_iteration(i, last):
                for u in range(sb_steps(last)):
                    if sb_live(i, u - 2):
                        m, par, blk, nq, q0, nk, buf = sb_unit(u - 2)
                        w_ps, a = sb_bank(u - 2), sb_tile(u - 2, 1)
                        sb_wait(act, "sb_o", 2 * NT, i, sb_out(u - 2 - SB_BUFS) + 1)
                        act.wait_ge(s["sb_wt"], SBN * i + u - 1)
                        ins = nc.scalar.copy(sb_wT[0:META, buf, 0, 0:nq], w_ps[0:META, 0:nq])
                        if blk:
                            ins = nc.scalar.copy(sb_wT[:, buf, 1:1 + blk, :].rearrange("p a n -> p (a n)"),
                                                 w_ps[:, a:a + blk * P])
                        ins.then_inc(s["sb_wc"], 1)
                    if u in SB_NORM:
                        j = SB_NORM.index(u)
                        act.wait_ge(s["hp"], HP0["ssd"] + j + 1 + 2 * i)
                        act.sem_inc(s["act_gate"], 1)
                        nc.scalar.copy(ys_hi[:, bass.ds(2 * i + j, 1), :], hp_ssd[:, j:j + 1, :])\
                          .then_inc(s["op_hi"], 1)
                    if sb_live(i, u - 1):
                        m, par, blk, nq, q0, nk, buf = sb_unit(u - 1)
                        total = sb_sum[0:nq, buf, 0:nk]
                        act.wait_ge(s["sb_d"], SBN * i + u)
                        nc.scalar.activation(total, total, ACT.Exp).then_inc(s["sb_wr"], 1)
                    if u in SB_TAKE and (u <= len(SBU) or not last):
                        m, kind, g = SB_TAKE[u]
                        take(m, kind, g0 + 3 + g + 1 + 6 * i)
                    if sb_scored(u + 1, last):
                        sb_logs(i, u + 1)

            sb_logs(0, 0)
            sb_iteration(0, False)
            with act.Fori(1, SB_PAIRS // 2 - 1) as i:
                sb_iteration(i, False)
            sb_iteration(SB_PAIRS // 2 - 1, True)
            act.wait_ge(s["sb_y"], SB_PAIRS * NT + 1)
            norm_squares("sbn")
            norm_hi("sbn")
            evacuate("wo_2", lambda b: two(mixT[:, bass.ds(b, 1), :].rearrange("p a n -> p (a n)")), halves,
                     ACT.Copy, ("post", mixT), late=1)
            for k in range(KC):
                act.wait_ge(s["norm_done"], 8 + k + 1)
                nc.scalar.activation(u_hi[:, k, :], xT[:, k, :], ACT.Identity, scale=col("ffn_pre", k))\
                  .then_inc(s["op_hi"], 1)
            norm_squares("ffn")
            g0, b0 = SLAB0["up"], BLOCK0["up"]
            nc.scalar.preload_act_table_set("gelu_apprx_tanh_and_others")
            with act.Fori(0, FC) as i:
                act.wait_ge(s["gate_conv"], i + 1)
                nc.scalar.activation(gacc[:, :], gacc[:, :], ACT.Gelu_apprx_tanh).then_inc(s["gelu"], 1)
                act.wait_ge(s["ffn_f"], i + 1)
                nc.scalar.copy(f_hi[:, bass.ds(i, 1), :], fgl[:, :].unsqueeze(1)).then_inc(s["ffn_hi"], 1)
            evacuate("down", lambda b: two(fT[:, bass.ds(b, 1), :].rearrange("p a n -> p (a n)")), halves,
                     ACT.Copy, ("fin", fT))
            for t in range(1, S // P, 2):
                act.wait_ge(s["out_turned"], t + 1)
                nc.scalar.copy(y_out[:, t, :], (gemm_ps + pair_ps)[t][:, :]).then_inc(s["out_ready_act"], 1)

        @block.vector
        def _(dve):
            steps = Steps(dve, s["dve_steps"])

            def clear_sum(name):
                steps(nc.vector.memset(NORMS[name][3][:, 2, :], 0.0))
                steps.wait()

            def add_squares(name, k, slot):
                k0, tiles, _, sq, _ = NORMS[name]
                dve.wait_ge(s["sq"], 8 * k0 + 1 + k)
                n = sum(n for _, n in tiles)
                if k0 or k:
                    dve.wait_ge(s["sq_used"], 8 * k0 + k)
                nc.vector.tensor_tensor(sq[:, 2, 0:n], sq[:, 2, 0:n], sq[:, slot, 0:n], ALU.add)\
                  .then_inc(s["sq_used"], 1)

            def norm_adds(name):
                clear_sum(name)
                for k in range(KC):
                    add_squares(name, k, k % 2)

            def stream_adds(name):
                clear_sum(name)
                with dve.Fori(0, KC // 2) as i:
                    for j in range(2):
                        add_squares(name, 2 * i + j, j)

            def norm_rstd(name):
                k0, tiles, _, _, _ = NORMS[name]
                dve.wait_ge(s["std"], k0 + 1)
                nc.vector.reciprocal(rstd[:, 0:len(tiles)], stat[:, 0:len(tiles)]).then_inc(s["rstd"], 1)
                dve.wait_ge(s["rstd_rows"], k0 + 1)

            def norm_operand(name):
                _, _, _, _, hp = NORMS[name]
                hi, lo, c = OPERAND[name]
                hi0 = OP_DONE[name] - KC
                for k in range(KC + 1):
                    if k < KC:
                        if k >= 3:
                            dve.wait_ge(s["op_ready"], hi0 + k - 2)
                        for src, c0, n, gain, _ in norm_sources(name, k):
                            ins = nc.vector.scalar_tensor_tensor(hp[:, k % 3, c0:c0 + n], src, gain,
                                                                 rstd_rows(name, c0, n), ALU.mult, ALU.mult)
                        ins.then_inc(s["hp"], 1)
                    if k >= 1:
                        dve.wait_ge(s["op_hi"], hi0 + k)
                        for _, c0, n, _, shift in norm_sources(name, k - 1):
                            o, h = lo[:, c + k - 1, c0:c0 + n], hi[:, c + k - 1, c0:c0 + n].bitcast(F32)
                            a = hp[:, (k - 1) % 3, c0:c0 + n]
                            if shift is None:
                                ins = nc.vector.tensor_tensor(o, a, h, ALU.subtract)
                            else:
                                ins = nc.vector.scalar_tensor_tensor(o, a, shift, h, ALU.add, ALU.subtract)
                        ins.then_inc(s["op_ready"], 1)

            def take_cols(v, src):
                dve.wait_ge(s["vec_turned"], 3 if v else 1)
                r = VEC_ROWS[v]
                nc.vector.tensor_copy(cols[:, v, 0:r], src[:, 0:r]).then_inc(s["cols_ready"], 1)

            take_cols(0, bank(0))
            for k in range(KC):
                dve.wait_ge(s["x_turned"], k + 1)
                nc.vector.tensor_copy(lat(k), bank(k % 4)[:, :]).then_inc(s["x_ready"], 1)
            for k in range(0, KC, 2):
                dve.wait_ge(s["x_turned"], KC + k // 2 + 1)
                nc.vector.tensor_copy(ctxT[:, k:k + 2, :].rearrange("p k n -> p (k n)"),
                                      bank(k // 2 % 4)[:, :]).then_inc(s["x_ready"], 1)
            dve.wait_ge(s["x_turned"], 13)
            nc.vector.tensor_copy(xT[:, :, 0:META], bank(0)[:, 0:KC * META].rearrange("p (k n) -> p k n", k=KC))\
              .then_inc(s["x_ready"], 1)
            norm_adds("l0")
            norm_rstd("l0")

            def modulation(n0, n, src):
                steps(nc.vector.tensor_tensor(mod[:, n0:n0 + n, :], src.rearrange("p (n c) -> p n c", c=2),
                                              col("ada_b", n0, n).unsqueeze(2).to_broadcast([P, n, 2]), ALU.add))
                steps.wait()

            def norm_gain(layer):
                for k in range(2):
                    steps(nc.vector.scalar_tensor_tensor(
                        modg[:, layer, k, :], mod[:, 24 * layer + KC:24 * layer + 2 * KC, k], 1.0,
                        col("norm_g", KC * layer, KC), ALU.add, ALU.mult))
                steps.wait()

            dve.wait_ge(s["rows_turned"], 1)
            modulation(0, 2 * KC, bank(2)[:, 0:4 * KC])
            norm_gain(0)
            dve.sem_inc(s["mod_ready"], 1)
            norm_operand("l0")
            for v in range(1, 3):
                take_cols(v, bank(7)[:, (v - 1) * P:v * P])

            def ada_products(w, acc):
                for k in range(KC):
                    for c_ in range(2):
                        if k:
                            steps.wait(but=1)
                            steps(nc.vector.scalar_tensor_tensor(acc(c_), w[:, k, :], cond[:, k, c_:c_ + 1], acc(c_),
                                                                 ALU.mult, ALU.add))
                        else:
                            steps(nc.vector.tensor_scalar(acc(c_), w[:, k, :], cond[:, k, c_:c_ + 1], None,
                                                          ALU.mult))
                steps.wait()
                dve.sem_inc(s["ada_acc"], 1)

            with dve.Fori(0, ADA_L0 // ADA_RING) as i:
                steps.begin(i, ADA_RING * 2 * KC)
                for j in range(ADA_RING):
                    dve.wait_ge(s_ada_in[j], 16 + 16 * i)
                    ada_products(ada_ring[:, j, :, :],
                                 lambda c_: ada_acc[:, bass.ds(ADA_RING * i + j, 1), c_, :])
                steps.end(ADA_L0 // ADA_RING)
            dve.wait_ge(s["ada_sums"], 1)
            modulation(2 * KC, ADA_L0, bank(7)[:, 0:2 * ADA_L0])
            norm_gain(1)
            dve.sem_inc(s["mod1_ready"], 1)

            def v_norm(t):
                dve.wait_ge(s["v_turned"], t + 1)
                v_ps = bank(7)[:, :]
                if t:
                    dve.wait_ge(s["v_ready"], t)
                steps(nc.vector.bn_stats(bn[:, 0:6], v_ps))
                steps.wait()
                nc.vector.bn_aggr(mv[:, 0:2], bn[:, 0:6]).then_inc(s["v_stat"], 1)
                dve.wait_ge(s["v_std"], t + 1)
                steps(nc.vector.reciprocal(mv[:, 3:4], mv[:, 2:3]))
                steps.wait()
                nc.vector.tensor_scalar(vt[:, t, :], v_ps, mv[:, 0:1], mv[:, 3:4], ALU.subtract, ALU.mult)\
                  .then_inc(s["v_ready"], 1)

            def fourier_gate(g):
                dve.wait_ge(s["seq_dft"], g + 1)
                f_ps = gemm_ps[g % 2]
                nc.vector.tensor_tensor(zT[:, 12 + g, 0:S], f_ps[:, 0:S], zT[:, 16 + g, 0:S], ALU.mult)
                nc.vector.scalar_tensor_tensor(zT[:, 12 + g, S:SX], f_ps[:, S:SX], float(np.sqrt(S / CTX)),
                                               zT[:, 16 + g, S:SX], ALU.mult, ALU.mult).then_inc(s["yb_ready"], 1)

            for g in range(3):
                v_norm(2 * g)
                v_norm(2 * g + 1)
                if g == 2:
                    dve.wait_ge(s["sw_turned"], 1)
                    nc.vector.tensor_copy(swT[:, :, :].rearrange("p h q -> p (h q)"), bank(7)[:, :])\
                      .then_inc(s["sw_ready"], 1)
                fourier_gate(g)
            dve.wait_ge(s["small_in"], SMALL)
            for h in range(4):
                dve.wait_ge(s["spatial"], h + 1)
                nt = SX // P
                steps(nc.vector.scalar_tensor_tensor(
                    gmlp[:, :].rearrange("p (t q) -> p t q", t=nt),
                    pair_ps[h % 2][:, 0:SX].rearrange("p (t q) -> p t q", t=nt), col("v_norm", h),
                    s_bias[:, h:h + 1, :].to_broadcast([P, nt, P]), ALU.mult, ALU.add))
                steps.wait()
                steps(nc.vector.tensor_tensor(zT[:, h, :], zT[:, h, :], gmlp[:, :], ALU.mult))
                steps.wait()
                nc.vector.tensor_tensor(zT[:, h, :], zT[:, h, :], zT[:, 8 + h, :], ALU.mult).then_inc(s["ya_ready"], 1)
            for k in range(KC):
                if k == 7:
                    fourier_gate(3)
                dve.wait_ge(s["op_hi"], OP_DONE["l0"] + k + 1)
                nc.vector.tensor_tensor(op_lo[:, k, :], y0_chunk(k), op_hi[:, k, :].bitcast(F32), ALU.subtract)\
                  .then_inc(s["op_ready"], 1)

            def add_gated(name, layer, with_ctx, norm):
                b0 = BLOCK0[name]
                clear_sum(norm)

                def blocks(i, adds):
                    for j in range(2):
                        dve.wait_ge(s["slab_done"], block_done(name, j + 1) + 2 * i)
                        o = gemm_ps[(b0 + j) % 2]
                        gate = mod[:, bass.ds(2 * i + (24 * layer + 2 * KC + j), 1), :]
                        x_k = xT[:, bass.ds(2 * i + j, 1), META:T2]
                        ins = nc.vector.scalar_tensor_tensor(x_k, o[:, 0:S].unsqueeze(1), gate[:, 0, 0:1], x_k,
                                                             ALU.mult, ALU.add)
                        if with_ctx:
                            c_k = ctxT[:, bass.ds(2 * i + j, 1), :]
                            ins = nc.vector.scalar_tensor_tensor(c_k, o[:, S:SX].unsqueeze(1), gate[:, 0, 1:2], c_k,
                                                                 ALU.mult, ALU.add)
                        ins.then_inc(s_evac[(b0 + j) % 2], 1)
                    for j in range(2):
                        if adds:
                            add_squares(norm, 2 * i + (j - 2), j)

                blocks(0, False)
                with dve.Fori(1, KC // 2) as i:
                    blocks(i, True)
                for j in range(2):
                    add_squares(norm, KC - 2 + j, j)

            add_gated("wo_ab", 0, True, "l1")
            all_evacuated(dve, "wo_ab")
            norm_rstd("l1")
            norm_operand("l1")
            for j in range(ADA_L1):
                dve.wait_ge(s["ada1_in"], 16 * ADA_L1)
                ada_products(ada_ring1[:, j, :, :], lambda c_: ada_acc1[:, j, c_, :])
            steps(nc.vector.tensor_scalar(neg_sink[:, :], sink[:, :], -1.0, None, ALU.mult))
            HALF_SWAP = [p ^ 16 for p in range(32)]
            dve.wait_ge(s["consts_in"], 16 * 10)
            all_evacuated(dve, "q")
            with dve.Fori(0, KC) as i:
                steps.begin(i, 5)
                q_k = q_t[:, bass.ds(i, 1), :]
                steps.wait()
                steps(nc.vector.tensor_copy(rot[:, 1:2, :], q_k))
                steps.wait()
                steps(nc.vector.tensor_tensor(q_k, rot[:, 1:2, :], cos[:, :].unsqueeze(1), ALU.mult))
                steps(nc.vector.stream_shuffle(rot[:, 0, :], rot[:, 1, :], HALF_SWAP))
                steps.wait()
                steps(nc.vector.tensor_tensor(rot[:, 0, :], rot[:, 0, :], sin[:, :], ALU.mult))
                steps.wait()
                steps(nc.vector.tensor_tensor(q_k, q_k, rot[:, 0:1, :], ALU.add))
                steps.end(KC)
            steps.wait()
            all_evacuated(dve, "kv")
            for k in range(2):
                steps(nc.vector.stream_shuffle(rot[:, 0, :], kv_t[:, k, 0:S], HALF_SWAP))
                steps.wait()
                steps(nc.vector.tensor_tensor(rot[:, 0, :], rot[:, 0, :], sin[:, :], ALU.mult))
                steps(nc.vector.tensor_tensor(rot[:, 1, :], kv_t[:, k, 0:S], cos[:, :], ALU.mult))
                steps.wait()
                steps(nc.vector.tensor_tensor(kv_t[:, k, 0:S], rot[:, 0, :], rot[:, 1, :], ALU.add))
                steps.wait()
            dve.sem_inc(s["rope_ready"], 1)
            dve.wait_ge(s["vtok_turned"], 1)
            steps(nc.vector.tensor_copy(v_tok[:, :, :],
                                        bank(4, 3).rearrange("p (t n) -> p t n", t=SX // P)))
            steps.wait()
            dve.sem_inc(s["vtok_ready"], 1)
            dve.wait_ge(s["ada_sums"], 2)
            modulation(2 * KC + ADA_L0, ADA_L1, bank(7)[:, 0:2 * ADA_L1])
            dve.sem_inc(s["gate1_ready"], 1)
            all_evacuated(dve, "gc")
            nu = len(UNITS)
            per = 3 * nu
            with dve.Fori(0, 2) as i:
                steps.begin(i, per)
                for u in range(nu + 1):
                    if u < nu:
                        j, c2, n, par = UNITS[u]
                        v, w = u % ATT_BUFS, att_lat(n)[1] * P
                        sc = pair_ps[u % 2]
                        dve.wait_ge(s["scores"], nu * i + u + 1)
                        steps(nc.vector.tensor_reduce(sm[:, v, 0:1], sc[:, CTX:S + w], AX.X, ALU.max))
                        steps.wait()
                        head = 4 * j + 2 * c2 + par
                        nc.vector.tensor_scalar(sm[:, v, 1:2], sm[:, v, 0:1], -ATT_SCALE,
                                                neg_sink[:, bass.ds(8 * i + head, 1)], ALU.mult, ALU.min)\
                          .then_inc(s["nmax"], 1)
                    if u >= 1:
                        v = (u - 1) % ATT_BUFS
                        w = att_lat(UNITS[u - 1][2])[1] * P
                        dve.wait_ge(s["exps"], 2 * nu * i + 2 * u)
                        steps(nc.vector.tensor_tensor(sm[:, v, 4:5], sm[:, v, 2:3], sm[:, v, 3:4], ALU.add))
                        steps.wait()
                        steps(nc.vector.reciprocal(sm[:, v, 5:6], sm[:, v, 4:5]))
                        steps.wait()
                        nc.vector.tensor_scalar(p_sb[:, v, 0:CTX + w], p_sb[:, v, 0:CTX + w], sm[:, v, 5:6], None,
                                                ALU.mult).then_inc(s["probs"], 1)
                    if u in (12, 20, 28, nu):
                        pair = (12, 20, 28, nu).index(u)
                        dve.wait_ge(s["att_out"], nu * i + nu + 8 * (pair + 1))
                        g_k = g_t[:, bass.ds(4 * i + pair, 1), :]
                        nc.vector.tensor_tensor(g_k, bank(2 + pair % 2)[:, :].unsqueeze(1), g_k, ALU.mult)\
                          .then_inc(s["att_o"], 1)
                steps.end(2)
            for k in range(KC):
                dve.wait_ge(s["op_hi"], OP_DONE["l1"] + k + 1)
                if k == 0:
                    dve.wait_ge(s["att_o"], 8)
                nc.vector.tensor_tensor(op_lo[:, k, 0:S], g_t[:, k, :], op_hi[:, k, 0:S].bitcast(F32), ALU.subtract)\
                  .then_inc(s["op_ready"], 1)
            add_gated("wo_c", 1, False, "final")
            all_evacuated(dve, "wo_c")
            norm_rstd("final")
            for k in range(KC):
                src, c0, n, gain, _ = norm_sources("final", k)[0]
                nc.vector.scalar_tensor_tensor(src, src, gain, rstd_rows("final", c0, n), ALU.mult, ALU.mult)\
                  .then_inc(s["norm_done"], 1)
            dve.wait_ge(s["norm_done"], 8)
            norm_rstd("pre")
            norm_operand("pre")
            steps(nc.vector.memset(xbc[:, :, 0:PAD], 0.0))
            steps(nc.vector.memset(prev[:, :], 0.0))
            all_evacuated(dve, "dt")
            dtr = xbc[0:16, XC, PAD:TP]
            dve.wait_ge(s["small_in"], SMALL)
            steps(nc.vector.tensor_scalar(dtm[0:16, 0, :], dtr, dt_bias[0:16, 0:1], None, ALU.add))
            steps.wait()
            steps(nc.vector.tensor_scalar(dtm[0:16, 2, :], dtm[0:16, 0, :], 0.0, -2.0, ALU.max, ALU.mult))
            steps.wait()
            nc.vector.tensor_tensor(dtm[0:16, 1, :], dtm[0:16, 0, :], dtm[0:16, 2, :], ALU.add)\
              .then_inc(s["dt_e"], 1)
            dve.wait_ge(s["dt_l"], 1)
            steps(nc.vector.scalar_tensor_tensor(dtr, dtm[0:16, 0, :], 0.0, dtm[0:16, 1, :], ALU.max, ALU.add))
            steps(nc.vector.tensor_scalar(neg_a[:, :], neg_a[:, :], -1.0, None, ALU.mult))
            steps.wait()
            b0 = BLOCK0["xbc"]
            taps = 4
            with dve.Fori(0, XC // 2) as i:
                steps.begin(i, 2 * (taps - 1))
                for j in range(2):
                    xk = xbc[:, bass.ds(2 * i + j, 1), :]

                    def w_col(k):
                        return cols[:, 1, bass.ds(2 * i + (j + XC * k), 1)]

                    dve.wait_ge(s_evac[(b0 + j) % 2], 2 + (b0 + j) // 2 + i)
                    dve.wait_ge(s["conv_done"], 2 * i + j + 1)
                    steps(nc.vector.tensor_scalar(conv[:, j:j + 1, :], xk[:, :, PAD:TP], w_col(taps - 1),
                                                  cols[:, 1, bass.ds(2 * i + (j + VEC_B["conv_b"]), 1)],
                                                  ALU.mult, ALU.add))
                    for k in range(1, taps):
                        steps.wait()
                        o = conv[:, j:j + 1, k:T2]
                        ins = nc.vector.scalar_tensor_tensor(o, xk[:, :, PAD:TP - k], w_col(taps - 1 - k), o,
                                                             ALU.mult, ALU.add)
                        if k < taps - 1:
                            steps(ins)
                        else:
                            ins.then_inc(s["conv_in"], 1)
                steps.end(XC // 2)
            dve.wait_ge(s["conv_done"], XC + 2)
            dve.sem_inc(s["dt_ready"], 1)
            dve.sem_inc(s["ssd_used"], 1)
            H = 16

            def by_head(ap, n):
                return ap.unsqueeze(2).to_broadcast([P, H, n])

            def chunk_start(i, j):
                dve.wait_ge(s["chunk_turned"], j + 1 + 2 * i)
                steps(nc.vector.tensor_copy(dt_k[:, :], pair_ps[1][:, 2 * P:2 * P + H]))
                nc.vector.tensor_copy(b_tok[:, j % 2, :], pair_ps[1][:, 0:2 * P]).then_inc(s["chunk_b"], 1)
                steps.wait()
                steps(nc.vector.tensor_tensor(adt[:, :], dt_k[:, :], neg_a[:, :], ALU.mult))
                steps(nc.vector.tensor_tensor(xdt[j % 2][:, :].rearrange("p (h d) -> p h d", h=H),
                                              bank(2, 2).rearrange("p (h d) -> p h d", h=H),
                                              by_head(dt_k[:, :], HEAD), ALU.mult))
                steps.wait()
                dve.sem_inc(s["chunk_scaled"], 1)

            def chunk(i, j, more):
                xst_t, xdt_t = xst[j % 2], xdt[j % 2]
                dve.wait_ge(s["chunk_sums"], j + 1 + 2 * i)
                a_ps = pair_ps[1][:, S:S + 2 * H]
                a_ps_cb = pair_ps[1][:, S + P:S + 3 * P].rearrange("p (g l) -> p g l", g=2)
                steps(nc.vector.tensor_copy(acs[:, :], a_ps))
                steps.wait()
                steps(nc.vector.tensor_tensor(cb[:, :, :], a_ps_cb, tri[:, :].unsqueeze(1).to_broadcast([P, 2, P]),
                                              ALU.mult))
                for g in range(2):
                    seg_g = seg[:, 8 * g:8 * g + 8, :]
                    dve.wait_ge(s["chunk_e"], 2 * j + g + 1 + 4 * i)
                    nc.vector.tensor_tensor(seg_g, bank(2, 2).rearrange("p (h l) -> p h l", h=8),
                                            acs[:, 8 * g:8 * g + 8].unsqueeze(2).to_broadcast([P, 8, P]),
                                            ALU.subtract).then_inc(s["seg_sub"], 1)
                    dve.wait_ge(s["seg_sub"], 2 * j + g + 1 + 4 * i)
                    nc.vector.tensor_scalar(seg_g, seg_g, 0.0, None, ALU.min).then_inc(s["seg_ready"], 1)
                    c_g = cexp[:, 8 * g:8 * g + 8, :]
                    steps(nc.vector.tensor_tensor(c_g, c_g, xst_t[:, 10 + g:11 + g, :].to_broadcast([P, 8, P]),
                                                  ALU.mult))
                steps(nc.vector.tensor_tensor(acs[:, 0:H], acs[:, H:2 * H], acs[:, 0:H], ALU.subtract))
                steps.wait()
                dve.sem_inc(s["dec_in"], 1)
                steps(nc.vector.tensor_tensor(xst_t[:, 0:KC, :], xst_t[:, 0:KC, :],
                                              skip[:, :].unsqueeze(2).to_broadcast([P, KC, P]), ALU.mult))
                for g in range(2):
                    l_g = seg[:, 8 * g:8 * g + 8, :]
                    dve.wait_ge(s["seg_e"], 2 * j + g + 1 + 4 * i)
                    steps(nc.vector.tensor_tensor(l_g, l_g, cb[:, g:g + 1, :].to_broadcast([P, 8, P]), ALU.mult))
                dve.wait_ge(s["dec_ready"], j + 1 + 2 * i)
                steps(nc.vector.tensor_tensor(xdd[:, :].rearrange("p (h d) -> p h d", h=H),
                                              xdt_t[:, :].rearrange("p (h d) -> p h d", h=H),
                                              by_head(dec[:, 0:H], HEAD), ALU.mult))
                steps.wait()
                dve.sem_inc(s["ssd_operands"], 1)
                if more:
                    chunk_start(i, j + 1)
                dve.wait_ge(s["ssd_y"], j + 1 + 2 * i)
                ins = nc.vector.tensor_tensor(xbc[:, 0:KC, bass.ds(i * 2 * P + j * P, P)], xst_t[:, 0:KC, :],
                                              pair_ps[0][:, :].rearrange("p (k l) -> p k l", k=KC), ALU.add)
                if not more:
                    ins.then_inc(s["ssd_used"], 1)
                    return
                steps(ins)
                pv = prev[:, :].rearrange("p (h d) -> p h d", h=H)
                steps(nc.vector.tensor_tensor(pv, pv, by_head(dec[:, H:2 * H], HEAD), ALU.mult))
                steps.wait()
                dve.wait_ge(s["ssd_state"], j + 1 + 2 * i)
                nc.vector.tensor_tensor(prev[:, :], prev[:, :], pair_ps[1][:, :], ALU.add).then_inc(s["ssd_used"], 1)

            chunk_start(0, 0)
            with dve.Fori(0, NT // 2) as i:
                steps.begin(i, 2 * 14)
                for j in range(2):
                    chunk(i, j, True)
                steps.end(NT // 2)
            chunk(NT // 2, 0, False)
            dve.wait_ge(s["ssd_used"], NT + 1)
            dve.wait_ge(s["z_silu"], 1)
            for k in range(KC):
                z_k = zs[:, k, PAD:TP]
                nc.vector.tensor_tensor(z_k, z_k, xbc[:, k, PAD:TP], ALU.mult).then_inc(s["gated"], 1)
            norm_rstd("ssd")
            nc.vector.tensor_copy(rstd_ssd[:, :], rstd_rows("ssd", 0, T2)).then_inc(s["rows_kept"], 1)
            dve.wait_ge(s["ssd_used"], NT + 1)

            dve.wait_ge(s["rows_kept"], 1)

            def sb_start(i, u):
                m, par, blk, nq, q0, nk, buf = sb_unit(u)
                neg, relu_u = (a[0:nq, buf, 0:nk] for a in (sb_neg, sb_relu))
                z_u = sb_bank(u)[0:nq, sb_key0(u):sb_key0(u) + nk]
                own, mask = (z_u[:, nk - P:nk], before) if blk else (z_u, before_meta)
                dve.wait_ge(s["sb_scores"], SBN * i + u + 1)
                steps(nc.vector.tensor_tensor(own, own, mask[0:nq, :], ALU.add))
                steps.wait()
                steps(nc.vector.tensor_scalar(relu_u, z_u, 0.0, None, ALU.max))
                steps.wait()
                nc.vector.scalar_tensor_tensor(neg, relu_u, -2.0, z_u, ALU.mult, ALU.add)\
                  .then_inc(s["sb_in"], 1)

            def sb_iteration(i, last):
                for u in range(sb_steps(last)):
                    if u + 1 in SB_NORM:
                        j = SB_NORM.index(u + 1)
                        nc.vector.scalar_tensor_tensor(hp_ssd[:, j:j + 1, :], zs[:, bass.ds(2 * i + j, 1), PAD:TP],
                                                       cols[:, 0, bass.ds(2 * i + (COL["ssd_norm"] + j), 1)],
                                                       rstd_ssd[:, :].unsqueeze(1), ALU.mult, ALU.mult)\
                          .then_inc(s["hp"], 1)
                    if u - 1 in SB_NORM:
                        j = SB_NORM.index(u - 1)
                        dve.wait_ge(s["op_hi"], OP_DONE["pre"] + j + 1 + 2 * i)
                        nc.vector.tensor_tensor(ys_lo[:, bass.ds(2 * i + j, 1), :], hp_ssd[:, j:j + 1, :],
                                                ys_hi[:, bass.ds(2 * i + j, 1), :].bitcast(F32), ALU.subtract)\
                          .then_inc(s["op_ready"], 1)
                    if sb_live(i, u - SB_SKEW) and sb_outputs(u - SB_SKEW):
                        m, par, blk, nq, q0, nk, buf = sb_unit(u - SB_SKEW)
                        n = P if blk else META
                        h = sb_out(u - SB_SKEW)
                        dve.wait_ge(s["sb_o"], 2 * NT * i + h + 1)
                        o = sb_bank(u - SB_SKEW)[:, 0:n].unsqueeze(1)
                        nc.vector.tensor_copy(ysb[:, bass.ds(2 * i + m, 1), q0:q0 + n], o).then_inc(s["sb_y"], 1)
                    if sb_live(i, u - 1):
                        m, par, blk, nq, q0, nk, buf = sb_unit(u - 1)
                        relu, neg, total = (a[0:nq, buf, :] for a in (sb_relu, sb_neg, sb_sum))
                        z_ps = sb_bank(u - 1)[0:nq, sb_key0(u - 1):sb_key0(u - 1) + nk]
                        sb_wait(dve, "sb_wt", SBN, i, u - SB_BUFS)
                        dve.wait_ge(s["sb_l"], 2 * SBN * i + 2 * u)
                        steps(nc.vector.tensor_tensor_scan(total[:, nk - 1::-1], relu[:, nk - 1::-1],
                                                           neg[:, nk - 1::-1], 0.0, ALU.add, ALU.add))
                        steps.wait()
                        nc.vector.tensor_tensor(total[:, 0:nk], z_ps, total[:, 0:nk], ALU.subtract)\
                          .then_inc(s["sb_d"], 1)
                    if u % len(SBU) == 1 and u < SBN:
                        m = u // len(SBU)
                        dve.wait_ge(s["sb_vt"], 2 * i + m + 1)
                        steps(nc.vector.tensor_copy(v_sb[0:META, m, 0, :], gemm_ps[0][0:META, 0:P]))
                        steps(nc.vector.tensor_copy(v_sb[:, m, 1:NT, :].rearrange("p t n -> p (t n)"),
                                                    gemm_ps[0][:, P:NT * P]))
                        steps.wait()
                        dve.sem_inc(s["sb_v"], 1)
                    if sb_scored(u + 1, last):
                        sb_start(i, u + 1)

            sb_start(0, 0)
            sb_iteration(0, False)
            with dve.Fori(1, SB_PAIRS // 2 - 1) as i:
                steps.begin(i - 1, 2 * (2 + 3 * len(SBU)))
                sb_iteration(i, False)
                steps.end(SB_PAIRS // 2 - 2)
            sb_iteration(SB_PAIRS // 2 - 1, True)
            dve.wait_ge(s["sb_y"], SB_PAIRS * NT + 1)
            norm_adds("sbn")
            norm_rstd("sbn")
            dve.wait_ge(s["slab_done"], SLAB0["wo_2"])
            norm_operand("sbn")

            def add_normed(name, operand=None):
                _, _, _, _, hp = NORMS[name]
                norm_rstd(name)
                n0 = 8 * (NORMS[name][0] == 6) + 16 * (NORMS[name][0] == 8)
                for k in range(KC + 3):
                    if k < KC:
                        src, c0, n, gain, _ = norm_sources(name, k)[0]
                        if k >= 3:
                            dve.wait_ge(s["norm_done"], n0 + k - 2)
                        nc.vector.scalar_tensor_tensor(hp[:, k % 3, 0:n], src, gain, rstd_rows(name, c0, n),
                                                       ALU.mult, ALU.mult).then_inc(s["normed"], 1)
                    if 1 <= k <= KC:
                        dve.wait_ge(s["normed"], n0 - 8 + k)
                        nc.vector.tensor_tensor(xT[:, k - 1, :], xT[:, k - 1, :], hp[:, (k - 1) % 3, 0:T2], ALU.add)\
                          .then_inc(s["norm_done"], 1)
                    if operand and 3 <= k:
                        operand(k - 3)

            def ffn_lo(k):
                dve.wait_ge(s["op_hi"], OP_DONE["sbn"] + k + 1)
                nc.vector.scalar_tensor_tensor(u_lo[:, k, :], xT[:, k, :], col("ffn_pre", k), u_hi[:, k, :].bitcast(F32),
                                               ALU.mult, ALU.subtract).then_inc(s["op_ready"], 1)

            stream_adds("post")
            add_normed("post", ffn_lo)
            norm_adds("ffn")
            norm_rstd("ffn")
            steps(nc.vector.tensor_copy(rstd_ffn[:, :], rstd_rows("ffn", 0, T2)))
            steps(nc.vector.memset(gp[:, 0:2], 0.0))
            steps.wait()
            g0, b0 = SLAB0["up"], BLOCK0["up"]
            with dve.Fori(0, FC) as i:
                steps.begin(i, 4)

                def w_col(k):
                    return cols[:, 2, bass.ds(i + FC * k, 1)]

                dve.wait_ge(s["slab_done"], g0 + 1 + 2 * i)
                steps.wait()
                nc.vector.tensor_tensor(two(gp[:, 2:2 + T2]), seg2(gemm_ps[b0 % 2]), two(rstd_ffn[:, :]), ALU.mult)\
                  .then_inc(s_evac[b0 % 2], 1)
                dve.wait_ge(s_evac[b0 % 2], 2 + b0 // 2 + i)
                steps(nc.vector.tensor_scalar(gacc[:, :], gp[:, 2:2 + T2], w_col(2),
                                              cols[:, 1, bass.ds(i + VEC_B["ffn_b"], 1)], ALU.mult, ALU.add))
                steps.wait()
                steps(nc.vector.scalar_tensor_tensor(gacc[:, :], gp[:, 1:1 + T2], w_col(1), gacc[:, :],
                                                     ALU.mult, ALU.add))
                steps.wait()
                nc.vector.scalar_tensor_tensor(gacc[:, :], gp[:, 0:T2], w_col(0), gacc[:, :], ALU.mult, ALU.add)\
                  .then_inc(s["gate_conv"], 1)
                dve.wait_ge(s["gelu"], i + 1)
                steps(nc.vector.tensor_tensor(gacc[:, :], gacc[:, :], rstd_ffn[:, :], ALU.mult))
                steps.wait()
                dve.wait_ge(s["slab_done"], g0 + 2 + 2 * i)
                nc.vector.tensor_tensor(two(fgl[:, :]), seg2(gemm_ps[(b0 + 1) % 2]), two(gacc[:, :]), ALU.mult)\
                  .then_inc(s["ffn_f"], 1)
                dve.wait_ge(s["ffn_f"], i + 1)
                dve.sem_inc(s_evac[(b0 + 1) % 2], 1)
                dve.wait_ge(s["ffn_hi"], i + 1)
                steps(nc.vector.tensor_tensor(f_lo[:, bass.ds(i, 1), :], fgl[:, :].unsqueeze(1),
                                              f_hi[:, bass.ds(i, 1), :].bitcast(F32), ALU.subtract))
                steps.wait()
                dve.sem_inc(s["op_ready"], 1)
                steps.end(FC)
            dve.wait_ge(s["op_ready"], OP_DONE["ffn"] + FC)
            stream_adds("fin")
            add_normed("fin")
            for t in range(0, S // P, 2):
                dve.wait_ge(s["out_turned"], t + 1)
                nc.vector.tensor_copy(y_out[:, t, :], (gemm_ps + pair_ps)[t][:, :]).then_inc(s["out_ready"], 1)

        @block.tensor
        def _(pe):
            mm = nc.tensor.matmul

            def sums_end(name):
                k0, tiles, _, sq, _ = NORMS[name]
                o = pair_ps[1]
                mm(o[:, 0:len(tiles)], zeros[:, :], zeros[:, 0:len(tiles)], start=True, stop=True)
                pe.wait_ge(s["sq_used"], 8 * k0 + 8)
                for t, (c0, n) in enumerate(tiles):
                    ins = mm(o[0:n, t:t + 1], sq[:, 2, c0:c0 + n], ones[:, 0:1], start=False, stop=True,
                             skip_group_check=True)
                ins.then_inc(s["ssq"], 1)
                sums_rows(name)

            def sums_chunks(name):
                k0, tiles, _, sq, _ = NORMS[name]
                o = pair_ps[1]
                mm(o[:, 0:len(tiles)], zeros[:, :], zeros[:, 0:len(tiles)], start=True, stop=True)
                for k in range(KC):
                    pe.wait_ge(s["sq"], 8 * k0 + k + 1)
                    for t, (c0, n) in enumerate(tiles):
                        ins = mm(o[0:n, t:t + 1], sq[:, k % 2, c0:c0 + n], ones[:, 0:1], start=False, stop=True,
                                 skip_group_check=True)
                    ins.then_inc(s["sq_used"], 1)
                pe.wait_ge(s["sq_used"], 8 * k0 + KC)
                pe.sem_inc(s["ssq"], 1)
                sums_rows(name)

            def sums_rows(name):
                k0, tiles, _, _, _ = NORMS[name]
                pe.wait_ge(s["rstd"], k0 + 1)
                for t, (c0, n) in enumerate(tiles):
                    ins = mm(rstd_rows(name, c0, n), rstd[0:n, t:t + 1].to_broadcast([n, P]), ident[0:n, 0:n],
                             start=True, stop=True)
                ins.then_inc(s["rstd_rows"], 1)

            def products(o, hi, lo, w_h, w_l, kn, k0, segs, first, last, slab_end=True, ready=None):
                for k in range(kn):
                    if ready is not None:
                        pe.wait_ge(s["op_ready"], ready + k0 + k + 1)
                    a, z = first and k == 0, last and k == kn - 1
                    for b, (c0, n) in enumerate(segs):
                        mm(o[:, 512 * b:512 * b + n], w_h[:, k, :], hi[:, k0 + k, c0:c0 + n], start=a, stop=False)
                        mm(o[:, 512 * b:512 * b + n], w_h[:, k, :], lo[:, k0 + k, c0:c0 + n], start=False, stop=False)
                    for b, (c0, n) in enumerate(segs):
                        ins = mm(o[:, 512 * b:512 * b + n], w_l[:, k, :], hi[:, k0 + k, c0:c0 + n], start=False,
                                 stop=z)
                if slab_end:
                    ins.then_inc(s["slab_done"], 1)

            def gemm(name, hi, lo, segs, ready=None, cuts=((0, KC),), beside=None):
                per, g0, b0 = PER[name], SLAB0[name], BLOCK0[name]
                n = SLABS[name] // per
                u = 2 if n % 2 == 0 else 1

                def body(i, ready=None):
                    for jb in range(u):
                        b = b0 + jb
                        pe.wait_ge(s_evac[b % 2], 1 + b // 2 + (i if u == 2 else 0))
                        for h, (k0, kn) in enumerate(cuts):
                            j = jb * per + h
                            slot = (g0 + j) % 2
                            pe.wait_ge(s["split"], g0 + j + 1 + u * per * i)
                            products(gemm_ps[b % 2], hi, lo, w_hi[:, slot, :, :], w_lo[:, slot, :, :], kn, k0, segs,
                                     h == 0, h == per - 1, ready=ready if jb == 0 else None)

                body(0, ready)
                if beside:
                    beside()
                if n > u:
                    with pe.Fori(1, n // u) as i:
                        body(i)

            def turn_cols(v, o):
                r = VEC_ROWS[v]
                nc.tensor.transpose(o[:, 0:r], vec_in[0:r, v, :], ident[0:r, 0:r]).then_inc(s["vec_turned"], 1)

            pe.wait_ge(s["vec_in"], 16 * 9)
            pe.wait_ge(s["consts_in"], 16)
            turn_cols(0, bank(0))

            def ada_rows(j):
                pe.wait_ge(s_ada_first[j], 16)
                if j >= 2:
                    pe.wait_ge(s["rows_taken"], j - 1)
                for k in range(KC):
                    ins = mm(ada_rows_at(j), cond[:, k, :], ada_first[:, j % 3, k, :], start=(k == 0),
                             stop=(k == KC - 1))
                ins.then_inc(s["ada_rows"], 1)

            pe.wait_ge(s["cond_ready"], 2)
            ada_rows(0)
            pe.wait_ge(s["x_in"], 16 * 3)
            for k in range(KC):
                if k >= 4:
                    pe.wait_ge(s["x_ready"], k - 3)
                for t in range(S // P):
                    ins = nc.tensor.transpose(bank(k % 4)[:, t * P:(t + 1) * P], x_in[:, t, k * P:(k + 1) * P],
                                              ident[:, :])
                ins.then_inc(s["x_turned"], 1)
            for k in range(0, KC, 2):
                pe.wait_ge(s["x_ready"], 5 + k // 2)
                for a in range(2):
                    for t in range(CTX // P):
                        ins = nc.tensor.transpose(bank(k // 2 % 4)[:, a * CTX + t * P:a * CTX + (t + 1) * P],
                                                  ctx_in[:, t, (k + a) * P:(k + a + 1) * P], ident[:, :])
                ins.then_inc(s["x_turned"], 1)
            pe.wait_ge(s["x_ready"], 9)
            for k in range(KC):
                ins = nc.tensor.transpose(bank(0)[:, k * META:(k + 1) * META], meta_in[:, k * P:(k + 1) * P],
                                          ident[0:META, 0:META])
            ins.then_inc(s["x_turned"], 1)
            pe.wait_ge(s["x_ready"], 13)
            ada_rows(1)
            pe.wait_ge(s["fill_ready"], 3)
            sums_end("l0")
            ada_rows(2)
            ada_rows(3)
            pe.wait_ge(s["rows_taken"], ADA_FIRST)
            for n in range(2 * KC):
                ins = nc.tensor.transpose(bank(2)[:, 2 * n:2 * n + 2], m_rows[:, n * P:(n + 1) * P], ident[0:2, 0:2])
            ins.then_inc(s["rows_turned"], 1)
            pe.wait_ge(s["vec2_in"], 16 * 7)
            for v in range(1, 3):
                turn_cols(v, bank(7)[:, (v - 1) * P:v * P])
            pe.wait_ge(s["mod_ready"], 1)
            gemm("uv", op_hi, op_lo, SEG_XC, ready=0)
            gemm("ga", op_hi, op_lo, SEG_XC)
            gemm("xb", op_hi, op_lo, SEG_XC)

            def modulation_sums():
                pe.wait_ge(s["cols_ready"], 3)
                pe.wait_ge(s["ada_acc"], ADA_RING + ADA_L0)
                for a in range(ADA_L0):
                    for c_ in range(2):
                        ins = mm(bank(7)[:, 2 * a + c_:2 * a + c_ + 1], ada_acc[:, a, c_, :], ones[:, 0:1], start=True,
                                 stop=True)
                ins.then_inc(s["ada_sums"], 1)

            gemm("gb", op_hi, op_lo, SEG_XC, beside=modulation_sums)
            all_evacuated(pe, "gb")
            pe.wait_ge(s["mod1_ready"], 1)
            pe.wait_ge(s["dft_in"], 16 * 2)

            def turn_v(t):
                if t:
                    pe.wait_ge(s["v_ready"], t)
                for h in range(4):
                    ins = nc.tensor.transpose(bank(7)[:, h * P:(h + 1) * P], zT[:, 4 + h, t * P:(t + 1) * P],
                                              ident[:, :])
                ins.then_inc(s["v_turned"], 1)

            for g in range(4):
                if g:
                    pe.wait_ge(s["pq_ready"], g)
                for t in range(SX // P):
                    ins = mm(ps[:, 4 * 512 + t * 2 * P:4 * 512 + (t + 1) * 2 * P], zT[:, 12 + g, t * P:(t + 1) * P],
                             dft_ch[:, :], start=True, stop=True)
                ins.then_inc(s["ch_dft"], 1)
                if g < 3:
                    turn_v(2 * g)
                else:
                    pe.wait_ge(s["v_ready"], SX // P)
                    pe.wait_ge(s["sw_ready"], 1)
                    pe.wait_ge(s["pq_ready"], 4)
                    for h in range(4):
                        if h >= 2:
                            pe.wait_ge(s["ya_ready"], h - 1)
                        for t in range(SX // P):
                            ins = mm(pair_ps[h % 2][:, t * P:(t + 1) * P], vt[:, t, h * P:(h + 1) * P], swT[:, h, :],
                                     start=True, stop=True)
                        ins.then_inc(s["spatial"], 1)
                pe.wait_ge(s["pq_ready"], g + 1)
                if g >= 2:
                    pe.wait_ge(s["yb_ready"], g - 1)
                o = gemm_ps[g % 2]
                nx = S // P
                for t in range(nx):
                    for r in range(2):
                        mm(o[:, 0:S], pq[:, t, r * P:(r + 1) * P], dft_seq[:, t, r, :], start=(t + r == 0),
                           stop=(t == nx - 1 and r == 1))
                for t in range(CTX // P):
                    for r in range(2):
                        ins = mm(o[:, S:SX], pq[:, nx + t, r * P:(r + 1) * P], dft_seq[:, t, r, 0:S:S // CTX],
                                 start=(t + r == 0), stop=(t == CTX // P - 1 and r == 1))
                ins.then_inc(s["seq_dft"], 1)
                if g < 3:
                    turn_v(2 * g + 1)
                if g == 2:
                    pe.wait_ge(s["small_in"], SMALL)
                    pe.wait_ge(s["v_ready"], SX // P)
                    for h in range(4):
                        ins = nc.tensor.transpose(bank(7)[:, h * P:(h + 1) * P], sw[:, h, :], ident[:, :])
                    ins.then_inc(s["sw_turned"], 1)
            pe.wait_ge(s["yb_ready"], 4)
            gemm("wo_ab", op_hi, op_lo, SEG_XC, ready=OP_DONE["l0"])
            sums_end("l1")
            gemm("q", op_hi, op_lo, SEG_X, ready=OP_DONE["y0"])
            pe.sem_inc(s["att_out"], len(UNITS))
            gemm("kv", op_hi, op_lo, SEG_XC)
            gemm("gc", op_hi, op_lo, SEG_X)
            all_evacuated(pe, "kv")
            for t in range(SX // P):
                for k in range(2):
                    a = 4 * 512 + t * CTX + k * P
                    ins = nc.tensor.transpose(ps[:, a:a + P], kv_t[:, 2 + k, t * P:(t + 1) * P], ident[:, :])
            ins.then_inc(s["vtok_turned"], 1)
            pe.wait_ge(s["ada_acc"], ADA_RING + ADA_L0 + ADA_L1)
            for a in range(ADA_L1):
                for c_ in range(2):
                    ins = mm(bank(7)[:, 2 * a + c_:2 * a + c_ + 1], ada_acc1[:, a, c_, :], ones[:, 0:1], start=True,
                             stop=True)
            ins.then_inc(s["ada_sums"], 1)
            pe.wait_ge(s["vtok_ready"], 1)
            pe.wait_ge(s["gate1_ready"], 1)
            all_evacuated(pe, "gc")
            nu = len(UNITS)
            with pe.Fori(0, 2) as i:
                for u in range(nu + 3):
                    if u < nu:
                        j, c2, n, par = UNITS[u]
                        lo, nb = att_lat(n)
                        h = slice(HEAD * par, HEAD * par + HEAD)
                        sc = pair_ps[u % 2]
                        if n == 0 and par == 0:
                            pe.wait_ge(s["att_in"], 3 * j + 2 * c2 + 1 + 6 * i)
                        if u >= 2:
                            pe.wait_ge(s["exps"], 2 * nu * i + 2 * (u - 1))
                        q_u = q_st[:, j, 2 * c2 + par, n * P:(n + 1) * P]
                        for o, k0, k1 in ((sc[:, CTX:S], S, SX), (sc[:, S:S + nb * P], lo * P, (lo + nb) * P)):
                            mm(o, q_u, k_st[:, j, 0, k0:k1], start=True, stop=False)
                            if k1 < SX and n > 0:
                                mm(sc[:, S:S + P], ident_r[:, :], masks[:, 0, :], start=False, stop=False,
                                   skip_group_check=True)
                            if k1 < SX and n < S // P - 1:
                                mm(o[:, (nb - 1) * P:nb * P], ident_r[:, :], masks[:, 1, :], start=False, stop=False,
                                   skip_group_check=True)
                            ins = mm(o, q_u[h, :], k_st[h, j, 1, k0:k1], start=False, stop=True)
                        ins.then_inc(s["scores"], 1)
                    if 2 <= u < nu + 2:
                        nb = att_lat(UNITS[u - 2][2])[1] + CTX // P
                        pe.wait_ge(s["probs"], nu * i + u - 1)
                        if u >= 3:
                            pe.wait_ge(s["p_copied"], nu * i + u - 2)
                        for b in range(nb):
                            ins = nc.tensor.transpose(bank(0, 2)[:, b * P:(b + 1) * P],
                                                      p_sb[:, (u - 2) % ATT_BUFS, b * P:(b + 1) * P], ident[:, :])
                        ins.then_inc(s["p_turned"], 1)
                    if u >= 3:
                        j, c2, n, par = UNITS[u - 3]
                        lo, nb = att_lat(n)
                        if c2 == 0 and n == 0 and par == 0:
                            pe.wait_ge(s["att_in"], 3 * j + 2 + 6 * i)
                        if j and n == 0 and par == 0:
                            pe.wait_ge(s["att_o"], c2 + 1 + 4 * i)
                        pe.wait_ge(s["p_copied"], nu * i + u - 2)
                        o = bank(2 + c2)[HEAD * par:HEAD * par + HEAD, n * P:(n + 1) * P]
                        tiles = [S // P, S // P + 1] + list(range(lo, lo + nb))
                        for b, t in enumerate(tiles):
                            ins = mm(o, v_st[:, j, t, :], pT[:, (u - 3) % 2, b * P:(b + 1) * P], start=(b == 0),
                                     stop=(b == len(tiles) - 1))
                        ins.then_inc(s["att_out"], 1)
            gemm("wo_c", op_hi, op_lo, SEG_X, ready=OP_DONE["l1"])
            sums_end("final")
            sums_chunks("pre")
            gemm("dt", xn_hi, xn_lo, SEG_2, ready=OP_DONE["y1"])
            gemm("xbc", xn_hi, xn_lo, SEG_2)
            all_evacuated(pe, "xbc")

            def slab_chunk(slot, k):
                products(gemm_ps[0], xn_hi, xn_lo, w_hi[:, slot, k:k + 1, :], w_lo[:, slot, k:k + 1, :], 1, k,
                         SEG_2, k == 0, k == KC - 1, k == KC - 1)

            g0z = SLAB0["z"]

            def z_chunks(t, j, k0, k1):
                for k in range(k0, k1):
                    if k == 0:
                        pe.wait_ge(s["split"], g0z + j + 1 + 2 * t)
                        pe.wait_ge(s["z_evac"], j + 1 + 2 * t)
                    slab_chunk((g0z + j) % 2, k)

            H = 16

            def first_chunks(g, k0, k1):
                for k in range(k0, k1):
                    if k == 0:
                        pe.wait_ge(s["split"], SLAB0["sb"] + 3 + g + 1)
                        if g > -3:
                            pe.wait_ge(s["sb_evac"], 3 + g)
                        else:
                            pe.wait_ge(s["z_evac"], KC + 1)
                    slab_chunk((SLAB0["sb"] + 3 + g) % 2, k)

            def chunk_turn(i, j):
                pe.wait_ge(s["chunk_in"], 2 * j + 2 + 4 * i)
                for k in range(KC):
                    nc.tensor.transpose(bank(2, 2)[:, k * P:(k + 1) * P], xst[j % 2][:, k, :], ident[:, :])
                for g in range(2):
                    nc.tensor.transpose(pair_ps[1][:, g * P:(g + 1) * P], xst[j % 2][:, KC + g, :], ident[:, :])
                nc.tensor.transpose(pair_ps[1][:, 2 * P:2 * P + H], dt_t[0:H, :], ident[0:H, 0:H])\
                    .then_inc(s["chunk_turned"], 1)

            def chunk(i, j, more):
                xst_t, xdt_t, t = xst[j % 2], xdt[j % 2], 2 * i + j
                pe.wait_ge(s["chunk_scaled"], j + 1 + 2 * i)
                for g in range(2):
                    if g:
                        pe.wait_ge(s["seg_sub"], 2 * j + 1 + 4 * i)
                    for h in range(8):
                        ins = mm(bank(2, 2)[:, h * P:(h + 1) * P], adt[:, 8 * g + h:8 * g + h + 1].to_broadcast([P, P]),
                                 tri[:, :], start=True, stop=True)
                    ins.then_inc(s["chunk_acs"], 1)
                    if g == 0:
                        pe.wait_ge(s["ssd_used"], j + 1 + 2 * i)
                        mm(pair_ps[1][:, S:S + H], tri[:, :], adt[:, :], start=True, stop=True)
                        mm(pair_ps[1][:, S + H:S + 2 * H], ones[:, :], adt[:, :], start=True, stop=True)
                        for c in range(2):
                            ins = mm(pair_ps[1][:, S + P + c * P:S + 2 * P + c * P], xst_t[:, KC + c, :],
                                     xst_t[:, KC + 2 + c, :], start=True, stop=True)
                        ins.then_inc(s["chunk_sums"], 1)
                    if more:
                        z_chunks(t, 0, 4 * g, 4 * g + 4)
                    else:
                        first_chunks(-3, 4 * g, 4 * g + 4)
                if not more:
                    first_chunks(-2, 0, KC)
                else:
                    z_chunks(t, 1, 0, KC)
                    pe.wait_ge(s["seg_sub"], 2 * j + 2 + 4 * i)
                    chunk_turn(i, j + 1)
                pe.wait_ge(s["ssd_operands"], j + 1 + 2 * i)
                for h in range(H):
                    o = pair_ps[0][HEAD * (h % 2):HEAD * (h % 2) + HEAD, (h // 2) * P:(h // 2 + 1) * P]
                    mm(o, xdt_t[:, h * HEAD:(h + 1) * HEAD], seg[:, h, :], start=True, stop=False)
                    ins = mm(o, prev[:, h * HEAD:(h + 1) * HEAD], cexp[:, h, :], start=False, stop=True)
                ins.then_inc(s["ssd_y"], 1)
                if not more:
                    return
                pe.wait_ge(s["chunk_b"], j + 2 + 2 * i)
                for g in range(2):
                    ins = mm(pair_ps[1][:, g * S:(g + 1) * S], b_tok[:, j % 2, g * P:(g + 1) * P],
                             xdd[:, g * S:(g + 1) * S], start=True, stop=True)
                ins.then_inc(s["ssd_state"], 1)

            chunk_turn(0, 0)
            with pe.Fori(0, NT // 2) as i:
                for j in range(2):
                    chunk(i, j, True)
            chunk(NT // 2, 0, False)
            g0 = SLAB0["sb"]

            def sb_chunk(i, g, k):
                if k == 0:
                    pe.wait_ge(s["split"], g0 + 3 + g + 1 + 6 * i)
                    if g % 3:
                        pe.wait_ge(s["sb_evac"], 3 + g + 6 * i)
                    else:
                        pe.wait_ge(s["sb_v"], 1 + g // 3 + 2 * i)
                slab_chunk((g0 + 3 + g) % 2, k)

            first_chunks(-1, 0, KC // 2)
            pe.wait_ge(s["ssd_used"], NT + 1)
            sums_chunks("ssd")
            pe.wait_ge(s["rows_kept"], 1)

            def sb_scores(i, u):
                m, par, blk, nq, q0, nk, buf = sb_unit(u)
                pe.wait_ge(s["sb_evac"], 3 * m + 2 + 6 * i)
                held = [w + u // SBN * SBN for w in SB_HELD[u % SBN]]
                outputs = [w for w in held if sb_outputs(w)]
                turned = [w for w in held if not sb_outputs(w)]
                if outputs:
                    sb_wait(pe, "sb_y", 2 * NT, i, sb_out(outputs[-1]) + 2)
                if turned:
                    sb_wait(pe, "sb_wc", SBN, i, turned[-1] + 1)
                z_ps = sb_bank(u)
                if blk == 0:
                    pe.sem_inc(s["pe_gate"], 1)
                    for half in range(2):
                        h = slice(HEAD * half, HEAD * half + HEAD)
                        ins = mm(z_ps[32 * half:32 * half + 32, 0:META], qs[h, m % 2, 0:32],
                                 ks[h, m % 2, 0:META], start=True, stop=True)
                else:
                    h = slice(HEAD * par, HEAD * par + HEAD)
                    q_u = qs[h, m % 2, q0:q0 + nq]
                    if SB_BANKS[u % SBN][1] == 1:
                        ins = mm(z_ps[:, 0:nk], q_u, ks[h, m % 2, 0:nk], start=True, stop=True)
                    else:
                        mm(z_ps[:, S - META:S], q_u, ks[h, m % 2, 0:META], start=True, stop=True)
                        ins = mm(z_ps[:, S:S + blk * P], q_u, ks[h, m % 2, META:nk], start=True, stop=True)
                ins.then_inc(s["sb_scores"], 1)

            def sb_iteration(i, last):
                chunk = -4
                for u in range(sb_steps(last)):
                    chunks = SB_CHUNKS.get(u, 0) if u <= len(SBU) or not last else 0
                    for j in range(max(chunks, 1)):
                        if j < chunks:
                            sb_chunk(i, chunk // KC, chunk % KC)
                            chunk += 1
                        if j == 0 and sb_scored(u + 1, last):
                            sb_scores(i, u + 1)
                    if u % len(SBU) == 1 and u < SBN:
                        m = u // len(SBU)
                        pe.wait_ge(s["sb_evac"], 3 * m + 3 + 6 * i)
                        for t in range(NT):
                            n, c0 = (META, 0) if t == 0 else (P, META + (t - 1) * P)
                            ins = nc.tensor.transpose(gemm_ps[0][0:n, t * P:(t + 1) * P], vs[:, m, c0:c0 + n],
                                                      ident[:, :])
                        ins.then_inc(s["sb_vt"], 1)
                    if sb_live(i, u - 1):
                        m, par, blk, nq, q0, nk, buf = sb_unit(u - 1)
                        o = sb_bank(u - 1)
                        pe.wait_ge(s["sb_wr"], SBN * i + u)
                        if blk == 0:
                            pe.sem_inc(s["pe_gate"], 1)
                        for t in range(blk + 1):
                            n, c0 = (META, 0) if t == 0 else (P, META + (t - 1) * P)
                            at_ = sb_tile(u - 1, t)
                            ins = nc.tensor.transpose(o[0:n, at_:at_ + nq], sb_sum[0:nq, buf, c0:c0 + n],
                                                      ident[0:nq, 0:nq])
                        ins.then_inc(s["sb_wt"], 1)
                    if sb_live(i, u - 2) and sb_outputs(u - 2):
                        m, par, blk, nq, q0, nk, buf = sb_unit(u - 2)
                        o = sb_bank(u - 2)
                        pe.wait_ge(s["sb_wc"], SBN * i + u - 1)
                        if blk == 0:
                            pe.wait_ge(s["sb_v"], 2 * i + m + 1)
                            pe.sem_inc(s["pe_gate"], 1)
                        for half in range(2):
                            h = slice(HEAD * half, HEAD * half + HEAD)
                            if blk == 0:
                                ins = mm(o[h, 0:META], v_sb[0:META, m % 2, 0, h],
                                         sb_wT[0:META, buf, 0, 32 * half:32 * half + META], start=True, stop=True)
                                continue
                            wb = (buf + half - 1) % SB_BUFS
                            for t in range(blk + 1):
                                n = META if t == 0 else P
                                ins = mm(o[h, 0:P], v_sb[0:n, m % 2, t, h], sb_wT[0:n, wb, t, 0:nq],
                                         start=(t == 0), stop=(t == blk))
                        ins.then_inc(s["sb_o"], 1)

            sb_scores(0, 0)
            sb_iteration(0, False)
            with pe.Fori(1, SB_PAIRS // 2 - 1) as i:
                sb_iteration(i, False)
            sb_iteration(SB_PAIRS // 2 - 1, True)
            pe.wait_ge(s["sb_y"], SB_PAIRS * NT + 1)
            g0, b0 = SLAB0["wo_2"], BLOCK0["wo_2"]

            def half(i, h, jb, ready=None):
                b, j = b0 + jb, 2 * h + jb
                if h == 0:
                    pe.wait_ge(s_evac[b % 2], 1 + b // 2 + i)
                pe.wait_ge(s["split"], g0 + j + 1 + 4 * i)
                hi, lo = ((ys_hi, ys_lo), (xn_hi, xn_lo))[h]
                slot = (g0 + j) % 2
                products(gemm_ps[b % 2], hi, lo, w_hi[:, slot, :, :], w_lo[:, slot, :, :], KC, 0, SEG_2, h == 0, h == 1,
                         ready=ready)

            pe.wait_ge(s["op_ready"], OP_DONE["ssd"])
            half(0, 0, 0)
            half(0, 0, 1)
            sums_end("sbn")
            half(0, 1, 0, ready=OP_DONE["ssd"])
            half(0, 1, 1)
            with pe.Fori(1, KC // 2) as i:
                for j in range(4):
                    half(i, j // 2, j % 2)
            sums_end("post")
            gemm("up", u_hi, u_lo, SEG_2, ready=OP_DONE["sbn"], beside=lambda: sums_end("ffn"))
            gemm("down", f_hi, f_lo, SEG_2, ready=OP_DONE["ffn"], cuts=DOWN)
            sums_end("fin")
            for first in range(0, S // P, 2):
                for k in range(KC):
                    pe.wait_ge(s["norm_done"], 16 + (k + 1 if first == 0 else KC))
                    for t in range(first, first + 2):
                        ins = nc.tensor.transpose((gemm_ps + pair_ps)[t][:, k * P:(k + 1) * P],
                                                  xT[:, k, META + t * P:META + (t + 1) * P], ident[:, :])
                        if k == KC - 1:
                            ins.then_inc(s["out_turned"], 1)


INPUTS = ["x", "c", "ctx", "c_ctx", "norm_g", "ada_w", "ada_b", "w_in_ab", "v_norm_g", "spatial_w", "spatial_b",
          "w_out_ab", "w_in_c", "sink_logit", "w_out_c", "final_g", "meta_tokens_2", "mix_pre_g_2", "w_in_2",
          "ssd_conv_w_2", "ssd_conv_b_2", "ssd_dt_bias_2", "ssd_a_log_2", "ssd_d_2", "ssd_norm_g_2",
          "sb_norm_g_2", "w_out_2", "mix_post_g_2", "ffn_pre_g_2", "w_up_2", "ffn_conv_w_2", "ffn_conv_b_2",
          "w_down_2", "ffn_post_g_2"]
FLAT = {"c", "c_ctx", "norm_g", "ada_b", "v_norm_g", "spatial_b", "sink_logit", "final_g", "mix_pre_g_2",
        "ssd_conv_w_2", "ssd_conv_b_2", "ssd_dt_bias_2", "ssd_a_log_2", "ssd_d_2", "ssd_norm_g_2", "sb_norm_g_2",
        "mix_post_g_2", "ffn_pre_g_2", "ffn_conv_w_2", "ffn_conv_b_2", "ffn_post_g_2"}


def kernel(**inputs):
    import concourse.bacc as bacc
    from concourse.bass_utils import run_bass_kernel_spmd

    nc = bacc.Bacc("TRN2", target_bir_lowering=False, num_devices=1)
    nc, arrays = build(nc, inputs)
    r = run_bass_kernel_spmd(nc, [arrays], core_ids=[0])
    return r.results[0]["out_dram"].reshape(1, S, D)


def build(nc, inputs):
    arrays, args = {}, []
    for name in INPUTS:
        a = np.ascontiguousarray(inputs[name])
        if name in FLAT:
            a = a.reshape(-1)
        elif name not in ("ada_w", "meta_tokens_2"):
            a = a.reshape(a.shape[1:])
        arrays[f"in_{name}"] = a
        args.append(nc.dram_tensor(f"in_{name}", a.shape, F32, kind="ExternalInput").ap())
    arrays["consts"] = shape_constants()[0]
    args.append(nc.dram_tensor("consts", arrays["consts"].shape, F32, kind="ExternalInput").ap())
    args.append(nc.dram_tensor("out_dram", (S, D), F32, kind="ExternalOutput").ap())
    two_blocks(nc, *args)
    return nc, arrays
```
